# Optimizing a Trainium2 kernel written in Bass

```python
import jax, jax.numpy as jnp
from jax import lax
import numpy as np

D_MODEL = 1024
BATCH = 1
SEQ = 512
DEPTH = 2

D_PLE = 256
D_LRU = 3 * D_MODEL // 4
D_RET = 3 * D_MODEL // 4
D_SGU = D_MODEL // 2
D_MIX = D_LRU + D_RET + D_SGU
LRU_BLOCKS = 8
LRU_BLOCK_DIM = D_LRU // LRU_BLOCKS
CONV_WIDTH = 4
LRU_C = 8.0
RET_HEADS = 6
RET_HEAD_DIM = D_RET // RET_HEADS
RET_CHUNK = 128
ROPE_BASE = 10000.0
SGU_GROUPS = 4
SGU_GROUP_DIM = D_SGU // SGU_GROUPS
SGU_CHUNK = 128
D_IN = 2 * D_LRU + 4 * D_RET + 3 * D_SGU
EPS = 1e-6


def rms_norm(x, g):
    xf = x.astype(jnp.float32)
    y = xf * lax.rsqrt(jnp.mean(xf * xf, axis=-1, keepdims=True) + EPS)
    return (y * g.astype(jnp.float32)).astype(x.dtype)

def causal_depthwise_conv(x, w, b):
    S = x.shape[1]
    xp = jnp.pad(x, ((0, 0), (CONV_WIDTH - 1, 0), (0, 0)))
    y = b + xp[:, 0:S] * w[0]
    for k in range(1, CONV_WIDTH):
        y = y + xp[:, k:k + S] * w[k]
    return y

def rg_lru(x, w_a, b_a, w_x, b_x, lam):
    B, S, _ = x.shape
    f32 = jnp.float32
    xf = x.astype(f32)
    xb = xf.reshape(B, S, LRU_BLOCKS, LRU_BLOCK_DIM)
    r = jax.nn.sigmoid(jnp.einsum('bsnc,ncd->bsnd', xb, w_a.astype(f32)).reshape(B, S, D_LRU) + b_a.astype(f32))
    i = jax.nn.sigmoid(jnp.einsum('bsnc,ncd->bsnd', xb, w_x.astype(f32)).reshape(B, S, D_LRU) + b_x.astype(f32))
    log_a = -LRU_C * r * jax.nn.softplus(-lam.astype(f32))
    a = jnp.exp(log_a)
    u = jnp.sqrt(-jnp.expm1(2.0 * log_a)) * (i * xf)

    def combine(c1, c2):
        a1, b1 = c1
        a2, b2 = c2
        return a1 * a2, a2 * b1 + b2

    _, h = lax.associative_scan(combine, (a, u), axis=1)
    return h.astype(x.dtype)

def rope(x, positions):
    half = RET_HEAD_DIM // 2
    inv = ROPE_BASE ** (-jnp.arange(half, dtype=jnp.float32) / half)
    ang = positions.astype(jnp.float32)[..., None] * inv
    cos = jnp.cos(ang)[:, :, None, :]
    sin = jnp.sin(ang)[:, :, None, :]
    x1, x2 = x[..., :half], x[..., half:]
    return jnp.concatenate([x1 * cos - x2 * sin, x2 * cos + x1 * sin], axis=-1)

def retention(q, k, v, positions, g_norm):
    B, S, _ = q.shape
    f32 = jnp.float32
    H, Dh, C = RET_HEADS, RET_HEAD_DIM, RET_CHUNK
    N = S // C
    qh = rope(q.reshape(B, S, H, Dh).astype(f32), positions)
    kh = rope(k.reshape(B, S, H, Dh).astype(f32), positions) * (Dh ** -0.5)
    vh = v.reshape(B, S, H, Dh).astype(f32)
    log_g = jnp.log1p(-jnp.exp2(-5.0 - jnp.arange(H, dtype=f32)))
    idx = jnp.arange(C, dtype=f32)
    diff = idx[:, None] - idx[None, :]
    causal = diff >= 0
    decay = jnp.where(causal[None], jnp.exp(jnp.where(causal, diff, 0.0)[None] * log_g[:, None, None]), 0.0)
    qc = qh.reshape(B, N, C, H, Dh)
    kc = kh.reshape(B, N, C, H, Dh)
    vc = vh.reshape(B, N, C, H, Dh)
    scores = jnp.einsum('bnihd,bnjhd->bnhij', qc, kc) * decay
    intra = jnp.einsum('bnhij,bnjhe->bnihe', scores, vc)
    k_w = jnp.exp((C - 1.0 - idx)[:, None] * log_g[None, :])
    kv = jnp.einsum('bnjhd,jh,bnjhe->nbhde', kc, k_w, vc)
    chunk_decay = jnp.exp(C * log_g)[None, :, None, None]

    def step(state, kv_n):
        return state * chunk_decay + kv_n, state

    _, s_prev = lax.scan(step, jnp.zeros((B, H, Dh, Dh), f32), kv)
    q_w = jnp.exp((idx + 1.0)[:, None] * log_g[None, :])
    cross = jnp.einsum('bnihd,ih,nbhde->bnihe', qc, q_w, s_prev)
    o = (intra + cross).reshape(B, S, H, Dh)
    o = o * lax.rsqrt(jnp.mean(o * o, axis=-1, keepdims=True) + EPS)
    o = o.reshape(B, S, D_RET) * g_norm.astype(f32)
    return o.astype(q.dtype)

def spatial_gating(u, v, ln_g, ln_b, w_s, b_s):
    B, S, _ = u.shape
    f32 = jnp.float32
    N = S // SGU_CHUNK
    vf = v.astype(f32)
    mu = jnp.mean(vf, axis=-1, keepdims=True)
    var = jnp.mean(jnp.square(vf - mu), axis=-1, keepdims=True)
    vn = (vf - mu) * lax.rsqrt(var + EPS) * ln_g.astype(f32) + ln_b.astype(f32)
    vc = vn.reshape(B, N, SGU_CHUNK, SGU_GROUPS, SGU_GROUP_DIM)
    mask = jnp.tril(jnp.ones((SGU_CHUNK, SGU_CHUNK), dtype=bool))
    ws = jnp.where(mask[None], w_s.astype(f32), 0.0)
    mixed = jnp.einsum('gij,bnjgc->bnigc', ws, vc) + b_s.astype(f32).T[None, None, :, :, None]
    return (u.astype(f32) * mixed.reshape(B, S, D_SGU)).astype(u.dtype)

def first_inputs(seed: int = 0) -> dict:
    key = jax.random.key(seed)
    ks = jax.random.split(key, 24)
    f32 = jnp.float32

    def nrm(k, shape, scale):
        return jax.random.normal(k, shape, f32) * scale

    x = jax.random.normal(ks[0], (BATCH, SEQ, D_MODEL), f32)
    p = jax.random.normal(ks[1], (DEPTH, BATCH, SEQ, D_PLE), f32)
    positions = jnp.broadcast_to(jnp.arange(SEQ, dtype=jnp.int32), (BATCH, SEQ))
    a_init = jax.random.uniform(ks[9], (DEPTH, D_LRU), f32, 0.9, 0.999)
    return {
        "x": x,
        "p": p,
        "positions": positions,
        "mix_norm": 1.0 + nrm(ks[2], (DEPTH, D_MODEL), 0.02),
        "w_in": nrm(ks[3], (DEPTH, D_MODEL, D_IN), D_MODEL ** -0.5),
        "lru_conv_w": nrm(ks[4], (DEPTH, CONV_WIDTH, D_LRU), CONV_WIDTH ** -0.5),
        "lru_conv_b": nrm(ks[5], (DEPTH, D_LRU), 0.01),
        "lru_w_a": nrm(ks[6], (DEPTH, LRU_BLOCKS, LRU_BLOCK_DIM, LRU_BLOCK_DIM), LRU_BLOCK_DIM ** -0.5),
        "lru_b_a": nrm(ks[7], (DEPTH, D_LRU), 0.01),
        "lru_w_x": nrm(ks[8], (DEPTH, LRU_BLOCKS, LRU_BLOCK_DIM, LRU_BLOCK_DIM), LRU_BLOCK_DIM ** -0.5),
        "lru_b_x": nrm(ks[10], (DEPTH, D_LRU), 0.01),
        "lru_lambda": jnp.log(a_init) - jnp.log1p(-a_init),
        "ret_norm": 1.0 + nrm(ks[11], (DEPTH, D_RET), 0.02),
        "sgu_ln_g": 1.0 + nrm(ks[12], (DEPTH, D_SGU), 0.02),
        "sgu_ln_b": nrm(ks[13], (DEPTH, D_SGU), 0.01),
        "sgu_w_s": nrm(ks[14], (DEPTH, SGU_GROUPS, SGU_CHUNK, SGU_CHUNK), 0.5 * SGU_CHUNK ** -0.5),
        "sgu_b_s": 1.0 + nrm(ks[15], (DEPTH, SGU_GROUPS, SGU_CHUNK), 0.02),
        "w_out": nrm(ks[16], (DEPTH, D_MIX, D_MODEL), D_MIX ** -0.5),
        "ple_norm": 1.0 + nrm(ks[17], (DEPTH, D_MODEL), 0.02),
        "w_ple_gate": nrm(ks[18], (DEPTH, D_MODEL, D_MODEL), D_MODEL ** -0.5),
        "w_ple_proj": nrm(ks[19], (DEPTH, D_PLE, D_MODEL), D_PLE ** -0.5),
        "final_norm": 1.0 + nrm(ks[20], (D_MODEL,), 0.02),
    }

def first_block(x, p, positions, mix_norm, w_in, lru_conv_w, lru_conv_b, lru_w_a, lru_b_a, lru_w_x, lru_b_x,
              lru_lambda, ret_norm, sgu_ln_g, sgu_ln_b, sgu_w_s, sgu_b_s, w_out, ple_norm, w_ple_gate,
              w_ple_proj, final_norm):
    sizes = (D_LRU, D_LRU, D_RET, D_RET, D_RET, D_RET, D_SGU, D_SGU, D_SGU)
    split_points = []
    acc = 0
    for s in sizes[:-1]:
        acc += s
        split_points.append(acc)
    h = x
    for i in range(DEPTH):
        y = rms_norm(h, mix_norm[i])
        proj = y @ w_in[i]
        x_lru, g_lru, q, k, v, g_ret, u_sgu, v_sgu, g_sgu = jnp.split(proj, split_points, axis=-1)
        lru_out = rg_lru(causal_depthwise_conv(x_lru, lru_conv_w[i], lru_conv_b[i]),
                         lru_w_a[i], lru_b_a[i], lru_w_x[i], lru_b_x[i], lru_lambda[i])
        ret_out = retention(q, k, v, positions, ret_norm[i])
        sgu_out = spatial_gating(u_sgu, v_sgu, sgu_ln_g[i], sgu_ln_b[i], sgu_w_s[i], sgu_b_s[i])
        mixed = jnp.concatenate([lru_out * jax.nn.silu(g_lru),
                                 ret_out * jax.nn.silu(g_ret),
                                 sgu_out * jax.nn.silu(g_sgu)], axis=-1)
        h = h + mixed @ w_out[i]
        z = rms_norm(h, ple_norm[i])
        h = h + jax.nn.sigmoid(z @ w_ple_gate[i]) * (p[i] @ w_ple_proj[i])
    return rms_norm(h, final_norm)


_first_inputs = first_inputs


def first_inputs(seed=0):
    import zlib

    import numpy as np

    out = dict(_first_inputs(seed))
    spreads = {}
    factors = {}
    for name, (base, spread) in spreads.items():
        noise = np.random.default_rng([zlib.crc32(name.encode()), seed]).standard_normal(out[name].shape)
        drawn = base * np.exp(spread * noise) if base else spread * noise
        out[name] = __import__('jax').numpy.asarray(drawn.astype(out[name].dtype))
    for name, factor in factors.items():
        out[name] = (out[name] * factor).astype(out[name].dtype)
    return out


_narrow_inputs = first_inputs


def first_inputs(seed=0):
    out = dict(_narrow_inputs(seed))
    wider = {'lru_conv_b': 6.99,
     'lru_b_a': 12.0,
     'lru_b_x': 12.0,
     'ret_norm': 7.89,
     'sgu_ln_g': 12.0,
     'sgu_ln_b': 12.0,
     'sgu_b_s': 9.69,
     'ple_norm': 12.0,
     'final_norm': 3.33}
    for name, times in wider.items():
        mean = out[name].mean()
        out[name] = (mean + times * (out[name] - mean)).astype(out[name].dtype)
    return out


DEPTH_2 = 1

GRID_W = 64
CTX_LEN = 256
HEAD_DIM = 128
N_Q_HEADS = 4
N_KV_HEADS = 2
Q_PER_KV = N_Q_HEADS // N_KV_HEADS
ATTN_WIDTH = N_Q_HEADS * HEAD_DIM
KV_WIDTH = N_KV_HEADS * HEAD_DIM
AXIS_DIM = HEAD_DIM // 2
ROPE_THETA = 10000.0
Q_BLOCK = 128
CONV_WIDTH_2 = D_MODEL - ATTN_WIDTH
CONV_K = 3
MIX_WIDTH = ATTN_WIDTH + CONV_WIDTH_2
Q_END = ATTN_WIDTH
K_END = Q_END + KV_WIDTH
KV_END = K_END + KV_WIDTH
CB_END = KV_END + CONV_WIDTH_2
CC_END = CB_END + CONV_WIDTH_2
IN_COLS = CC_END + CONV_WIDTH_2
N_EXPERTS = 32
TOP_K = 4
D_FF = D_MODEL
SWIGLU_LIMIT = 7.0
SWIGLU_ALPHA = 1.702
MOE_BLOCK = 128
N_MOD = 6
NORM_EPS = 1e-6


def rmsnorm(x, gain):
    x32 = x.astype(jnp.float32)
    y = x32 * lax.rsqrt(jnp.mean(x32 * x32, axis=-1, keepdims=True) + NORM_EPS)
    return y.astype(x.dtype) * gain

def ada_params(cond, w_ada, b_ada):
    mod = jax.nn.silu(cond) @ w_ada + b_ada
    return jnp.split(mod[..., None, :], N_MOD, axis=-1)

def modulate(x, gain, shift, scale):
    return rmsnorm(x, gain) * (1.0 + scale) + shift

def split_in(p):
    return jnp.split(p, [Q_END, K_END, KV_END, CB_END, CC_END], axis=-1)

def to_heads(t, n_heads, gain=None):
    b, n, _ = t.shape
    t = t.reshape(b, n, n_heads, HEAD_DIM)
    return t if gain is None else rmsnorm(t, gain)

def axial_rope_tables(n_tokens):
    rows = n_tokens // GRID_W
    row = jnp.broadcast_to(jnp.arange(rows, dtype=jnp.float32)[:, None], (rows, GRID_W)).reshape(-1)
    col = jnp.broadcast_to(jnp.arange(GRID_W, dtype=jnp.float32)[None, :], (rows, GRID_W)).reshape(-1)
    inv_freq = ROPE_THETA ** (-jnp.arange(0, AXIS_DIM, 2, dtype=jnp.float32) / AXIS_DIM)
    ang = jnp.stack([row[:, None] * inv_freq, col[:, None] * inv_freq], axis=1)
    return jnp.cos(ang), jnp.sin(ang)

def apply_axial_rope(t, cos, sin):
    b, n, h, _ = t.shape
    tr = t.astype(jnp.float32).reshape(b, n, h, 2, 2, AXIS_DIM // 2)
    t1, t2 = tr[..., 0, :], tr[..., 1, :]
    cs, sn = cos[None, :, None], sin[None, :, None]
    out = jnp.stack([t1 * cs - t2 * sn, t2 * cs + t1 * sn], axis=-2)
    return out.reshape(b, n, h, HEAD_DIM).astype(t.dtype)

def dense_attention(q, k, v):
    b, nq, _, _ = q.shape
    qg = q.reshape(b, nq, N_KV_HEADS, Q_PER_KV, HEAD_DIM)
    s = jnp.einsum('bqkgd,bskd->bkgqs', qg, k, preferred_element_type=jnp.float32) * (HEAD_DIM ** -0.5)
    p = jax.nn.softmax(s, axis=-1).astype(v.dtype)
    o = jnp.einsum('bkgqs,bskd->bqkgd', p, v)
    return o.reshape(b, nq, ATTN_WIDTH)

def blocked_attention(q, k, v):
    b, n, _, _ = q.shape
    nblk = n // Q_BLOCK
    qb = q.reshape(b, nblk, Q_BLOCK, N_Q_HEADS, HEAD_DIM).transpose(1, 0, 2, 3, 4)
    o = lax.map(lambda qblk: dense_attention(qblk, k, v), qb)
    return o.transpose(1, 0, 2, 3).reshape(b, n, ATTN_WIDTH)

def short_conv_mixer(cb, cc, cx, conv_w):
    u = cc * cx
    up = jnp.pad(u, ((0, 0), (1, 1), (0, 0)))
    y = up[:, :-2] * conv_w[0] + up[:, 1:-1] * conv_w[1] + up[:, 2:] * conv_w[2]
    return cb * y

def clamped_swiglu(gu):
    glu, lin = jnp.split(gu, 2, axis=-1)
    glu = jnp.minimum(glu, SWIGLU_LIMIT)
    lin = jnp.clip(lin, -SWIGLU_LIMIT, SWIGLU_LIMIT)
    return glu * jax.nn.sigmoid(SWIGLU_ALPHA * glu) * (lin + 1.0)

def moe_ffn(h, w_router, b_router, w_gate_up, b_gate_up, w_down, b_down):
    n_tok, d = h.shape
    logits = jnp.dot(h, w_router, preferred_element_type=jnp.float32) + b_router.astype(jnp.float32)
    top_logit, top_idx = lax.top_k(logits, TOP_K)
    gate = jax.nn.softmax(top_logit, axis=-1)
    n_pair = n_tok * TOP_K
    n_blocks = -(-(n_pair + N_EXPERTS * (MOE_BLOCK - 1)) // MOE_BLOCK)
    n_slots = n_blocks * MOE_BLOCK
    flat_e = top_idx.reshape(-1).astype(jnp.int32)
    flat_tok = jnp.repeat(jnp.arange(n_tok, dtype=jnp.int32), TOP_K, total_repeat_length=n_pair)
    flat_gate = gate.reshape(-1)
    order = jnp.argsort(flat_e, stable=True)
    e_sorted = flat_e[order]
    counts = jnp.zeros((N_EXPERTS,), jnp.int32).at[flat_e].add(1)
    padded = (counts + MOE_BLOCK - 1) // MOE_BLOCK * MOE_BLOCK
    start = jnp.cumsum(counts) - counts
    pad_end = jnp.cumsum(padded)
    pad_start = pad_end - padded
    slot = pad_start[e_sorted] + jnp.arange(n_pair, dtype=jnp.int32) - start[e_sorted]
    slot_tok = jnp.full((n_slots,), n_tok, jnp.int32).at[slot].set(flat_tok[order])
    slot_gate = jnp.zeros((n_slots,), jnp.float32).at[slot].set(flat_gate[order])
    block_start = jnp.arange(n_blocks, dtype=jnp.int32) * MOE_BLOCK
    block_expert = jnp.minimum(jnp.searchsorted(pad_end, block_start, side='right'), N_EXPERTS - 1)
    h_pad = jnp.concatenate([h, jnp.zeros((1, d), h.dtype)], axis=0)

    def expert_block(args):
        tok, g, e = args
        xb = h_pad[tok]
        gu = xb @ w_gate_up[e] + b_gate_up[e]
        y = clamped_swiglu(gu) @ w_down[e] + b_down[e]
        return y * g[:, None].astype(y.dtype)

    y = lax.map(expert_block, (slot_tok.reshape(n_blocks, MOE_BLOCK),
                               slot_gate.reshape(n_blocks, MOE_BLOCK), block_expert))
    out = jnp.zeros((n_tok + 1, d), y.dtype).at[slot_tok].add(y.reshape(n_slots, d))
    return out[:n_tok]

def second_inputs(seed: int = 0) -> dict:
    key = jax.random.key(seed)
    ks = jax.random.split(key, 20)
    f32 = jnp.float32
    nrm = lambda k, shape, s: jax.random.normal(k, shape, f32) * s
    return {
        "x": nrm(ks[0], (BATCH, SEQ, D_MODEL), 1.0),
        "c": nrm(ks[1], (BATCH, D_MODEL), 1.0),
        "ctx": nrm(ks[2], (BATCH, CTX_LEN, D_MODEL), 1.0),
        "c_ctx": nrm(ks[3], (D_MODEL,), 1.0),
        "w_ada": nrm(ks[4], (DEPTH_2, D_MODEL, N_MOD * D_MODEL), 0.2 * D_MODEL ** -0.5),
        "b_ada": nrm(ks[5], (DEPTH_2, N_MOD * D_MODEL), 0.01),
        "g_norm1": 1.0 + nrm(ks[6], (DEPTH_2, D_MODEL), 0.01),
        "g_norm2": 1.0 + nrm(ks[7], (DEPTH_2, D_MODEL), 0.01),
        "w_in": nrm(ks[8], (DEPTH_2, D_MODEL, IN_COLS), D_MODEL ** -0.5),
        "g_q": 1.0 + nrm(ks[9], (DEPTH_2, HEAD_DIM), 0.01),
        "g_k": 1.0 + nrm(ks[10], (DEPTH_2, HEAD_DIM), 0.01),
        "w_conv": nrm(ks[11], (DEPTH_2, CONV_K, CONV_WIDTH_2), CONV_K ** -0.5),
        "w_out": nrm(ks[12], (DEPTH_2, MIX_WIDTH, D_MODEL), MIX_WIDTH ** -0.5),
        "w_router": nrm(ks[13], (DEPTH_2, D_MODEL, N_EXPERTS), D_MODEL ** -0.5),
        "b_router": nrm(ks[14], (DEPTH_2, N_EXPERTS), 0.01),
        "w_gate_up": nrm(ks[15], (DEPTH_2, N_EXPERTS, D_MODEL, 2 * D_FF), D_MODEL ** -0.5),
        "b_gate_up": nrm(ks[16], (DEPTH_2, N_EXPERTS, 2 * D_FF), 0.01),
        "w_down": nrm(ks[17], (DEPTH_2, N_EXPERTS, D_FF, D_MODEL), D_FF ** -0.5),
        "b_down": nrm(ks[18], (DEPTH_2, N_EXPERTS, D_MODEL), 0.01),
        "g_final": 1.0 + nrm(ks[19], (D_MODEL,), 0.01),
    }

def second_block(x, c, ctx, c_ctx, w_ada, b_ada, g_norm1, g_norm2, w_in, g_q, g_k, w_conv, w_out,
              w_router, b_router, w_gate_up, b_gate_up, w_down, b_down, g_final):
    b, n, d = x.shape
    cos, sin = axial_rope_tables(n)
    for layer in range(DEPTH_2):
        last = layer == DEPTH_2 - 1
        sh1, sc1, gt1, sh2, sc2, gt2 = ada_params(c, w_ada[layer], b_ada[layer])
        csh1, csc1, cgt1, csh2, csc2, cgt2 = ada_params(c_ctx, w_ada[layer], b_ada[layer])
        w_in_l = w_in[layer]

        hc = modulate(ctx, g_norm1[layer], csh1, csc1)
        if last:
            kc, vc = jnp.split(hc @ w_in_l[:, Q_END:KV_END], 2, axis=-1)
        else:
            qc, kc, vc, cbc, ccc, cxc = split_in(hc @ w_in_l)
        kc = to_heads(kc, N_KV_HEADS, g_k[layer])
        vc = to_heads(vc, N_KV_HEADS)
        if not last:
            qc = to_heads(qc, N_Q_HEADS, g_q[layer])
            mix_c = jnp.concatenate([dense_attention(qc, kc, vc),
                                     short_conv_mixer(cbc, ccc, cxc, w_conv[layer])], axis=-1)
            ctx_next = ctx + cgt1 * (mix_c @ w_out[layer])
            hc2 = modulate(ctx_next, g_norm2[layer], csh2, csc2).reshape(-1, d)
            ctx_next = ctx_next + cgt2 * moe_ffn(hc2, w_router[layer], b_router[layer], w_gate_up[layer],
                                                 b_gate_up[layer], w_down[layer], b_down[layer]).reshape(ctx.shape)

        h = modulate(x, g_norm1[layer], sh1, sc1)
        q, k, v, cb, cc, cx = split_in(h @ w_in_l)
        q = apply_axial_rope(to_heads(q, N_Q_HEADS, g_q[layer]), cos, sin)
        k = apply_axial_rope(to_heads(k, N_KV_HEADS, g_k[layer]), cos, sin)
        v = to_heads(v, N_KV_HEADS)
        k_all = jnp.concatenate([k, kc], axis=1)
        v_all = jnp.concatenate([v, vc], axis=1)
        attn = blocked_attention(q, k_all, v_all)
        conv = short_conv_mixer(cb, cc, cx, w_conv[layer])
        x = x + gt1 * (jnp.concatenate([attn, conv], axis=-1) @ w_out[layer])

        h2 = modulate(x, g_norm2[layer], sh2, sc2).reshape(-1, d)
        x = x + gt2 * moe_ffn(h2, w_router[layer], b_router[layer], w_gate_up[layer], b_gate_up[layer],
                              w_down[layer], b_down[layer]).reshape(b, n, d)
        if not last:
            ctx = ctx_next
    return rmsnorm(x, g_final)


_first_inputs_2 = second_inputs


def second_inputs(seed=0):
    import zlib

    import numpy as np

    out = dict(_first_inputs_2(seed))
    spreads = {}
    factors = {'ctx': 8.0,
     'c_ctx': 8.0,
     'b_ada': 4.928,
     'g_norm1': 8.0,
     'g_norm2': 8.0,
     'g_q': 8.0,
     'g_k': 8.0,
     'b_router': 8.0,
     'b_gate_up': 8.0,
     'b_down': 8.0,
     'g_final': 5.671}
    for name, (base, spread) in spreads.items():
        noise = np.random.default_rng([zlib.crc32(name.encode()), seed]).standard_normal(out[name].shape)
        drawn = base * np.exp(spread * noise) if base else spread * noise
        out[name] = __import__('jax').numpy.asarray(drawn.astype(out[name].dtype))
    for name, factor in factors.items():
        out[name] = (out[name] * factor).astype(out[name].dtype)
    return out


_narrow_inputs_2 = second_inputs


def second_inputs(seed=0):

    out = dict(_narrow_inputs_2(seed))
    wider = {'ctx': 4.22,
     'c_ctx': 4.4,
     'g_norm1': 3.5,
     'g_norm2': 12.0,
     'g_q': 12.0,
     'g_k': 12.0,
     'b_router': 12.0,
     'b_gate_up': 12.0,
     'b_down': 12.0,
     'g_final': 6.47}
    for name, times in wider.items():
        mean = out[name].mean()
        out[name] = (mean + times * (out[name] - mean)).astype(out[name].dtype)
    return out


def setup_inputs(seed=0):
    out = dict(first_inputs(seed))
    for name, value in second_inputs(seed + 1).items():
        if name != "x":
            out[name + "_2"] = value
    return out


def reference(
    x, p, positions, mix_norm, w_in, lru_conv_w, lru_conv_b, lru_w_a, lru_b_a, lru_w_x, lru_b_x,
    lru_lambda, ret_norm, sgu_ln_g, sgu_ln_b, sgu_w_s, sgu_b_s, w_out, ple_norm, w_ple_gate,
    w_ple_proj, final_norm, c_2, ctx_2, c_ctx_2, w_ada_2, b_ada_2, g_norm1_2, g_norm2_2, w_in_2,
    g_q_2, g_k_2, w_conv_2, w_out_2, w_router_2, b_router_2, w_gate_up_2, b_gate_up_2, w_down_2,
    b_down_2, g_final_2,
):
    x = first_block(
        x, p, positions, mix_norm, w_in, lru_conv_w, lru_conv_b, lru_w_a, lru_b_a, lru_w_x,
        lru_b_x, lru_lambda, ret_norm, sgu_ln_g, sgu_ln_b, sgu_w_s, sgu_b_s, w_out, ple_norm,
        w_ple_gate, w_ple_proj, final_norm,
    )
    return second_block(
        x, c_2, ctx_2, c_ctx_2, w_ada_2, b_ada_2, g_norm1_2, g_norm2_2, w_in_2, g_q_2, g_k_2,
        w_conv_2, w_out_2, w_router_2, b_router_2, w_gate_up_2, b_gate_up_2, w_down_2, b_down_2,
        g_final_2,
    )


_drawn_inputs = setup_inputs


def setup_inputs(seed=0):
    import zlib

    import numpy as np

    out = dict(_drawn_inputs(seed))
    spreads = {}
    factors = {'lru_b_a': 4.919,
     'lru_b_x': 2.79,
     'g_norm2_2': 3.917,
     'g_q_2': 2.812,
     'b_router_2': 4.48,
     'b_gate_up_2': 6.141,
     'b_down_2': 22.208}
    for name, (base, spread) in spreads.items():
        noise = np.random.default_rng([zlib.crc32(name.encode()), seed]).standard_normal(out[name].shape)
        drawn = base * np.exp(spread * noise) if base else spread * noise
        out[name] = __import__('jax').numpy.asarray(drawn.astype(out[name].dtype))
    for name, factor in factors.items():
        out[name] = (out[name] * factor).astype(out[name].dtype)
    return out
```

```python
from contextlib import ExitStack

import numpy as np
import concourse.bass as bass
from concourse import mybir

F32 = mybir.dt.float32
I32 = mybir.dt.int32
U32 = mybir.dt.uint32
ALU = mybir.AluOpType
ACT = mybir.ActivationFunctionType
AX = mybir.AxisListType

N_CONST = 9
EPSC = EPS = 1e-6
_LOW = int((2 * np.pi - 6.28125) * 2 ** 21) / 2 ** 21
TWO_PI = (6.28125, _LOW, 2 * np.pi - 6.28125 - _LOW)

P = 128
S = 512
D = 1024
DK = D // P
ST = S // P
L = 2
LRU_T = 768 // P
LRU_BLOCK = 96
HEADS = 6
CONV = 4
SGU_G = 4
CTX = 256
QH, KVH = 4, 2
KEYS = S + CTX
KT = KEYS // P
E_N, TOP = 32, 4
DFF = 1024
LIMIT, ALPHA = 7.0, 1.702
BLOCKS = 48
LIST_ROWS = (BLOCKS + 1) * P
ACC_ROWS = S + P

UNIT = 4096
RING = 4
UNITS_LAYER = 20
UNITS_TAIL = 20

PC = {}
_n = 0
for _name, _w in (("mix_norm", DK), ("ple_norm", DK), ("conv_w", CONV * LRU_T), ("conv_b", LRU_T),
                  ("b_a", LRU_T), ("b_x", LRU_T), ("lam", LRU_T), ("ret_norm", HEADS),
                  ("decay_rate", LRU_T)):
    PC[_name] = _n
    _n += _w
NPAR = _n
QC = {}
_n = 0
for _name, _w in (("final_norm", DK), ("b_ada", 48), ("g_norm1", DK), ("g_norm2", DK), ("g_q", 1), ("g_k", 1),
                  ("w_conv", 12), ("g_final", DK), ("cond", 2 * DK), ("inv_freq", 1), ("rope_sign", 1),
                  ("part", 1)):
    QC[_name] = _n
    _n += _w
NPAR2 = _n


def q_(par2, name, i=0, n=1):
    return par2[:, QC[name] + i:QC[name] + i + n]


class Groups:

    def __init__(self, nc, ctx, name, banks, order):
        self.full = ctx.enter_context(nc.semaphore(f"{name}_full"))
        self.free = ctx.enter_context(nc.semaphore(f"{name}_free"))
        self.banks, self.order, self.n = banks, order, len(order)
        self.at = {g: i for i, g in enumerate(order)}
        assert len(self.at) == self.n

    def bank(self, g):
        return self.banks[self.at[g] % len(self.banks)]

    def done(self, layer, g):
        return layer * self.n + self.at[g] + 1

    def reusable(self, layer, g):
        i, c = self.at[g], len(self.banks)
        if i >= c:
            return layer * self.n + i + 1
        last = max(j for j in range(self.n) if j % c == i)
        return layer * self.n + last + 1 + c - self.n


def lru_pairs():
    return [(k, m) for m in range(3) for k in range(3)
            if any(max(k * P, b * LRU_BLOCK) < min((k + 1) * P, (b + 1) * LRU_BLOCK)
                   and max(m * P, b * LRU_BLOCK) < min((m + 1) * P, (b + 1) * LRU_BLOCK) for b in range(4))]


PAIRS = lru_pairs()


def build(nc, io, stop=99):
    ctx = ExitStack()
    with ctx:
        def sb(name, shape, dt=F32):
            return ctx.enter_context(nc.sbuf_tensor(name, shape, dt))

        def sem(name):
            return ctx.enter_context(nc.semaphore(name))

        ring = sb("ring", [P, RING, UNIT])
        mix = sb("mix", [P, 16, S])
        hT = sb("hT", [P, DK, S])
        yT = sb("yT", [P, DK, S])
        ident = sb("ident", [P, P])
        ones = sb("ones", [P, P])
        before = sb("before", [P, P])
        cst = sb("cst", [P, E_N + 24])
        cst_i = sb("cst_i", [P, ST * TOP], I32)
        brt = sb("router_bias", [P, E_N])
        cond = sb("cond", [P, DK, 2])
        tri = sb("tri", [P, P])
        par_all = sb("par_all", [P, L, NPAR])
        par = sb("par", [P, NPAR])
        par2 = sb("par2", [P, NPAR2])
        mv = sb("mv", [P, ST, 2])
        bn = sb("bn", [P, ST, 6])
        small = sb("small", [P, 64])
        ada = sb("ada", [P, 48, 2])
        coef = sb("coef", [P, 3, DK])
        scr_size = 17700
        scr = sb("scr", [P, scr_size])
        ps = ctx.enter_context(nc.psum_tensor("ps", [P, 8, 512], F32))

        def carve(at, *dims):
            n = int(np.prod(dims))
            assert at[0] + n <= scr_size, at
            v = scr[:, at[0]:at[0] + n]
            at[0] += n
            if len(dims) == 2:
                v = v.rearrange("p (a b) -> p a b", a=dims[0])
            return v

        at = [0]
        vnat = carve(at, ST, 768)
        decay = carve(at, HEADS, S)
        rcos, rsin = carve(at, S), carve(at, S)
        sq = carve(at, 2, S)
        std = carve(at, 2, S)
        tmp = carve(at, 4, S)
        xl = carve(at, 2, S + 4)
        work = carve(at, 3328)
        lngb = carve(at, 2, S)
        bsb = carve(at, SGU_G, P)
        wsT = carve(at, SGU_G, P)
        xc = work[:, 0:LRU_T * S].rearrange("p (a b) -> p a b", a=LRU_T)
        qk = work[:, 0:4 * S].rearrange("p (a b) -> p a b", a=4)
        dec_s = work[:, 4 * S:4 * S + 1280]
        vs = vnat[:, :, 0:S]

        at = [0]
        acos, asin = carve(at, S), carve(at, S)
        sq2 = carve(at, 2, S)
        std2 = carve(at, 2, S)
        tmp2 = carve(at, 4, S)
        kTa = carve(at, KVH, KEYS)
        vall = carve(at, KT, KVH * P)
        qTa = carve(at, QH, S)
        eT = carve(at, KT, S)
        prob = carve(at, 2, KEYS)
        ccb = carve(at, 4, S)
        ubuf = carve(at, S + 4)
        ctxT = mix[:, 0:4, :].rearrange("p a b -> p (a b)").rearrange("p (a b) -> p a b", a=DK)
        hcT = mix[:, 4:8, :].rearrange("p a b -> p (a b)").rearrange("p (a b) -> p a b", a=DK)

        at = [0]
        logits = carve(at, ST, E_N)
        mx8 = carve(at, ST, 8)
        ix8 = carve(at, ST, 8)
        ixf = carve(at, ST, 8)
        hot = carve(at, ST * TOP, E_N)
        hot2 = carve(at, ST * TOP, E_N)
        chosen = carve(at, ST, E_N)
        posn = carve(at, ST, E_N)
        nblk, pend, pbase, zer, ended = (carve(at, E_N) for _ in range(5))
        gates = carve(at, ST, TOP)
        gsum = carve(at, ST)
        slotf = carve(at, ST * TOP)
        beI, npI = carve(at, 1), carve(at, 1)
        hot2n = carve(at, 24)
        h2n = carve(at, ST, D)
        assert at[0] <= scr_size
        at = [0]
        xg = carve(at, 2, D)
        xgT = carve(at, 2, D)
        h_sb = carve(at, D)
        hTe = carve(at, D)
        y_sb = carve(at, 2, D)
        brow = carve(at, 2, 3 * D)
        glu, thb, lin = carve(at, S), carve(at, S), carve(at, S)
        lst = sb("lst", [P, 2, 2], I32)
        np_i = sb("np_i", [1, 1], I32)
        be_i = sb("be_i", [P, 1], I32)
        be_r = sb("be_r", [1, P], I32)
        slot_u = sb("slot_u", [P, ST * TOP], U32)
        ent_i = sb("ent_i", [P, ST * TOP, 2], I32)

        h2_dram = nc.dram_tensor("h2_rows", [S, D], F32, kind="Internal").ap()
        acc_dram = nc.dram_tensor("acc_rows", [ACC_ROWS, D], F32, kind="Internal").ap()
        list_dram = nc.dram_tensor("slot_list", [LIST_ROWS, 2], I32, kind="Internal").ap()
        be_dram = nc.dram_tensor("block_expert", [P, 1], I32, kind="Internal").ap()

        v_order, a_order = [], []
        a_order += ["norm1"] + [f"xl{i}" for i in range(6)]
        v_order += [f"gl{i}" for i in range(6)]
        for g in range(2):
            a_order += [f"{w}{3 * g + m}" for m in range(3) for w in ("r", "i")]
            a_order += [f"v{g}.{t}" for t in range(ST)]
        v_order += [f"gr{i}" for i in range(6)]
        for h in range(HEADS + 1):
            if h < HEADS:
                v_order += [f"q{h}", f"k{h}"]
            if h >= 2:
                a_order += [f"oss{h - 2}"]
            if h >= 1:
                v_order += [f"s{h - 1}.{c}" for c in range(ST)] + [f"o{h - 1}"]
        a_order += ["oss5"]
        a_order += [f"vs{t}" for t in range(ST)]
        v_order += [f"gs{i}" for i in range(4)] + [f"u{i}" for i in range(4)] + [f"mx{i}" for i in range(4)]
        v_order += [f"w{i}" for i in range(DK)]
        a_order += ["norm2"] + [f"g{i}" for i in range(DK)]
        v_order += [f"p{i}" for i in range(DK)]
        V = Groups(nc, ctx, "v", [0, 1, 2, 3, 4], v_order)
        A = Groups(nc, ctx, "a", [5, 6, 7], a_order)
        unit_last = [(V, "gl0"), (V, "gl1"), (V, "gl5"), (A, "i5"), (A, "v0.3"), (V, "gr1"), (V, "gr5"),
                     (V, "k1"), (V, "k3"), (V, "k5"), (A, "vs3"), (V, "gs3"), (V, "u3"),
                     (V, "w1"), (V, "w3"), (V, "w5"), (V, "w7"), (A, "g3"), (A, "g7"), (V, "p7")]
        assert len(unit_last) == UNITS_LAYER
        bv_order = [f"ada{j}" for j in range(12)] + [f"kc{i}" for i in range(2)] + [f"kx{i}" for i in range(2)]
        ba_order = ["norm0", "cnorm", "xnorm"] + [f"vc{t}" for t in range(2)] + [f"vx{t}" for t in range(ST)]
        ba_order += ["skc0", "skc1", "skx0", "skx1"]
        bv_order += [f"q{i}" for i in range(QH)]
        ba_order += [f"cb{i}" for i in range(4)] + [f"sq{i}" for i in range(QH)]
        ba_order += [f"cc{i}" for i in range(4)]
        bv_order += [f"cx{i}" for i in range(4)]
        BV = Groups(nc, ctx, "bv", [0, 1, 2, 3], bv_order)
        BA = Groups(nc, ctx, "ba", [4, 5, 6, 7], ba_order)
        CV = Groups(nc, ctx, "cv", [0, 1, 2, 3, 4, 5], [f"w{i}" for i in range(DK)] + ["logits", "pos"])
        CA = Groups(nc, ctx, "ca", [6, 7], ["norm2"] + [f"t{i}" for i in range(8)])
        DV = Groups(nc, ctx, "dv", [0, 1, 2, 3, 4, 5], [f"t{i}" for i in range(8)])

        const_in = sem("const_in")
        x_in = sem("x_in")
        pos_in = sem("pos_in")
        w_in = [sem(f"unit_in{i}") for i in range(RING)]
        sgu_in = sem("sgu_in")
        h_ready = sem("h_ready")
        sq_ready, sq_free = sem("sq_ready"), sem("sq_free")
        std_ready, std_free = sem("std_ready"), sem("std_free")
        y_ready = sem("y_ready")
        pool_turns = sem("pool_turns")
        xl_ready, xl_free = sem("xl_ready"), sem("xl_free")
        xc_ready = sem("xc_ready")
        th_ready = sem("th_ready")
        ri_ready = sem("ri_ready")
        la_ready = sem("la_ready")
        at_ready = sem("at_ready")
        ratio_ready = sem("ratio_ready")
        us_ready = sem("us_ready")
        lru_done = sem("lru_done")
        vn_ready = sem("v_natural_ready")
        qk_ready = sem("qk_ready")
        s_ready = sem("s_ready")
        vs_ready = sem("vs_ready")
        var_ready = sem("var_ready")
        sgu_std = sem("sgu_std")
        vn2_ready = sem("gating_v_ready")
        mix_ready = sem("mix_ready")
        pg_ready = sem("ple_gate_ready")
        prep_v, prep_a = sem("prep_v"), sem("prep_a")

        NSQ, NSTD = 22, 8
        prep = sb("prep", [P, 7, L * LRU_T])
        prep_t, prep_n, prep_w, prep_e, prep_l, prep_c, prep_r = (
            prep[:, i, :].rearrange("p (l t) -> p l t", l=L) for i in range(7))

        tail_last = [(BV, f"ada{j}") for j in range(12)] + [
            (BA, f"vx{ST - 1}"), (BV, f"q{QH - 1}"), (BA, "cb3"), (BA, "cc3"), (BV, "cx3"),
            (CV, "w3"), (CV, "w7"), (CV, "logits")]
        f_ready, fm_ready = sem("x_ready"), sem("x_modulated")
        c_in, cm_ready, cmm_ready = sem("ctx_in"), sem("ctx_scaled"), sem("ctx_modulated")
        y2_ready = sem("x_shifted")
        cond_ready = sem("cond_ready")
        sq2_ready, sq2_free, std2_ready, std2_free = (sem(f"{n}2") for n in ("sqr", "sqf", "stdr", "stdf"))
        late_in = sem("late_const_in")
        v_done, qkv_done = sem("v_done"), sem("qkv_done")
        cb_ready, cc_ready = sem("cb_ready"), sem("cc_ready")
        sc_full, max_ready, exp_ready, prob_ready = sem("sc_full"), sem("max_ready"), sem("exp_ready"), sem("prob_ready")
        pt_full, pt_ready, o_full, o_ready = sem("pt_full"), sem("pt_ready"), sem("o_full"), sem("o_ready")
        conv_ready = sem("conv_ready")
        h3_ready, n2_scaled, h2_ready = sem("h3_ready"), sem("norm2_scaled"), sem("h2_ready")
        h2n_ready, h2_out = sem("h2n_ready"), sem("h2_out")
        chosen_ready, gate_exp, gate_d = sem("chosen_ready"), sem("gate_exp"), sem("gate_d")
        ent_ready, be_ready, be_out, be_in, np_ready = (sem(n) for n in ("ent_ready", "be_ready", "be_out", "be_in", "np_ready"))
        list_init, list_out, acc_init = sem("list_init"), sem("list_out"), sem("acc_init")

        ATT_SCALE = float(P) ** -0.5
        SH1, SC1, GT1, SH2, SC2, GT2 = range(0, 48, 8)

        def tail_sp(sp):
            for t in range(RING, UNITS_TAIL):
                pool, g = tail_last[t - RING]
                sp.wait_ge(pool.full, pool.done(0, g))
                sp.dma_start(ring[:, t % RING, :], io["units"][L * UNITS_LAYER + t]).then_inc(w_in[t % RING], 16)
            for t in range(ST):
                sp.wait_ge(h2n_ready, t + 1)
                sp.dma_start(h2_dram[t * P:(t + 1) * P, :], h2n[:, t, :]).then_inc(h2_out, 16)
            sp.wait_ge(be_ready, 1)
            sp.dma_start(be_dram[:, :], be_i[:]).then_inc(be_out, 16)
            sp.wait_ge(be_out, 16)
            sp.dma_start(be_r[:], be_dram.rearrange("p a -> a p")).then_inc(be_in, 16)
            experts_sp(sp)

        def tail_pe(pe, mm):
            def need(t):
                pe.wait_ge(w_in[t % RING], 16 * ((L * UNITS_LAYER + t) // RING + 1))
                return ring[:, t % RING, :].rearrange("p (k n) -> p k n", k=DK)

            def slot(t):
                return ring[:, t % RING, :].rearrange("p (k n) -> p k n", k=DK)

            def group(pool, g, pairs, out=None, cols=S):
                pe.wait_ge(pool.free, pool.reusable(0, g))
                out = ps[:, pool.bank(g), 0:cols] if out is None else out
                for j, (a, b) in enumerate(pairs):
                    m = mm(out, a, b, j == 0, j == len(pairs) - 1)
                m.then_inc(pool.full, 1)

            def sums(pool, g, first, n, free_n=True, cols=S):
                pe.wait_ge(pool.free, pool.reusable(0, g))
                for k in range(n):
                    pe.wait_ge(sq2_ready, first + k + 1)
                    m = mm(ps[:, pool.bank(g), 0:cols], ones[:], sq2[:, (first + k) % 2, 0:cols], k == 0, k == n - 1)
                    if k < n - 2:
                        m.then_inc(sq2_free, 1)
                m.then_inc(pool.full, 1)

            pe.wait_ge(V.free, L * V.n + len(V.banks))
            pe.wait_ge(A.free, L * A.n + len(A.banks))
            pe.wait_ge(cond_ready, 1)

            def modulation(j):
                g = f"ada{j}"
                w = need(j)
                pe.wait_ge(BV.free, BV.reusable(0, g))
                for i in range(4):
                    for k in range(DK):
                        m = mm(ps[:, BV.bank(g), 2 * i:2 * i + 2], w[:, k, i * P:(i + 1) * P], cond[:, k, :],
                               k == 0, k == DK - 1)
                m.then_inc(BV.full, 1)

            for j in range(4):
                modulation(j)
            sums(BA, "norm0", 0, DK)
            for j in range(4, 12):
                modulation(j)
            sums(BA, "cnorm", DK, DK, cols=CTX)
            sums(BA, "xnorm", 2 * DK, DK)

            w = need(12)
            pe.wait_ge(cmm_ready, DK)
            for i in range(KVH):
                group(BV, f"kc{i}", [(w[:, k, i * P:(i + 1) * P], hcT[:, k, :]) for k in range(DK)], cols=CTX)
            pe.wait_ge(y2_ready, DK)
            for i in range(KVH):
                group(BV, f"kx{i}", [(w[:, k, i * P:(i + 1) * P], yT[:, k, :]) for k in range(DK)])
            for t in range(2):
                group(BA, f"vc{t}", [(hcT[:, k, t * P:(t + 1) * P], w[:, k, 256:512]) for k in range(DK)], cols=256)
            for t in range(ST):
                group(BA, f"vx{t}", [(yT[:, k, t * P:(t + 1) * P], w[:, k, 256:512]) for k in range(DK)], cols=256)
            for i, g in enumerate(("skc0", "skc1", "skx0", "skx1")):
                sums(BA, g, 3 * DK + i, 1, cols=CTX if i < 2 else S)
            w = need(13)
            for i in range(QH):
                group(BV, f"q{i}", [(w[:, k, i * P:(i + 1) * P], yT[:, k, :]) for k in range(DK)])
            w = need(14)
            for i in range(4):
                group(BA, f"cb{i}", [(w[:, k, i * P:(i + 1) * P], yT[:, k, :]) for k in range(DK)])
            for i in range(QH):
                sums(BA, f"sq{i}", 3 * DK + 4 + i, 1)
            w = need(15)
            for i in range(4):
                group(BA, f"cc{i}", [(w[:, k, i * P:(i + 1) * P], yT[:, k, :]) for k in range(DK)])
            w = need(16)
            for i in range(4):
                group(BV, f"cx{i}", [(w[:, k, i * P:(i + 1) * P], yT[:, k, :]) for k in range(DK)])

            pe.wait_ge(BV.free, BV.n + len(BV.banks))
            pe.wait_ge(BA.free, BA.n + len(BA.banks))
            pe.wait_ge(qkv_done, 1)

            def scores(n):
                h, t, b = n // ST, n % ST, 2 * (n % 2)
                if n >= 2:
                    pe.wait_ge(exp_ready, n - 1)
                q = qTa[:, h, t * P:(t + 1) * P]
                mm(ps[:, b, :], q, kTa[:, h // 2, 0:S], True, True)
                mm(ps[:, b + 1, 0:CTX], q, kTa[:, h // 2, S:KEYS], True, True).then_inc(sc_full, 1)

            def turned(n):
                pe.wait_ge(prob_ready, n + 1)
                if n >= 1:
                    pe.wait_ge(pt_ready, n)
                for j in range(KT):
                    m = pe.transpose(ps[:, 4 + j // 4, (j % 4) * P:(j % 4 + 1) * P],
                                     prob[:, n % 2, j * P:(j + 1) * P], ident[:])
                m.then_inc(pt_full, 1)

            scores(0)
            for n in range(QH * ST):
                if n + 1 < QH * ST:
                    scores(n + 1)
                turned(n)
                if n % ST == ST - 1:
                    h = n // ST
                    pe.wait_ge(pt_ready, n + 1)
                    if h >= 1:
                        pe.wait_ge(o_ready, h)
                    for j in range(KT):
                        m = mm(ps[:, 6, :], vall[:, j, (h // 2) * P:(h // 2 + 1) * P], eT[:, j, :], j == 0, j == KT - 1)
                    m.then_inc(o_full, 1)
            pe.wait_ge(o_ready, QH)
            pe.wait_ge(conv_ready, 4)
            for m_ in range(DK):
                w = need(17 + m_ // 4) if m_ % 4 == 0 else slot(17 + m_ // 4)
                group(CV, f"w{m_}", [(w[:, k, (m_ % 4) * P:(m_ % 4 + 1) * P], mix[:, 8 + k, :]) for k in range(DK)])
            sums(CA, "norm2", 3 * DK + 8, DK)

            w = need(19)
            g = "logits"
            pe.wait_ge(CV.free, CV.reusable(0, g))
            pe.wait_ge(h2_ready, DK)
            for t in range(ST):
                for k in range(DK):
                    m = mm(ps[:, CV.bank(g), t * E_N:(t + 1) * E_N], yT[:, k, t * P:(t + 1) * P], w[:, k, 0:E_N],
                           k == 0, k == DK - 1)
            m.then_inc(CV.full, 1)
            for i in range(8):
                g, t = f"t{i}", i // 2
                pe.wait_ge(CA.free, CA.reusable(0, g))
                for j in range(4):
                    m = pe.transpose(ps[:, CA.bank(g), j * P:(j + 1) * P],
                                     yT[:, 4 * (i % 2) + j, t * P:(t + 1) * P], ident[:])
                m.then_inc(CA.full, 1)
            g = "pos"
            pe.wait_ge(chosen_ready, 1)
            pe.wait_ge(CV.free, CV.reusable(0, g))
            for t in range(ST + 1):
                for t2 in range(min(t + 1, ST)):
                    lhs = before[:] if t2 == t else ones[:]
                    m = mm(ps[:, CV.bank(g), t * E_N:(t + 1) * E_N], lhs, chosen[:, t2, :], t2 == 0, t2 == min(t, ST - 1))
            m.then_inc(CV.full, 1)
            experts_pe(pe, mm)

        def tail_act(act, squares, root):
            sk = dict(rd=sq2_ready, fr=sq2_free)

            def copy(out, pool, g, cols=S):
                act.wait_ge(pool.full, pool.done(0, g))
                nc.scalar.activation(out, ps[:, pool.bank(g), 0:cols], ACT.Copy).then_inc(pool.free, 1)

            def root2(pool, g, i, width, cols=S):
                root(pool, g, 0, i, width, std2, cols=cols, ready=std2_ready, free=std2_free)
                act.drain().then_inc(pool.free, 1)

            squares(0, DK, lambda k: hT[:, k, :], h_ready, lambda k: L * 2 * DK + k + 1, sq2, free_at=0, **sk)
            root2(BA, "norm0", 0, D)
            act.wait_ge(c_in, 16)
            squares(DK, DK, lambda k: ctxT[:, k, :], c_in, lambda k: 16, sq2, cols=CTX, free_at=DK - 2, **sk)
            root2(BA, "cnorm", 1, D, cols=CTX)
            squares(2 * DK, DK, lambda k: hT[:, k, :], f_ready, lambda k: k + 1, sq2, free_at=2 * (DK - 2), **sk)
            root2(BA, "xnorm", 2, D)

            def shift(tile, k, row, who, ready, at, out):
                act.wait_ge(ready, at)
                nc.scalar.activation(tile, tile, ACT.Identity, bias=ada[:, row + k, who:who + 1]).then_inc(out, 1)

            for k in range(DK):
                shift(hcT[:, k, :], k, SH1, 1, cm_ready, k + 1, cmm_ready)
            for k in range(DK):
                shift(yT[:, k, :], k, SH1, 0, fm_ready, k + 1, y2_ready)

            def head_square(i, pool, g, cols=S):
                squares(3 * DK + i, 1, lambda k: ps[:, pool.bank(g), 0:cols], pool.full, lambda k: pool.done(0, g),
                        sq2, cols=cols, **sk)

            head_square(0, BV, "kc0", CTX)
            head_square(1, BV, "kc1", CTX)
            for t in range(2):
                copy(vall[:, ST + t, :], BA, f"vc{t}", 256)
            for t in range(ST):
                copy(vall[:, t, :], BA, f"vx{t}", 256)
            root2(BA, "skc0", 3, P, cols=CTX)
            head_square(2, BV, "kx0")
            root2(BA, "skc1", 4, P, cols=CTX)
            head_square(3, BV, "kx1")
            root2(BA, "skx0", 5, P)
            root2(BA, "skx1", 6, P)
            head_square(4, BV, "q0")
            head_square(5, BV, "q1")
            for i in range(4):
                copy(mix[:, 12 + i, :], BA, f"cb{i}")
            act.drain().then_inc(cb_ready, 1)
            for i in range(QH):
                root2(BA, f"sq{i}", 7 + i, P)
                if i < 2:
                    head_square(6 + i, BV, f"q{2 + i}")
            for i in range(4):
                copy(ccb[:, i, :], BA, f"cc{i}")
            act.drain().then_inc(cc_ready, 1)

            for n in range(QH * ST):
                act.wait_ge(max_ready, n + 1)
                if n >= 2:
                    act.wait_ge(pt_full, n - 1)
                b = 2 * (n % 2)
                s_ = ps[:, b:b + 2, :].rearrange("p a b -> p (a b)")[:, 0:KEYS]
                nc.scalar.activation(prob[:, n % 2, :], s_, ACT.Exp, bias=small[:, 16 + n % 2:17 + n % 2],
                                     scale=ATT_SCALE, accum_out=small[:, 18 + n % 2:19 + n % 2]).then_inc(exp_ready, 1)
                if n >= 1:
                    turned_copy(act, n - 1)
            turned_copy(act, QH * ST - 1)

            squares(3 * DK + 8, DK, lambda k: hT[:, k, :], h3_ready, lambda k: k + 1, sq2, free_at=3 * (DK - 2), **sk)
            root2(CA, "norm2", 11, D)
            for k in range(DK):
                shift(yT[:, k, :], k, SH2, 0, n2_scaled, k + 1, h2_ready)
            for i in range(8):
                t = i // 2
                copy(h2n[:, t, (i % 2) * S:(i % 2 + 1) * S], CA, f"t{i}")
                if i % 2:
                    act.drain().then_inc(h2n_ready, 1)
            act.wait_ge(gate_d, 1)
            nc.scalar.activation(gates, gates, ACT.Exp).then_inc(gate_exp, 1)
            experts_act(act)

        def turned_copy(act, n):
            act.wait_ge(pt_full, n + 1)
            t = n % ST
            src = ps[:, 4:6, :].rearrange("p a b -> p (a b)")[:, 0:KEYS].rearrange("p (j q) -> p j q", j=KT)
            nc.scalar.activation(eT[:, :, t * P:(t + 1) * P], src, ACT.Copy).then_inc(pt_ready, 1)

        def tail_dve(dve, inverse, rope):
            def full(pool, g, cols=S):
                dve.wait_ge(pool.full, pool.done(0, g))
                return ps[:, pool.bank(g), 0:cols]

            dve.sem_inc(BV.free, len(BV.banks))
            dve.sem_inc(BA.free, len(BA.banks))
            dve.sem_inc(std2_free, 2)

            def modulation(j):
                x = full(BV, f"ada{j}")[:, 0:8].rearrange("p (m c) -> p m c", m=4)
                b = q_(par2, "b_ada", 4 * j, 4).unsqueeze(2).to_broadcast([P, 4, 2])
                nc.vector.tensor_tensor(ada[:, 4 * j:4 * j + 4, :], x, b, ALU.add).then_inc(BV.free, 1)

            for j in range(4):
                modulation(j)
            r = inverse(0, std2_ready, 1, std2)
            for k in range(DK):
                nc.vector.scalar_tensor_tensor(hT[:, k, :], hT[:, k, :], q_(par2, "final_norm", k), r, ALU.mult,
                                               ALU.mult).then_inc(f_ready, 1)
            dve.drain().then_inc(std2_free, 1)
            for j in range(4, 12):
                modulation(j)
            dve.drain()
            for i, (sc, who, gn) in enumerate(((SC1, 0, "g_norm1"), (SC1, 1, "g_norm1"), (SC2, 0, "g_norm2"))):
                nc.vector.scalar_tensor_tensor(coef[:, i, :], ada[:, sc:sc + DK, who], 1.0, q_(par2, gn, 0, DK),
                                               ALU.add, ALU.mult)
            dve.drain()
            r = inverse(1, std2_ready, 2, std2, cols=CTX)
            for k in range(DK):
                nc.vector.scalar_tensor_tensor(hcT[:, k, :], ctxT[:, k, :], coef[:, 1, k:k + 1], r, ALU.mult,
                                               ALU.mult).then_inc(cm_ready, 1)
            dve.drain().then_inc(std2_free, 1)
            r = inverse(2, std2_ready, 3, std2)
            for k in range(DK):
                nc.vector.scalar_tensor_tensor(yT[:, k, :], hT[:, k, :], coef[:, 0, k:k + 1], r, ALU.mult,
                                               ALU.mult).then_inc(fm_ready, 1)
            dve.drain().then_inc(std2_free, 1)

            quads = [((a, a + 32), (b, b + 32)) for a, b in ((0, 32), (32, 0), (64, 96), (96, 64))]

            def head(i, g, gain, out, cols, rotate):
                x = full(BV, g, cols)
                r = inverse(3 + i, std2_ready, 3 + i + 1, std2, cols=cols)
                dst = tmp2[:, 0, :] if rotate else out
                nc.vector.scalar_tensor_tensor(dst, x, q_(par2, gain), r, ALU.mult, ALU.mult)
                dve.drain().then_inc(BV.free, 1)
                dve.sem_inc(std2_free, 1)
                if rotate:
                    rope(tmp2[:, 0, :], out, tmp2[:, 1, :], acos, asin, quads)
                    dve.drain()

            dve.wait_ge(late_in, 32)
            head(0, "kc0", "g_k", kTa[:, 0, S:KEYS], CTX, False)
            head(1, "kc1", "g_k", kTa[:, 1, S:KEYS], CTX, False)
            head(2, "kx0", "g_k", kTa[:, 0, 0:S], S, True)
            head(3, "kx1", "g_k", kTa[:, 1, 0:S], S, True)
            for i in range(QH):
                head(4 + i, f"q{i}", "g_q", qTa[:, i, :], S, True)
            dve.drain().then_inc(qkv_done, 1)

            nc.vector.memset(ubuf, 0.0)
            dve.wait_ge(cb_ready, 1)
            dve.wait_ge(cc_ready, 1)
            for i in range(4):
                x = full(BV, f"cx{i}")
                dve.drain()
                nc.vector.tensor_tensor(ubuf[:, 1:1 + S], x, ccb[:, i, :], ALU.mult)
                dve.drain().then_inc(BV.free, 1)
                t = tmp2[:, i % 2, :]
                nc.vector.tensor_scalar(t, ubuf[:, 0:S], q_(par2, "w_conv", i), None, ALU.mult)
                for w in (1, 2):
                    dve.drain()
                    nc.vector.scalar_tensor_tensor(t, ubuf[:, w:w + S], q_(par2, "w_conv", 4 * w + i), t, ALU.mult,
                                                   ALU.add)
                dve.drain()
                nc.vector.tensor_tensor(mix[:, 12 + i, :], mix[:, 12 + i, :], t, ALU.mult).then_inc(conv_ready, 1)

            def rows_max(n):
                b = 2 * (n % 2)
                dve.wait_ge(sc_full, n + 1)
                s_ = ps[:, b:b + 2, :].rearrange("p a b -> p (a b)")[:, 0:KEYS]
                nc.vector.reduce_max(small[:, 20 + n % 2:21 + n % 2], s_, AX.X)
                dve.drain()
                nc.vector.tensor_scalar(small[:, 16 + n % 2:17 + n % 2], small[:, 20 + n % 2:21 + n % 2], -ATT_SCALE, None,
                                        ALU.mult).then_inc(max_ready, 1)

            rows_max(0)
            for n in range(QH * ST):
                if n + 1 < QH * ST:
                    if n >= 1:
                        dve.wait_ge(exp_ready, n)
                    rows_max(n + 1)
                dve.wait_ge(exp_ready, n + 1)
                nc.vector.reciprocal(small[:, 22:23], small[:, 18 + n % 2:19 + n % 2])
                dve.drain()
                nc.vector.tensor_scalar(prob[:, n % 2, :], prob[:, n % 2, :], small[:, 22:23], None,
                                        ALU.mult).then_inc(prob_ready, 1)
                dve.drain()
                if n % ST == ST - 1:
                    h = n // ST
                    dve.wait_ge(o_full, h + 1)
                    nc.vector.tensor_copy(mix[:, 8 + h, :], ps[:, 6, :]).then_inc(o_ready, 1)

            dve.sem_inc(CV.free, len(CV.banks))
            dve.sem_inc(CA.free, len(CA.banks))
            for m in range(DK):
                nc.vector.scalar_tensor_tensor(hT[:, m, :], full(CV, f"w{m}"), ada[:, GT1 + m, 0:1], hT[:, m, :],
                                               ALU.mult, ALU.add).then_inc(h3_ready, 1)
                dve.drain().then_inc(CV.free, 1)
            r = inverse(11, std2_ready, 12, std2)
            for k in range(DK):
                nc.vector.scalar_tensor_tensor(yT[:, k, :], hT[:, k, :], coef[:, 2, k:k + 1], r, ALU.mult,
                                               ALU.mult).then_inc(n2_scaled, 1)
            dve.drain()

            x = full(CV, "logits")[:, 0:ST * E_N].rearrange("p (t e) -> p t e", t=ST)
            nc.vector.tensor_tensor(logits, x, brt[:].unsqueeze(1).to_broadcast([P, ST, E_N]), ALU.add)
            dve.drain().then_inc(CV.free, 1)
            for t in range(ST):
                nc.vector.max(mx8[:, t, :], logits[:, t, :])
            dve.drain()
            for t in range(ST):
                nc.vector.max_index(ix8[:, t, :].bitcast(U32), mx8[:, t, :], logits[:, t, :])
                nc.vector.tensor_scalar(gates[:, t, :], mx8[:, t, 0:TOP], mx8[:, t, 0:1], None, ALU.subtract)
            dve.drain().then_inc(gate_d, 1)
            nc.vector.tensor_copy(ixf, ix8.bitcast(U32))
            dve.drain()
            for t in range(ST):
                for k in range(TOP):
                    nc.vector.tensor_scalar(hot[:, t * TOP + k, :], cst[:, 0:E_N], ixf[:, t, k:k + 1], None, ALU.is_equal)
            dve.drain()
            hk = hot.rearrange("p (t k) e -> p t k e", k=TOP)
            nc.vector.tensor_tensor(chosen, hk[:, :, 0, :], hk[:, :, 1, :], ALU.add)
            for k in (2, 3):
                dve.drain()
                nc.vector.tensor_tensor(chosen, chosen, hk[:, :, k, :], ALU.add)
            dve.drain().then_inc(chosen_ready, 1)
            dve.wait_ge(gate_exp, 1)
            nc.vector.reduce_sum(gsum, gates, AX.X)
            dve.drain()
            nc.vector.reciprocal(gsum, gsum)
            dve.drain()
            nc.vector.tensor_tensor(gates, gates, gsum.unsqueeze(2).to_broadcast([P, ST, TOP]), ALU.mult)
            dve.drain()
            x = full(CV, "pos")
            nc.vector.tensor_copy(posn, x[:, 0:ST * E_N].rearrange("p (t e) -> p t e", t=ST))
            count = x[:, ST * E_N:(ST + 1) * E_N]
            nc.vector.tensor_scalar(nblk, count, 0.0, None, ALU.is_gt)
            nc.vector.memset(zer, 0.0)
            for t in range(1, ST):
                dve.drain()
                nc.vector.scalar_tensor_tensor(nblk, count, float(t * P), nblk, ALU.is_gt, ALU.add)
            dve.drain().then_inc(CV.free, 1)
            nc.vector.tensor_tensor_scan(pend, nblk, zer, 0.0, ALU.add, ALU.add)
            dve.drain()
            nc.vector.tensor_tensor(pbase, pend, nblk, ALU.subtract)
            nc.vector.tensor_scalar(ended, pend, q_(par2, "part"), None, ALU.is_le)
            nc.vector.tensor_scalar(hot2n, cst[:, E_N:E_N + 24], pend[:, E_N - 1:E_N], None, ALU.is_lt)
            dve.drain()
            nc.vector.reduce_sum(beI, ended, AX.X)
            nc.vector.reduce_sum(npI, hot2n, AX.X)
            nc.vector.tensor_scalar(pbase, pbase, float(P), None, ALU.mult)
            dve.drain()
            nc.vector.tensor_scalar(be_i[:], beI, float(E_N - 1), None, ALU.min).then_inc(be_ready, 1)
            nc.vector.tensor_copy(np_i[:], npI[0:1, :]).then_inc(np_ready, 1)
            nc.vector.tensor_tensor(posn, posn, pbase.unsqueeze(1).to_broadcast([P, ST, E_N]), ALU.add)
            dve.drain()
            h2k = hot2.rearrange("p (t k) e -> p t k e", k=TOP)
            for k in range(TOP):
                nc.vector.tensor_tensor(h2k[:, :, k, :], hk[:, :, k, :], posn, ALU.mult)
            dve.drain()
            nc.vector.reduce_sum(slotf, hot2, AX.X)
            nc.vector.tensor_copy(ent_i[:, :, 0], cst_i[:])
            nc.vector.tensor_copy(ent_i[:, :, 1].bitcast(F32), gates.rearrange("p t k -> p (t k)"))
            dve.drain()
            nc.vector.tensor_copy(slot_u[:], slotf)
            dve.drain().then_inc(ent_ready, 1)
            experts_dve(dve)

        n_in = [sem(f"expert_unit{j}") for j in range(6)]
        brow_in = [sem(f"bias_in{j}") for j in range(2)]
        lst_in, xg_in = sem("slots_in"), sem("rows_in")
        gu_full, dn_full, t_full, t_out = sem("gu_full"), sem("dn_full"), sem("t_full"), sem("t_out")
        glu_ready, th2_ready, act_ready = sem("glu_ready"), sem("tanh_ready"), sem("act_ready")
        ye_ready, scattered, y_free = sem("ye_ready"), sem("scattered"), sem("y_free")
        acc_in, fin_ready, out_done, z_ready = sem("acc_in"), sem("fin_ready"), sem("out_done"), sem("z_ready")
        sq3_ready, std3_ready = sem("sq3_ready"), sem("std3_ready")

        def eslot(j):
            if j < RING:
                return ring[:, j, :].rearrange("p (k n) -> p k n", k=DK)
            return mix[:, 8 * (j - RING):8 * (j - RING + 1), :]

        def eslot_flat(j):
            return ring[:, j, :] if j < RING else mix[:, 8 * (j - RING):8 * (j - RING + 1), :].rearrange("p a b -> p (a b)")

        def block_pairs(eng):
            eng.wait_ge(np_ready, 1)
            return eng.value_load(np_i[0:1, 0:1], min_val=1, max_val=BLOCKS // 2)

        def experts_sp(sp):
            sp.wait_ge(be_in, 16)
            n = block_pairs(sp)
            sp.wait_ge(CV.full, CV.n)
            with sp.Fori(0, n) as i:
                for s in range(2):
                    b = 2 * i + s
                    e = sp.value_load(be_r[0:1, bass.ds(b, 1)], min_val=0, max_val=E_N - 1)
                    sp.wait_ge(dn_full, 2 * b + 2)
                    sp.dma_start(brow[0:1, s, :], io["b_moe"][bass.ds(e, 1), :]).then_inc(brow_in[s], 16)
                    for j in range(6):
                        if j < 4:
                            sp.wait_ge(gu_full, 4 * b + j + 1)
                        else:
                            sp.wait_ge(dn_full, 2 * b + 4)
                        sp.dma_start(eslot_flat(j).unsqueeze(1),
                                     io["w_moe"][bass.ds(6 * e + j, 1)].rearrange("a p n -> p a n")).then_inc(n_in[j], 16)
            final_sp(sp)

        def experts_pe(pe, mm):
            n = block_pairs(pe)
            pe.wait_ge(CA.free, CA.n + len(CA.banks))
            pe.wait_ge(CV.free, CV.n + len(CV.banks))
            pe.sem_inc(gu_full, 4)
            pe.sem_inc(dn_full, 4)

            def turn(src, bank):
                for j in range(4):
                    m = pe.transpose(ps[:, bank, j * P:(j + 1) * P], src[:, j * P:(j + 1) * P], ident[:])
                m.then_inc(t_full, 1)

            pe.wait_ge(xg_in, 16)
            turn(xg[:, 0, 0:S], 6)
            turn(xg[:, 0, S:D], 7)
            with pe.Fori(0, n) as i:
                for s in range(2):
                    b = 2 * i + s
                    pe.wait_ge(t_out, 4 * b + 2)
                    pe.wait_ge(brow_in[s], 16 * i + 16)

                    def first(j):
                        pe.wait_ge(n_in[j], 16 * b + 16)
                        w = eslot(j)
                        mm(ps[:, j, :], ones[0:1, :], brow[0:1, s, j * S:(j + 1) * S], True, False)
                        for k in range(DK):
                            m = mm(ps[:, j, :], xgT[:, s, k * P:(k + 1) * P], w[:, k, :], False, k == DK - 1)
                        m.then_inc(gu_full, 1)

                    def second(ks):
                        for j in range(2):
                            if ks[0] == 0:
                                pe.wait_ge(n_in[4 + j], 16 * b + 16)
                                mm(ps[:, 4 + j, :], ones[0:1, :], brow[0:1, s, (4 + j) * S:(5 + j) * S], True, False)
                            w = eslot(4 + j)
                            for k in ks:
                                m = mm(ps[:, 4 + j, :], hTe[:, k * P:(k + 1) * P], w[:, k, :], False, k == DK - 1)
                            if ks[-1] == DK - 1:
                                m.then_inc(dn_full, 1)

                    for j in range(3):
                        first(j)
                    pe.wait_ge(act_ready, 2 * b + 1)
                    turn(h_sb[:, 0:S], 6)
                    first(3)
                    pe.wait_ge(ye_ready, 2 * b + 2)
                    pe.wait_ge(t_out, 4 * b + 3)
                    second(range(0, 4))
                    pe.wait_ge(xg_in, 16 * b + 32)
                    turn(xg[:, 1 - s, 0:S], 6)
                    pe.wait_ge(act_ready, 2 * b + 2)
                    turn(h_sb[:, S:D], 7)
                    pe.wait_ge(t_out, 4 * b + 5)
                    second(range(4, 8))
                    turn(xg[:, 1 - s, S:D], 7)
            final_pe(pe, mm)

        def experts_act(act):
            n = block_pairs(act)

            def turned_out(dst, bank, at, scale=1.0):
                act.wait_ge(t_full, at)
                nc.scalar.activation(dst, ps[:, bank, :], ACT.Copy, scale=scale).then_inc(t_out, 1)

            turned_out(xgT[:, 0, 0:S], 6, 1)
            turned_out(xgT[:, 0, S:D], 7, 2)
            with act.Fori(0, n) as i:
                for s in range(2):
                    b = 2 * i + s
                    act.wait_ge(glu_ready, 2 * b + 1)
                    nc.scalar.activation(thb, glu, ACT.Tanh, scale=ALPHA / 2).then_inc(th2_ready, 1)
                    turned_out(hTe[:, 0:S], 6, 4 * b + 3, 0.5)
                    act.wait_ge(glu_ready, 2 * b + 2)
                    nc.scalar.activation(thb, glu, ACT.Tanh, scale=ALPHA / 2).then_inc(th2_ready, 1)
                    turned_out(xgT[:, 1 - s, 0:S], 6, 4 * b + 4)
                    turned_out(hTe[:, S:D], 7, 4 * b + 5, 0.5)
                    turned_out(xgT[:, 1 - s, S:D], 7, 4 * b + 6)
            final_act(act)

        def experts_dve(dve):
            n = block_pairs(dve)
            dve.sem_inc(ye_ready, 2)
            dve.sem_inc(y_free, 2)
            with dve.Fori(0, n) as i:
                for s in range(2):
                    b = 2 * i + s
                    for half in range(2):
                        dve.wait_ge(gu_full, 4 * b + 2 * half + 5)
                        nc.vector.tensor_scalar(glu, ps[:, 2 * half, :], LIMIT, None, ALU.min).then_inc(glu_ready, 1)
                        dve.wait_ge(gu_full, 4 * b + 2 * half + 6)
                        nc.vector.tensor_scalar(lin, ps[:, 2 * half + 1, :], LIMIT, -LIMIT, ALU.min, ALU.max)
                        dve.wait_ge(th2_ready, 2 * b + half + 1)
                        nc.vector.scalar_tensor_tensor(glu, thb, 1.0, glu, ALU.add, ALU.mult)
                        dve.drain()
                        nc.vector.scalar_tensor_tensor(h_sb[:, half * S:(half + 1) * S], lin, 1.0, glu, ALU.add,
                                                       ALU.mult).then_inc(act_ready, 1)
                        dve.drain()
                    dve.wait_ge(y_free, b + 1)
                    for half in range(2):
                        dve.wait_ge(dn_full, 2 * b + half + 5)
                        nc.vector.tensor_scalar(y_sb[:, s, half * S:(half + 1) * S], ps[:, 4 + half, :],
                                                lst[:, s, 1:2].bitcast(F32), None, ALU.mult).then_inc(ye_ready, 1)
            final_dve(dve)

        def experts_pool(pool):
            n = block_pairs(pool)
            pool.wait_ge(list_out, 16 * ST * TOP)
            pool.wait_ge(h2_out, 16 * ST)
            nc.gpsimd.memset(xg, 0.0)
            pool.drain()

            def fetch(b, s, count):
                pool.dma_start(lst[:, s, :].unsqueeze(1),
                               list_dram.rearrange("(b p) c -> p b c", p=P)[:, bass.ds(b, 1), :]).then_inc(lst_in, 16)
                pool.wait_ge(lst_in, count)
                pool.sem_inc(pool_turns, 1)
                nc.gpsimd.indirect_dma_start(out=xg[:, s, :], out_offset=None, in_=h2_dram[:, :],
                                             in_offset=bass.IndirectOffsetOnAxis(ap=lst[:, s, 0:1].bitcast(U32), axis=0),
                                             bounds_check=S - 1, oob_is_err=False).then_inc(xg_in, 16)

            fetch(0, 0, 16)
            with pool.Fori(0, n) as i:
                for s in range(2):
                    b = 2 * i + s
                    fetch(b + 1, 1 - s, 16 * b + 32)
                    pool.wait_ge(ye_ready, 2 * b + 4)
                    pool.sem_inc(pool_turns, 1)
                    nc.gpsimd.indirect_dma_start(out=acc_dram[:, :],
                                                 out_offset=bass.IndirectOffsetOnAxis(ap=lst[:, s, 0:1].bitcast(U32), axis=0),
                                                 in_=y_sb[:, s, :], in_offset=None, compute_op=ALU.add).then_inc(scattered, 16)
                    pool.wait_ge(scattered, 16 * b + 16)
                    pool.sem_inc(y_free, 1)
            pool.wait_ge(xg_in, 32 * n + 16)
            pool.sem_inc(z_ready, 1)

        accn = yT[:].rearrange("p a b -> p (a b)").rearrange("p (t n) -> p t n", t=ST)

        def final_sp(sp):
            sp.wait_ge(z_ready, 1)
            for t in range(ST):
                sp.dma_start(accn[:, t, :], acc_dram[t * P:(t + 1) * P, :]).then_inc(acc_in, 16)
            for k in range(DK):
                sp.wait_ge(fin_ready, DK + k + 1)
                sp.dma_start(io["out"][k * P:(k + 1) * P, :], hT[:, k, :]).then_inc(out_done, 16)
            sp.wait_ge(out_done, 16 * DK)

        def final_pe(pe, mm):
            pe.wait_ge(acc_in, 16 * ST)
            pe.wait_ge(z_ready, 1)
            for k in range(DK):
                g = f"t{k}"
                pe.wait_ge(DV.free, DV.reusable(0, g))
                for t in range(ST):
                    m = pe.transpose(ps[:, DV.bank(g), t * P:(t + 1) * P], accn[:, t, k * P:(k + 1) * P], ident[:])
                m.then_inc(DV.full, 1)
            for k in range(DK):
                pe.wait_ge(sq3_ready, k + 1)
                m = mm(ps[:, 6, :], ones[:], xg_flat[:, k * S:(k + 1) * S], k == 0, k == DK - 1)
            m.then_inc(sq3_ready, 1)

        def final_act(act):
            act.drain()
            for k in range(DK):
                act.wait_ge(fin_ready, k + 1)
                nc.scalar.activation(xg_flat[:, k * S:(k + 1) * S], hT[:, k, :], ACT.Square).then_inc(sq3_ready, 1)
            act.wait_ge(sq3_ready, DK + 1)
            nc.scalar.activation(glu, ps[:, 6, :], ACT.Sqrt, bias=EPSC, scale=1.0 / D).then_inc(std3_ready, 1)

        def final_dve(dve):
            dve.sem_inc(DV.free, len(DV.banks))
            for k in range(DK):
                dve.wait_ge(DV.full, DV.done(0, f"t{k}"))
                nc.vector.scalar_tensor_tensor(hT[:, k, :], ps[:, DV.bank(f"t{k}"), :], ada[:, GT2 + k, 0:1],
                                               hT[:, k, :], ALU.mult, ALU.add).then_inc(fin_ready, 1)
                dve.drain().then_inc(DV.free, 1)
            dve.wait_ge(std3_ready, 1)
            nc.vector.reciprocal(glu, glu)
            dve.drain()
            for k in range(DK):
                nc.vector.scalar_tensor_tensor(hT[:, k, :], hT[:, k, :], q_(par2, "g_final", k), glu, ALU.mult,
                                               ALU.mult).then_inc(fin_ready, 1)

        xg_flat = scr[:, 0:4 * D]

        block = ctx.enter_context(nc.Block())

        @block.sync
        def _(sp):
            for kt in range(DK):
                sp.dma_start(hT[:, kt, :], io["xT"][kt * P:(kt + 1) * P, :]).then_inc(x_in, 16)
            for s in range(RING):
                sp.dma_start(ring[:, s, :], io["units"][s]).then_inc(w_in[s], 16)
            with sp.Fori(0, L) as layer:
                for u, (pool, g) in enumerate(unit_last):
                    sp.wait_ge(pool.full, pool.done(layer, g))
                    n = layer * UNITS_LAYER + (u + RING)
                    sp.dma_start(ring[:, u % RING, :].unsqueeze(1),
                                 io["units"][bass.ds(n, 1)].rearrange("a p n -> p a n")).then_inc(w_in[u % RING], 16)

            tail_sp(sp)

        def unit_landed(layer, u):
            return w_in[u % RING], 16 * (layer * (UNITS_LAYER // RING) + u // RING + 1)

        @block.tensor
        def _(pe):
            pe.wait_ge(const_in, 16 * N_CONST)

            def mm(out, lhsT, rhs, start, stop):
                return pe.matmul(out, lhsT, rhs, start=start, stop=stop)

            def norm_sums(pool, g, layer, first, n, ready, free, buf, cols=S, per=NSQ):
                pe.wait_ge(pool.free, pool.reusable(layer, g))
                for k in range(n):
                    pe.wait_ge(ready, layer * per + first + k + 1)
                    m = mm(ps[:, pool.bank(g), 0:cols], ones[:], buf[:, (first + k) % 2, 0:cols], k == 0, k == n - 1)
                    if k < n - 2:
                        m.then_inc(free, 1)
                m.then_inc(pool.full, 1)

            def project(pool, g, layer, w, rhs, n=DK):
                pe.wait_ge(pool.free, pool.reusable(layer, g))
                for k in range(n):
                    m = mm(ps[:, pool.bank(g), :], w(k), rhs(k), k == 0, k == n - 1)
                m.then_inc(pool.full, 1)

            def natural(pool, g, layer, t, w, cols):
                pe.wait_ge(pool.free, pool.reusable(layer, g))
                for k in range(DK):
                    m = mm(ps[:, pool.bank(g), 0:cols], yT[:, k, t * P:(t + 1) * P], w(k), k == 0, k == DK - 1)
                m.then_inc(pool.full, 1)

            with pe.Fori(0, L) as layer:
                def need(u):
                    s, value = unit_landed(layer, u)
                    pe.wait_ge(s, value)
                    return ring[:, u % RING, :]

                def columns(u, j):
                    w = need(u) if j == 0 else ring[:, u % RING, :]
                    w = w.rearrange("p (k n) -> p k n", k=DK)
                    return lambda k: w[:, k, j * P:(j + 1) * P]

                y = lambda k: yT[:, k, :]

                norm_sums(A, "norm1", layer, 0, DK, sq_ready, sq_free, sq)
                pe.wait_ge(y_ready, layer * 2 * DK + DK)
                for u in range(3):
                    for j in range(4):
                        if u < 2:
                            pool, g = (A, f"xl{3 * u + j}") if j < 3 else (V, f"gl{u}")
                        else:
                            pool, g = V, f"gl{2 + j}"
                        project(pool, g, layer, columns(u, j), y)

                wbd = need(3)[:, 0:2 * 2 * 7 * P].rearrange("p (w g n m) -> p w g n m", w=2, g=2, n=7)
                for g in range(2):
                    pe.wait_ge(xc_ready, layer * 6 + 3 * g + 3)
                    for m in range(3):
                        ks = [(n, k) for n, (k, mm_) in enumerate(PAIRS) if mm_ == m]
                        for wi, wn in enumerate(("r", "i")):
                            name = f"{wn}{3 * g + m}"
                            pe.wait_ge(A.free, A.reusable(layer, name))
                            for j, (n, k) in enumerate(ks):
                                x = mm(ps[:, A.bank(name), :], wbd[:, wi, g, n, :], xc[:, 3 * g + k, :],
                                       j == 0, j == len(ks) - 1)
                            x.then_inc(A.full, 1)
                    w = need(4 + g).rearrange("p (k n) -> p k n", k=DK)
                    cols = 512 if g == 0 else 256
                    for t in range(ST):
                        natural(A, f"v{g}.{t}", layer, t, lambda k: w[:, k, 0:cols], cols)
                for j in range(2):
                    w5 = ring[:, 5 % RING, :].rearrange("p (k n) -> p k n", k=DK)
                    project(V, f"gr{j}", layer, lambda k: w5[:, k, (2 + j) * P:(3 + j) * P], y)
                for j in range(4):
                    project(V, f"gr{2 + j}", layer, columns(6, j), y)

                def out_sums(h):
                    norm_sums(A, f"oss{h}", layer, DK + h, 1, sq_ready, sq_free, sq)

                for h in range(HEADS + 1):
                    if h < HEADS:
                        u, j = 7 + h // 2, 2 * (h % 2)
                        project(V, f"q{h}", layer, columns(u, j), y)
                        project(V, f"k{h}", layer, columns(u, j + 1), y)
                    if h >= 2:
                        out_sums(h - 2)
                    if h == 0:
                        pe.wait_ge(vn_ready, layer + 1)
                        continue
                    g = h - 1
                    pe.wait_ge(qk_ready, layer * HEADS + g + 1)
                    for c in range(ST):
                        name = f"s{g}.{c}"
                        pe.wait_ge(V.free, V.reusable(layer, name))
                        mm(ps[:, V.bank(name), 0:S - c * P], qk[:, 2 * (g % 2) + 1, c * P:(c + 1) * P],
                           qk[:, 2 * (g % 2), c * P:S], True, True).then_inc(V.full, 1)
                    pe.wait_ge(V.free, V.reusable(layer, f"o{g}"))
                    at_c = 0
                    for c in range(ST):
                        pe.wait_ge(s_ready, (layer * HEADS + g) * ST + c + 1)
                        n = S - c * P
                        x = mm(ps[:, V.bank(f"o{g}"), c * P:S], vnat[:, c, g * P:(g + 1) * P],
                               dec_s[:, at_c:at_c + n], c == 0, c == ST - 1)
                        at_c += n
                    x.then_inc(V.full, 1)
                out_sums(5)

                w = need(10).rearrange("p (k n) -> p k n", k=DK)
                for t in range(ST):
                    natural(A, f"vs{t}", layer, t, lambda k: w[:, k, :], S)
                for j in range(4):
                    project(V, f"gs{j}", layer, columns(11, j), y)
                for j in range(4):
                    project(V, f"u{j}", layer, columns(12, j), y)
                pe.wait_ge(vn2_ready, layer + 1)
                for g in range(SGU_G):
                    name = f"mx{g}"
                    pe.wait_ge(V.free, V.reusable(layer, name))
                    for c in range(ST):
                        x = mm(ps[:, V.bank(name), c * P:(c + 1) * P], vs[:, c, g * P:(g + 1) * P],
                               wsT[:, g, :], True, True)
                    x.then_inc(V.full, 1)

                pe.wait_ge(mix_ready, layer + 1)
                for m in range(DK):
                    w = (need(13 + m // 2) if m % 2 == 0 else ring[:, (13 + m // 2) % RING, :])
                    w = w.rearrange("p (k n) -> p k n", k=16)
                    project(V, f"w{m}", layer, lambda k: w[:, k, (m % 2) * P:(m % 2 + 1) * P],
                            lambda k: mix[:, k, :], 16)

                norm_sums(A, "norm2", layer, 14, DK, sq_ready, sq_free, sq)
                pe.wait_ge(y_ready, layer * 2 * DK + 2 * DK)
                for m in range(DK):
                    project(A, f"g{m}", layer, columns(17 + m // 4, m % 4), y)
                w = need(19)
                wp = w[:, 0:2 * D].rearrange("p (k n) -> p k n", k=2)
                pT = w[:, 2 * D:2 * D + 2 * S].rearrange("p (k n) -> p k n", k=2)
                for m in range(DK):
                    project(V, f"p{m}", layer, lambda k: wp[:, k, m * P:(m + 1) * P], lambda k: pT[:, k, :], 2)
            tail_pe(pe, mm)

        @block.scalar
        def _(act):
            act.wait_ge(const_in, 16 * N_CONST)

            act.wait_ge(prep_v, 1)
            nc.scalar.activation(prep_e, prep_n, ACT.Exp).then_inc(prep_a, 1)
            act.wait_ge(prep_v, 2)
            nc.scalar.activation(prep_l, prep_w, ACT.Ln).then_inc(prep_a, 1)
            nc.scalar.activation(cond[:], q_(par2, "cond", 0, 2 * DK).rearrange("p (k c) -> p k c", k=DK), ACT.Tanh,
                                 scale=0.5).then_inc(prep_a, 1)
            act.wait_ge(prep_v, 3)
            nc.scalar.activation(rcos, tmp[:, 0, :], ACT.Sin)
            nc.scalar.activation(rsin, tmp[:, 1, :], ACT.Sin).then_inc(prep_a, 1)

            def squares(first, n, tile, ready, ready_at, buf, cols=S, free_at=0, rd=None, fr=None):
                for k in range(n):
                    act.wait_ge(ready, ready_at(k))
                    if k >= 2:
                        act.wait_ge(fr or sq_free, free_at + k - 1)
                    nc.scalar.activation(buf[:, (first + k) % 2, 0:cols], tile(k), ACT.Square).then_inc(rd or sq_ready, 1)

            def root(pool, g, layer, i, width, out, cols=S, ready=None, free=None, per=NSTD):
                act.wait_ge(pool.full, pool.done(layer, g))
                act.wait_ge(free or std_free, layer * per + i + 1)
                nc.scalar.activation(out[:, i % 2, 0:cols], ps[:, pool.bank(g), 0:cols], ACT.Sqrt,
                                     bias=EPSC, scale=1.0 / width).then_inc(ready or std_ready, 1)

            with act.Fori(0, L) as layer:
                def full(pool, g):
                    pool_ = pool
                    act.wait_ge(pool_.full, pool_.done(layer, g))
                    return ps[:, pool.bank(g), :]

                squares(0, DK, lambda k: hT[:, k, :], h_ready, lambda k: layer * 2 * DK + k + 1, sq,
                        free_at=layer * 2 * (DK - 2))
                root(A, "norm1", layer, 0, D, std)
                act.drain().then_inc(A.free, 1)

                def gate(g, tile, i):
                    nc.scalar.activation(mix[:, tile, :], full(V, g), ACT.Tanh, scale=0.5).then_inc(th_ready, 1)

                for u in range(2):
                    for j in range(3):
                        i = 3 * u + j
                        x = full(A, f"xl{i}")
                        act.wait_ge(xl_free, layer * 6 + i + 1)
                        nc.scalar.activation(xl[:, i % 2, 4:4 + S], x, ACT.Copy).then_inc(xl_ready, 1)
                        act.drain().then_inc(A.free, 1)
                    gate(f"gl{u}", u, u)
                for i in range(2, 6):
                    gate(f"gl{i}", i, i)

                for g in range(2):
                    if g == 1:
                        act.wait_ge(lru_done, layer * 6 + 3)
                    for m in range(3):
                        i = 3 * g + m
                        nc.scalar.activation(mix[:, 9 + m, :], full(A, f"r{i}"), ACT.Tanh, scale=0.5,
                                             bias=par[:, PC["b_a"] + i:PC["b_a"] + i + 1]).then_inc(A.free, 1)
                        nc.scalar.activation(tmp[:, m, :], full(A, f"i{i}"), ACT.Tanh, scale=0.5,
                                             bias=par[:, PC["b_x"] + i:PC["b_x"] + i + 1]).then_inc(A.free, 1)
                        act.drain().then_inc(ri_ready, 1)
                    for m in range(3):
                        act.wait_ge(la_ready, layer * 6 + 3 * g + m + 1)
                        nc.scalar.activation(mix[:, 6 + m, :], mix[:, 9 + m, :], ACT.Exp)
                        nc.scalar.activation(mix[:, 9 + m, :], mix[:, 9 + m, :], ACT.Tanh).then_inc(at_ready, 1)
                    for t in range(ST):
                        cols = 512 if g == 0 else 256
                        nc.scalar.activation(vnat[:, t, 512 * g:512 * g + cols], full(A, f"v{g}.{t}")[:, 0:cols],
                                             ACT.Copy).then_inc(A.free, 1)
                    for m in range(3):
                        act.wait_ge(ratio_ready, layer * 6 + 3 * g + m + 1)
                        nc.scalar.activation(mix[:, 9 + m, :], mix[:, 9 + m, :], ACT.Sqrt).then_inc(us_ready, 1)
                act.drain().then_inc(vn_ready, 1)
                act.wait_ge(lru_done, layer * 6 + 6)
                for i in range(6):
                    gate(f"gr{i}", 6 + i, 6 + i)

                def out_root(h):
                    root(A, f"oss{h}", layer, 1 + h, P, std)
                    act.drain().then_inc(A.free, 1)

                for h in range(HEADS):
                    if h >= 1:
                        out_root(h - 1)
                    squares(DK + h, 1, lambda k: ps[:, V.bank(f"o{h}"), :], V.full,
                            lambda k: V.done(layer, f"o{h}"), sq)
                out_root(5)

                for t in range(ST):
                    x = full(A, f"vs{t}")
                    nc.scalar.activation(vs[:, t, :], x, ACT.Copy).then_inc(A.free, 1)
                act.drain().then_inc(vs_ready, 1)
                for j in range(4):
                    gate(f"gs{j}", 12 + j, 12 + j)
                act.wait_ge(var_ready, layer + 1)
                nc.scalar.activation(small[:, 0:ST], mv[:, :, 1], ACT.Sqrt, bias=EPSC).then_inc(sgu_std, 1)

                squares(14, DK, lambda k: hT[:, k, :], h_ready, lambda k: layer * 2 * DK + DK + k + 1, sq,
                        free_at=layer * 2 * (DK - 2) + DK - 2)
                root(A, "norm2", layer, 7, D, std)
                act.drain().then_inc(A.free, 1)
                for m in range(DK):
                    nc.scalar.activation(mix[:, m, :], full(A, f"g{m}"), ACT.Tanh, scale=0.5).then_inc(A.free, 1)
                    act.drain().then_inc(pg_ready, 1)
            tail_act(act, squares, root)

        @block.vector
        def _(dve):
            dve.sem_inc(V.free, len(V.banks))
            dve.sem_inc(A.free, len(A.banks))
            dve.sem_inc(std_free, 2)
            dve.sem_inc(xl_free, 2)
            nc.vector.memset(xl[:, :, 0:4], 0.0)
            nc.vector.memset(ones[:], 1.0)
            dve.wait_ge(const_in, 16 * N_CONST)

            lam = par_all[:, :, PC["lam"]:PC["lam"] + LRU_T]
            rate = par_all[:, :, PC["decay_rate"]:PC["decay_rate"] + LRU_T]
            nc.vector.tensor_scalar(prep_t, lam, -1.0, None, ALU.mult)
            dve.drain()
            nc.vector.tensor_tensor(prep_n, prep_t, lam, ALU.min).then_inc(prep_v, 1)
            dve.wait_ge(prep_a, 1)
            nc.vector.tensor_scalar(prep_w, prep_e, 1.0, None, ALU.add).then_inc(prep_v, 1)
            dve.wait_ge(prep_v, 2)
            nc.vector.tensor_scalar(prep_c, prep_w, -1.0, None, ALU.add)
            nc.vector.reciprocal(prep_r, prep_w)
            dve.drain()
            nc.vector.tensor_tensor(prep_c, prep_e, prep_c, ALU.subtract)
            nc.vector.tensor_scalar(prep_t, prep_t, 0.0, None, ALU.max)
            dve.drain()
            nc.vector.tensor_tensor(prep_c, prep_c, prep_r, ALU.mult)
            dve.drain()
            dve.wait_ge(prep_a, 2)
            nc.vector.tensor_tensor(prep_c, prep_c, prep_l, ALU.add)
            dve.drain()
            nc.vector.tensor_tensor(prep_c, prep_c, prep_t, ALU.add)
            dve.drain()
            nc.vector.tensor_scalar(rate, prep_c, -4.0, None, ALU.mult)
            for name in ("b_a", "b_x"):
                v = par_all[:, :, PC[name]:PC[name] + LRU_T]
                nc.vector.tensor_scalar(v, v, 0.5, None, ALU.mult)

            dve.wait_ge(prep_a, 3)
            nc.vector.scalar_tensor_tensor(cond[:], cond[:], 1.0, q_(par2, "cond", 0, 2 * DK).rearrange(
                "p (k c) -> p k c", k=DK), ALU.add, ALU.mult)
            dve.drain()
            nc.vector.tensor_scalar(cond[:], cond[:], 0.5, None, ALU.mult).then_inc(cond_ready, 1)

            dve.wait_ge(pos_in, 16)
            posi, ang, turn, turni = tmp[:, 2, :], tmp[:, 3, :], xc[:, 0, :], xc[:, 1, :]
            nc.vector.tensor_copy(ang, posi.bitcast(I32))
            dve.drain()
            nc.vector.tensor_scalar(ang, ang, q_(par2, "inv_freq"), None, ALU.mult)
            dve.drain()
            for out, quarter in ((tmp[:, 0, :], 0.25), (tmp[:, 1, :], 0.0)):
                nc.vector.tensor_scalar(turni.bitcast(I32), ang, 1.0 / (2 * np.pi), quarter, ALU.mult, ALU.add)
                dve.drain()
                nc.vector.tensor_copy(turn, turni.bitcast(I32))
                dve.drain()
                if quarter:
                    nc.vector.tensor_scalar(turn, turn, -quarter, None, ALU.add)
                    dve.drain()
                nc.vector.scalar_tensor_tensor(out, turn, -TWO_PI[0], ang, ALU.mult, ALU.add)
                dve.drain()
                for part in TWO_PI[1:]:
                    nc.vector.scalar_tensor_tensor(out, turn, -part, out, ALU.mult, ALU.add)
                    dve.drain()
                nc.vector.tensor_scalar(out, out, 3.1415925, -3.1415925, ALU.min, ALU.max)
                dve.drain()
            dve.sem_inc(prep_v, 1)
            dve.wait_ge(prep_a, 4)
            nc.vector.tensor_scalar(rsin, rsin, q_(par2, "rope_sign"), None, ALU.mult)
            dve.drain()
            dve.wait_ge(x_in, 16 * DK)
            dve.sem_inc(h_ready, DK)

            def p_(name, i, n=1):
                return par[:, PC[name] + i:PC[name] + i + n]

            def inverse(i, ready, free_at, buf, cols=S):
                dve.wait_ge(ready, free_at)
                r = buf[:, i % 2, 0:cols]
                nc.vector.reciprocal(r, r)
                dve.drain()
                return r

            def rope(src, dst, t, cos, sin, halves):
                nc.vector.tensor_tensor(dst, src, cos, ALU.mult)
                for a, b in halves:
                    nc.vector.tensor_tensor(t[b[0]:b[1]], src[a[0]:a[1]], sin[a[0]:a[1]], ALU.mult)
                dve.drain()
                return nc.vector.tensor_tensor(dst, dst, t, ALU.add)

            with dve.Fori(0, L) as layer:
                def full(pool, g):
                    dve.wait_ge(pool.full, pool.done(layer, g))
                    return ps[:, pool.bank(g), :]

                nc.vector.tensor_copy(par[:].unsqueeze(1), par_all[:, bass.ds(layer, 1), :])
                dve.drain()

                r = inverse(0, std_ready, layer * NSTD + 1, std)
                for k in range(DK):
                    nc.vector.scalar_tensor_tensor(yT[:, k, :], hT[:, k, :], p_("mix_norm", k), r, ALU.mult,
                                                   ALU.mult).then_inc(y_ready, 1)
                dve.drain().then_inc(std_free, 1)

                def silu2(g, tile, n):
                    x = full(V, g)
                    dve.wait_ge(th_ready, layer * 16 + n + 1)
                    nc.vector.scalar_tensor_tensor(mix[:, tile, :], mix[:, tile, :], 1.0, x, ALU.add,
                                                   ALU.mult).then_inc(V.free, 1)

                def conv(i):
                    dve.wait_ge(xl_ready, layer * 6 + i + 1)
                    x, o = xl[:, i % 2, :], xc[:, i, :]
                    nc.vector.tensor_scalar(o, x[:, 1:1 + S], p_("conv_w", i), p_("conv_b", i), ALU.mult, ALU.add)
                    for w in range(1, CONV):
                        dve.drain()
                        last = nc.vector.scalar_tensor_tensor(o, x[:, 1 + w:1 + w + S], p_("conv_w", w * LRU_T + i),
                                                              o, ALU.mult, ALU.add)
                    last.then_inc(xc_ready, 1)
                    dve.drain().then_inc(xl_free, 1)

                for u in range(2):
                    for j in range(3):
                        conv(3 * u + j)
                    silu2(f"gl{u}", u, u)
                for i in range(2, 6):
                    silu2(f"gl{i}", i, i)

                for g in range(2):
                    for m in range(3):
                        dve.wait_ge(ri_ready, layer * 6 + 3 * g + m + 1)
                        t = mix[:, 9 + m, :]
                        nc.vector.tensor_scalar(t, t, 1.0, p_("decay_rate", 3 * g + m), ALU.add,
                                                ALU.mult).then_inc(la_ready, 1)
                    for m in range(3):
                        dve.wait_ge(at_ready, layer * 6 + 3 * g + m + 1)
                        t, d = mix[:, 9 + m, :], tmp[:, 3, :]
                        nc.vector.tensor_scalar(d, t, -1.0, 1.0, ALU.mult, ALU.add)
                        dve.drain()
                        nc.vector.reciprocal(d, d)
                        dve.drain()
                        nc.vector.scalar_tensor_tensor(t, t, -2.0, d, ALU.mult, ALU.mult).then_inc(ratio_ready, 1)
                        dve.drain()
                    dve.wait_ge(A.full, A.done(layer, f"i{3 * g + 2}"))
                    for m in range(3):
                        i = 3 * g + m
                        x, a, uu = xc[:, i, :], mix[:, 6 + m, :], mix[:, 9 + m, :]
                        nc.vector.scalar_tensor_tensor(x, tmp[:, m, :], 1.0, x, ALU.add, ALU.mult)
                        dve.drain()
                        dve.wait_ge(us_ready, layer * 6 + i + 1)
                        nc.vector.scalar_tensor_tensor(uu, x, 0.5, uu, ALU.mult, ALU.mult)
                        dve.drain()
                        nc.vector.tensor_tensor_scan(x, a, uu, 0.0, ALU.mult, ALU.add)
                        dve.drain()
                        nc.vector.scalar_tensor_tensor(mix[:, i, :], x, 0.5, mix[:, i, :], ALU.mult,
                                                       ALU.mult).then_inc(lru_done, 1)
                dve.drain()
                for i in range(6):
                    silu2(f"gr{i}", 6 + i, 6 + i)
                dve.drain()

                def rotated(h):
                    for w, name in enumerate(("q", "k")):
                        x = full(V, f"{name}{h}")
                        last = rope(x, qk[:, 2 * (h % 2) + w, :], tmp[:, w, :], rcos, rsin,
                                    (((0, 64), (64, 128)), ((64, 128), (0, 64))))
                        dve.drain().then_inc(V.free, 1)
                    dve.drain().then_inc(qk_ready, 1)

                def normed(h):
                    r = inverse(1 + h, std_ready, layer * NSTD + 1 + h + 1, std)
                    nc.vector.scalar_tensor_tensor(mix[:, 6 + h, :], mix[:, 6 + h, :], 0.5, r, ALU.mult, ALU.mult)
                    dve.drain().then_inc(std_free, 1)

                rotated(0)
                for h in range(1, HEADS + 1):
                    if h < HEADS:
                        rotated(h)
                    if h >= 2:
                        normed(h - 2)
                    g, at_c = h - 1, 0
                    for c in range(ST):
                        x, n = full(V, f"s{g}.{c}"), S - c * P
                        nc.vector.tensor_tensor(dec_s[:, at_c:at_c + n], x[:, 0:n], decay[:, g, 0:n],
                                                ALU.mult).then_inc(s_ready, 1)
                        dve.drain().then_inc(V.free, 1)
                        at_c += n
                    x = full(V, f"o{g}")
                    dve.wait_ge(sq_ready, layer * NSQ + DK + g + 1)
                    nc.vector.scalar_tensor_tensor(mix[:, 6 + g, :], x, p_("ret_norm", g), mix[:, 6 + g, :],
                                                   ALU.mult, ALU.mult)
                    dve.drain().then_inc(V.free, 1)
                normed(5)

                dve.wait_ge(sgu_in, layer * 64 + 64)
                nc.vector.tensor_tensor(wsT, wsT, tri[:].unsqueeze(1).to_broadcast([P, SGU_G, P]), ALU.mult)
                dve.wait_ge(vs_ready, layer + 1)
                for t in range(ST):
                    nc.vector.bn_stats(bn[:, t, :], vs[:, t, :])
                dve.drain()
                for t in range(ST):
                    nc.vector.bn_aggr(mv[:, t, :], bn[:, t, :])
                dve.drain().then_inc(var_ready, 1)
                for j in range(4):
                    silu2(f"gs{j}", 12 + j, 12 + j)
                dve.wait_ge(sgu_std, layer + 1)
                nc.vector.reciprocal(small[:, 4:4 + ST], small[:, 0:ST])
                dve.drain()
                for t in range(ST):
                    nc.vector.tensor_scalar(vs[:, t, :], vs[:, t, :], mv[:, t, 0:1], small[:, 4 + t:5 + t],
                                            ALU.subtract, ALU.mult)
                for k, op in ((0, ALU.mult), (1, ALU.add)):
                    dve.drain()
                    for t in range(ST):
                        nc.vector.tensor_tensor(vs[:, t, :], vs[:, t, :], lngb[:, k, :], op)
                dve.drain().then_inc(vn2_ready, 1)
                for j in range(4):
                    x = full(V, f"u{j}")
                    nc.vector.scalar_tensor_tensor(mix[:, 12 + j, :], x, 0.5, mix[:, 12 + j, :], ALU.mult,
                                                   ALU.mult).then_inc(V.free, 1)
                for j in range(4):
                    x = full(V, f"mx{j}")
                    nc.vector.tensor_tensor(tmp[:, j, :].rearrange("p (c i) -> p c i", c=ST),
                                            x.rearrange("p (c i) -> p c i", c=ST),
                                            bsb[:, j, :].unsqueeze(1).to_broadcast([P, ST, P]),
                                            ALU.add).then_inc(V.free, 1)
                dve.drain()
                for j in range(4):
                    nc.vector.tensor_tensor(mix[:, 12 + j, :], mix[:, 12 + j, :], tmp[:, j, :], ALU.mult)
                dve.drain().then_inc(mix_ready, 1)

                for m in range(DK):
                    nc.vector.tensor_tensor(hT[:, m, :], full(V, f"w{m}"), hT[:, m, :], ALU.add).then_inc(h_ready, 1)
                    dve.drain().then_inc(V.free, 1)
                r = inverse(7, std_ready, layer * NSTD + 8, std)
                for k in range(DK):
                    nc.vector.scalar_tensor_tensor(yT[:, k, :], hT[:, k, :], p_("ple_norm", k), r, ALU.mult,
                                                   ALU.mult).then_inc(y_ready, 1)
                dve.drain().then_inc(std_free, 1)
                for m in range(DK):
                    x = full(V, f"p{m}")
                    dve.wait_ge(pg_ready, layer * DK + m + 1)
                    t = tmp[:, m % 2, :]
                    nc.vector.scalar_tensor_tensor(t, mix[:, m, :], 1.0, x, ALU.add, ALU.mult)
                    dve.drain().then_inc(V.free, 1)
                    nc.vector.scalar_tensor_tensor(hT[:, m, :], t, 0.5, hT[:, m, :], ALU.mult,
                                                   ALU.add).then_inc(h_ready, 1)
                dve.drain()
            tail_dve(dve, inverse, rope)

        @block.gpsimd
        def _(pool):
            for dst, name in ((ident[:], "ident"), (tri[:], "tri"), (before[:], "before"), (cst[:], "cst"),
                              (par_all[:], "par"), (par2[:], "par2"), (cst_i[:], "cst_i")):
                pool.dma_start(dst, io[name]).then_inc(const_in, 16)
            pool.dma_start(decay, io["decay"]).then_inc(const_in, 16)
            pool.dma_start(brt[:], io["b_router"].partition_broadcast(P)).then_inc(const_in, 16)
            pool.dma_start(tmp[:, 2, :].bitcast(I32), io["positions"].partition_broadcast(P)).then_inc(pos_in, 16)
            pool.dma_start(list_dram[:, :], io["list_init"]).then_inc(list_init, 16)
            for t in range(ACC_ROWS // P):
                pool.dma_start(acc_dram[t * P:(t + 1) * P, :], io["zeros"]).then_inc(acc_init, 16)
            for layer in range(L):
                if layer:
                    pool.wait_ge(mix_ready, layer)
                pool.dma_start(lngb[:, 0, :], io["ln_g"][layer].partition_broadcast(P)).then_inc(sgu_in, 16)
                pool.dma_start(lngb[:, 1, :], io["ln_b"][layer].partition_broadcast(P)).then_inc(sgu_in, 16)
                pool.dma_start(bsb, io["b_s"][layer].partition_broadcast(P)).then_inc(sgu_in, 16)
                pool.dma_start(wsT, io["wsT"][layer]).then_inc(sgu_in, 16)
            pool.wait_ge(h_ready, (2 * L + 1) * DK)
            pool.dma_start(ctxT, io["ctxT"]).then_inc(c_in, 16)
            pool.dma_start(acos, io["axial_cos"]).then_inc(late_in, 16)
            pool.dma_start(asin, io["axial_sin"]).then_inc(late_in, 16)

            pool.wait_ge(list_init, 16)
            pool.wait_ge(acc_init, 16 * (ACC_ROWS // P))
            pool.wait_ge(ent_ready, 1)
            for j in range(ST * TOP):
                nc.gpsimd.indirect_dma_start(out=list_dram[:, :],
                                             out_offset=bass.IndirectOffsetOnAxis(ap=slot_u[:, j:j + 1], axis=0),
                                             in_=ent_i[:, j, :], in_offset=None).then_inc(list_out, 16)
            experts_pool(pool)


def constants():
    f = np.float32
    p = np.arange(P)
    j = np.arange(S)
    log_g = np.log1p(-np.exp2(f(-5.0) - np.arange(HEADS, dtype=f))).astype(f)
    diff = j[None, :] - p[:, None]
    decay = np.where(diff[:, None, :] >= 0,
                     np.exp(np.maximum(diff, 0)[:, None, :] * log_g[None, :, None].astype(np.float64)), 0.0)
    half = np.arange(64, dtype=f)
    inv = (f(10000.0) ** (-half / f(64))).astype(f)
    inv2 = (f(10000.0) ** (-np.arange(0, 64, 2, dtype=f) / f(64))).astype(f)
    axis, i = p // 64, p % 32
    place = np.where(axis[:, None] == 0, (j // 64)[None, :], (j % 64)[None, :]).astype(f)
    ang = (place * inv2[i][:, None]).astype(f).astype(np.float64)
    sign = np.where((p // 32) % 2 == 0, 1.0, -1.0)[:, None]
    slots = np.arange(LIST_ROWS)
    return {
        "ident": np.eye(P, dtype=f), "tri": np.triu(np.ones((P, P), f)), "before": np.triu(np.ones((P, P), f), 1),
        "cst": np.tile(np.concatenate([np.arange(E_N), 2 * np.arange(24)]).astype(f), (P, 1)),
        "cst_i": (p[:, None] + P * (np.arange(ST * TOP) // TOP)[None, :]).astype(np.int32),
        "decay": (decay * P ** -0.5).astype(f),
        "axial_cos": np.cos(ang).astype(f), "axial_sin": (np.sin(ang) * sign).astype(f),
        "list_init": np.stack([S + slots % P, 0 * slots], 1).astype(np.int32),
        "inv_freq": inv[p % 64][:, None], "rope_sign": np.where(p < 64, 1.0, -1.0).astype(f)[:, None],
        "part": p.astype(f)[:, None], "zeros": np.zeros((P, D), f),
    }


def tiles(v):
    v = np.asarray(v)
    return np.moveaxis(v.reshape(*v.shape[:-1], -1, P), -1, 0)


def unit(w, k):
    w = w.reshape(k, P, -1).transpose(1, 0, 2).reshape(P, -1)
    return np.pad(w, ((0, 0), (0, UNIT - w.shape[1])))


def layout(x):
    c = constants()
    X = {k: np.asarray(v) for k, v in x.items()}
    units = []
    for l in range(L):
        w = X["w_in"][l]
        sizes = np.cumsum([0, 768, 768, 768, 768, 768, 768, 512, 512, 512])
        xl, gl, q, k, v, gr, u, vs, gs = (w[:, a:b] for a, b in zip(sizes[:-1], sizes[1:]))
        t = lambda m, i, n=1: m[:, i * P:(i + n) * P]
        cat = lambda *a: np.concatenate(a, axis=1)
        wbd = np.zeros((2, 2, len(PAIRS), P, P), np.float32)
        for wi, name in enumerate(("lru_w_a", "lru_w_x")):
            for g in range(2):
                for n, (kt, mt) in enumerate(PAIRS):
                    for b in range(4):
                        r0, r1 = max(kt * P, b * 96), min((kt + 1) * P, (b + 1) * 96)
                        c0, c1 = max(mt * P, b * 96), min((mt + 1) * P, (b + 1) * 96)
                        if r0 < r1 and c0 < c1:
                            wbd[wi, g, n, r0 - kt * P:r1 - kt * P, c0 - mt * P:c1 - mt * P] = \
                                X[name][l, 4 * g + b, r0 - b * 96:r1 - b * 96, c0 - b * 96:c1 - b * 96]
        lru = wbd.transpose(3, 0, 1, 2, 4).reshape(P, -1)
        mats = [cat(t(xl, 0, 3), t(gl, 0)), cat(t(xl, 3, 3), t(gl, 1)), t(gl, 2, 4), None,
                v[:, 0:512], cat(v[:, 512:], t(gr, 0, 2)), t(gr, 2, 4)]
        mats += [cat(t(q, 2 * i), t(k, 2 * i), t(q, 2 * i + 1), t(k, 2 * i + 1)) for i in range(3)]
        mats += [vs, gs, u]
        units += [np.pad(lru, ((0, 0), (0, UNIT - lru.shape[1]))) if m is None else unit(m, DK) for m in mats]
        units += [unit(X["w_out"][l][:, i * 256:(i + 1) * 256], 16) for i in range(4)]
        units += [unit(X["w_ple_gate"][l][:, i * 512:(i + 1) * 512], DK) for i in range(2)]
        wp = X["w_ple_proj"][l].reshape(2, P, D).transpose(1, 0, 2).reshape(P, -1)
        pT = X["p"][l, 0].T.reshape(2, P, S).transpose(1, 0, 2).reshape(P, -1)
        last = np.concatenate([wp, pT], axis=1)
        units.append(np.pad(last, ((0, 0), (0, UNIT - last.shape[1]))))
    w = X["w_ada_2"][0]
    units += [unit(w[:, i * 512:(i + 1) * 512], DK) for i in range(12)]
    w = X["w_in_2"][0]
    units += [unit(w[:, 512:1024], DK), unit(w[:, 0:512], DK)]
    units += [unit(w[:, 1024 + 512 * i:1536 + 512 * i], DK) for i in range(3)]
    w = X["w_out_2"][0]
    units += [unit(w[:, i * 512:(i + 1) * 512], DK) for i in range(2)]
    units.append(np.pad(X["w_router_2"][0].reshape(DK, P, E_N), ((0, 0), (0, 0), (0, 512 - E_N)))
                 .transpose(1, 0, 2).reshape(P, -1))
    assert len(units) == L * UNITS_LAYER + UNITS_TAIL

    gu = X["w_gate_up_2"][0].reshape(E_N, DK, P, 2, 2, 512)
    dn = X["w_down_2"][0].reshape(E_N, DK, P, 2, 512)
    w_moe = np.empty((E_N, 6, P, DK, 512), np.float32)
    for half in range(2):
        for part in range(2):
            w_moe[:, 2 * half + part] = gu[:, :, :, part, half].transpose(0, 2, 1, 3)
        w_moe[:, 4 + half] = dn[:, :, :, half].transpose(0, 2, 1, 3)
    bg = X["b_gate_up_2"][0].reshape(E_N, 2, 2, 512).transpose(0, 2, 1, 3).reshape(E_N, 2048)
    par = np.concatenate([tiles(X["mix_norm"]), tiles(X["ple_norm"]),
                          tiles(X["lru_conv_w"]).reshape(P, L, -1), tiles(X["lru_conv_b"]), tiles(X["lru_b_a"]),
                          tiles(X["lru_b_x"]), tiles(X["lru_lambda"]), tiles(X["ret_norm"]),
                          np.zeros((P, L, LRU_T), np.float32)], axis=2)
    cond = np.stack([tiles(X["c_2"][0]), tiles(X["c_ctx_2"])], axis=-1).reshape(P, -1)
    par2 = np.concatenate([tiles(X["final_norm"]), tiles(X["b_ada_2"][0]), tiles(X["g_norm1_2"][0]),
                           tiles(X["g_norm2_2"][0]), X["g_q_2"][0][:, None], X["g_k_2"][0][:, None],
                           tiles(X["w_conv_2"][0]).reshape(P, -1), tiles(X["g_final_2"]), cond,
                           c.pop("inv_freq"), c.pop("rope_sign"), c.pop("part")], axis=1)
    out = dict(c)
    out.update({
        "xT": X["x"][0].T, "units": np.stack(units), "w_moe": w_moe.reshape(E_N * 6, P, UNIT),
        "b_moe": np.concatenate([bg, X["b_down_2"][0]], axis=1), "par": par, "par2": par2,
        "b_router": X["b_router_2"][0], "positions": X["positions"][0],
        "ln_g": X["sgu_ln_g"], "ln_b": X["sgu_ln_b"], "b_s": X["sgu_b_s"],
        "wsT": X["sgu_w_s"].transpose(0, 3, 1, 2),
        "ctxT": X["ctx_2"][0].T.reshape(DK, P, CTX).transpose(1, 0, 2),
    })
    return {k: np.ascontiguousarray(v) for k, v in out.items()}


def kernel(**inputs):
    import concourse.bacc as bacc
    from concourse.bass_utils import run_bass_kernel_spmd as run

    nc = bacc.Bacc("TRN2", target_bir_lowering=False, num_devices=1)
    arrays = {f"in_{k}": v for k, v in layout(inputs).items()}
    io = {k[3:]: nc.dram_tensor(k, v.shape, mybir.dt.from_np(v.dtype), kind="ExternalInput").ap()
          for k, v in arrays.items()}
    io["out"] = nc.dram_tensor("out_T", (D, S), F32, kind="ExternalOutput").ap()
    build(nc, io)
    r = run(nc, [arrays], core_ids=[0])
    return np.ascontiguousarray(np.asarray(r.results[0]["out_T"]).T).reshape(1, S, D)
```

```python
from contextlib import ExitStack

import numpy as np
import concourse.bass as bass
from concourse import mybir

F32 = mybir.dt.float32
F32R = mybir.dt.float32r
I32 = mybir.dt.int32
U32 = mybir.dt.uint32
ALU = mybir.AluOpType
ACT = mybir.ActivationFunctionType
AX = mybir.AxisListType

N_CONST = 9
EPSC = EPS = 1e-6
_LOW = int((2 * np.pi - 6.28125) * 2 ** 21) / 2 ** 21
TWO_PI = (6.28125, _LOW, 2 * np.pi - 6.28125 - _LOW)

P = 128
S = 512
D = 1024
DK = D // P
ST = S // P
L = 2
LRU_T = 768 // P
LRU_BLOCK = 96
HEADS = 6
CONV = 4
SGU_G = 4
CTX = 256
QH, KVH = 4, 2
KEYS = S + CTX
KT = KEYS // P
E_N, TOP = 32, 4
DFF = 1024
LIMIT, ALPHA = 7.0, 1.702
BLOCKS = 48
LIST_ROWS = (BLOCKS + 1) * P
ACC_ROWS = S + P

UNIT = 4096
RING = 4
HALF = UNIT // 2
HALVES = 12
RAW, SPLIT = 6, 4
ORDER = [(j, q) for j in range(4) for q in range(2)] + [(4, 0), (5, 0), (4, 1), (5, 1)]
POOL_LOW = (2, 6, 10)
DVE_LOW = tuple(h for h in range(HALVES) if h not in POOL_LOW)
UNITS_LAYER = 20
UNITS_TAIL = 20

PC = {}
_n = 0
for _name, _w in (("mix_norm", DK), ("ple_norm", DK), ("conv_w", CONV * LRU_T), ("conv_b", LRU_T),
                  ("b_a", LRU_T), ("b_x", LRU_T), ("lam", LRU_T), ("ret_norm", HEADS),
                  ("decay_rate", LRU_T)):
    PC[_name] = _n
    _n += _w
NPAR = _n
QC = {}
_n = 0
for _name, _w in (("final_norm", DK), ("b_ada", 48), ("g_norm1", DK), ("g_norm2", DK), ("g_q", 1), ("g_k", 1),
                  ("w_conv", 12), ("g_final", DK), ("cond", 2 * DK), ("inv_freq", 1), ("rope_sign", 1),
                  ("part", 1), ("part32", 1)):
    QC[_name] = _n
    _n += _w
NPAR2 = _n


def q_(par2, name, i=0, n=1):
    return par2[:, QC[name] + i:QC[name] + i + n]


class Groups:

    def __init__(self, nc, ctx, name, banks, order):
        self.full = ctx.enter_context(nc.semaphore(f"{name}_full"))
        self.free = ctx.enter_context(nc.semaphore(f"{name}_free"))
        self.banks, self.order, self.n = banks, order, len(order)
        self.at = {g: i for i, g in enumerate(order)}
        assert len(self.at) == self.n

    def bank(self, g):
        return self.banks[self.at[g] % len(self.banks)]

    def done(self, layer, g):
        return layer * self.n + self.at[g] + 1

    def reusable(self, layer, g):
        i, c = self.at[g], len(self.banks)
        if i >= c:
            return layer * self.n + i + 1
        last = max(j for j in range(self.n) if j % c == i)
        return layer * self.n + last + 1 + c - self.n


def lru_pairs():
    return [(k, m) for m in range(3) for k in range(3)
            if any(max(k * P, b * LRU_BLOCK) < min((k + 1) * P, (b + 1) * LRU_BLOCK)
                   and max(m * P, b * LRU_BLOCK) < min((m + 1) * P, (b + 1) * LRU_BLOCK) for b in range(4))]


PAIRS = lru_pairs()


def build(nc, io, stop=99):
    ctx = ExitStack()
    with ctx:
        def sb(name, shape, dt=F32):
            return ctx.enter_context(nc.sbuf_tensor(name, shape, dt))

        def sem(name):
            return ctx.enter_context(nc.semaphore(name))

        hT = sb("hT", [P, DK, S])
        ident = sb("ident", [P, P])
        ones = sb("ones", [P, P])
        before = sb("before", [P, P])
        cst = sb("cst", [P, E_N + 24])
        cst_i = sb("cst_i", [P, ST * TOP], I32)
        brt = sb("router_bias", [P, E_N])
        cond = sb("cond", [P, DK, 2])
        tri = sb("tri", [P, P])
        par_all = sb("par_all", [P, L, NPAR])
        par = sb("par", [P, NPAR])
        par2 = sb("par2", [P, NPAR2])
        mv = sb("mv", [P, ST, 2])
        bn = sb("bn", [P, ST, 6])
        small = sb("small", [P, 64])
        ada = sb("ada", [P, 48, 2])
        coef = sb("coef", [P, 3, DK])
        lst_all = sb("slots", [P, BLOCKS + 1, 2], I32)
        lst = sb("lst", [P, 2, 2], I32)
        rows_i = sb("rows_i", [P, 2], I32)
        np_i = sb("np_i", [1, 1], I32)
        be_i = sb("be_i", [P, 1], I32)
        be_r = sb("be_r", [1, P], I32)
        slot_u = sb("slot_u", [P, ST * TOP], U32)
        ent_i = sb("ent_i", [P, ST * TOP, 2], I32)
        prep = sb("prep", [P, 7, L * LRU_T])
        scr_size = 17700
        early = ExitStack()
        mix = early.enter_context(nc.sbuf_tensor("mix", [P, 16, S], F32))
        ring = early.enter_context(nc.sbuf_tensor("ring", [P, RING, UNIT], F32))
        yT = early.enter_context(nc.sbuf_tensor("yT", [P, DK, S], F32))
        scr = early.enter_context(nc.sbuf_tensor("scr", [P, scr_size], F32))
        early.close()
        raw = sb("raw", [P, RAW, HALF])
        wsp = sb("w_split", [P, SPLIT, 2, HALF], F32R)
        hTe = sb("hidden_T", [P, 2, D], F32R)
        xgT = sb("rows_T", [P, 2, 2, D], F32R)
        xgy = sb("rows", [P, 4, D])
        h_sb = sb("hidden", [P, D])
        act_buf = sb("act_buf", [P, 3, S])
        b_split = sb("bias_split", [2 * E_N, 3 * D], F32R)
        sel = sb("expert_rows", [2 * E_N, 2, P], F32R)
        be_bc = sb("block_experts", [2 * E_N, P])
        be_bi = sb("block_experts_int", [2 * E_N, P], I32)
        xg, y_sb = xgy[:, 0:2, :], xgy[:, 2:4, :]
        b_raw = xgy[0:2 * E_N, 0:3, :].rearrange("p a b -> p (a b)")
        glu, thb, lin = (act_buf[:, i, :] for i in range(3))
        ps = ctx.enter_context(nc.psum_tensor("ps", [P, 8, 512], F32))

        def carve(at, *dims):
            n = int(np.prod(dims))
            assert at[0] + n <= scr_size, at
            v = scr[:, at[0]:at[0] + n]
            at[0] += n
            if len(dims) == 2:
                v = v.rearrange("p (a b) -> p a b", a=dims[0])
            return v

        at = [0]
        vnat = carve(at, ST, 768)
        decay = carve(at, HEADS, S)
        rcos, rsin = carve(at, S), carve(at, S)
        sq = carve(at, 2, S)
        std = carve(at, 2, S)
        tmp = carve(at, 4, S)
        xl = carve(at, 2, S + 4)
        work = carve(at, 3328)
        lngb = carve(at, 2, S)
        bsb = carve(at, SGU_G, P)
        wsT = carve(at, SGU_G, P)
        xc = work[:, 0:LRU_T * S].rearrange("p (a b) -> p a b", a=LRU_T)
        qk = work[:, 0:4 * S].rearrange("p (a b) -> p a b", a=4)
        dec_s = work[:, 4 * S:4 * S + 1280]
        vs = vnat[:, :, 0:S]

        at = [0]
        acos, asin = carve(at, S), carve(at, S)
        sq2 = carve(at, 2, S)
        std2 = carve(at, 2, S)
        tmp2 = carve(at, 4, S)
        kTa = carve(at, KVH, KEYS)
        vall = carve(at, KT, KVH * P)
        qTa = carve(at, QH, S)
        eT = carve(at, KT, S)
        prob = carve(at, 2, KEYS)
        ccb = carve(at, 4, S)
        ubuf = carve(at, S + 4)
        ctxT = mix[:, 0:4, :].rearrange("p a b -> p (a b)").rearrange("p (a b) -> p a b", a=DK)
        hcT = mix[:, 4:8, :].rearrange("p a b -> p (a b)").rearrange("p (a b) -> p a b", a=DK)

        at = [0]
        logits = carve(at, ST, E_N)
        mx8 = carve(at, ST, 8)
        ix8 = carve(at, ST, 8)
        ixf = carve(at, ST, 8)
        hot = carve(at, ST * TOP, E_N)
        hot2 = carve(at, ST * TOP, E_N)
        chosen = carve(at, ST, E_N)
        posn = carve(at, ST, E_N)
        nblk, pend, pbase, zer, ended = (carve(at, E_N) for _ in range(5))
        gates = carve(at, ST, TOP)
        gsum = carve(at, ST)
        slotf = carve(at, ST * TOP)
        beI, npI = carve(at, 1), carve(at, 1)
        hot2n = carve(at, 24)
        h2n = carve(at, ST, D)
        assert at[0] <= 6 * D

        h2_dram = nc.dram_tensor("h2_rows", [S, D], F32, kind="Internal").ap()
        acc_dram = nc.dram_tensor("acc_rows", [ACC_ROWS, D], F32, kind="Internal").ap()
        list_dram = nc.dram_tensor("slot_list", [LIST_ROWS, 2], I32, kind="Internal").ap()
        be_dram = nc.dram_tensor("block_expert", [P, 1], I32, kind="Internal").ap()

        v_order, a_order = [], []
        a_order += ["norm1"] + [f"xl{i}" for i in range(6)]
        v_order += [f"gl{i}" for i in range(6)]
        for g in range(2):
            a_order += [f"{w}{3 * g + m}" for m in range(3) for w in ("r", "i")]
            a_order += [f"v{g}.{t}" for t in range(ST)]
        v_order += [f"gr{i}" for i in range(6)]
        for h in range(HEADS + 1):
            if h < HEADS:
                v_order += [f"q{h}", f"k{h}"]
            if h >= 2:
                a_order += [f"oss{h - 2}"]
            if h >= 1:
                v_order += [f"s{h - 1}.{c}" for c in range(ST)] + [f"o{h - 1}"]
        a_order += ["oss5"]
        a_order += [f"vs{t}" for t in range(ST)]
        v_order += [f"gs{i}" for i in range(4)] + [f"u{i}" for i in range(4)] + [f"mx{i}" for i in range(4)]
        v_order += [f"w{i}" for i in range(DK)]
        a_order += ["norm2"] + [f"g{i}" for i in range(DK)]
        v_order += [f"p{i}" for i in range(DK)]
        V = Groups(nc, ctx, "v", [0, 1, 2, 3, 4], v_order)
        A = Groups(nc, ctx, "a", [5, 6, 7], a_order)
        unit_last = [(V, "gl0"), (V, "gl1"), (V, "gl5"), (A, "i5"), (A, "v0.3"), (V, "gr1"), (V, "gr5"),
                     (V, "k1"), (V, "k3"), (V, "k5"), (A, "vs3"), (V, "gs3"), (V, "u3"),
                     (V, "w1"), (V, "w3"), (V, "w5"), (V, "w7"), (A, "g3"), (A, "g7"), (V, "p7")]
        assert len(unit_last) == UNITS_LAYER
        bv_order = [f"ada{j}" for j in range(12)] + [f"kc{i}" for i in range(2)] + [f"kx{i}" for i in range(2)]
        ba_order = ["norm0", "cnorm", "xnorm"] + [f"vc{t}" for t in range(2)] + [f"vx{t}" for t in range(ST)]
        ba_order += ["skc0", "skc1", "skx0", "skx1"]
        bv_order += [f"q{i}" for i in range(QH)]
        ba_order += [f"cb{i}" for i in range(4)] + [f"sq{i}" for i in range(QH)]
        ba_order += [f"cc{i}" for i in range(4)]
        bv_order += [f"cx{i}" for i in range(4)]
        BV = Groups(nc, ctx, "bv", [0, 1, 2, 3], bv_order)
        BA = Groups(nc, ctx, "ba", [4, 5, 6, 7], ba_order)
        CV = Groups(nc, ctx, "cv", [0, 1, 2, 3, 4, 5], [f"w{i}" for i in range(DK)] + ["logits", "pos"])
        CA = Groups(nc, ctx, "ca", [6, 7], ["norm2"] + [f"t{i}" for i in range(8)])
        DV = Groups(nc, ctx, "dv", [0, 1, 2, 3, 4, 5], [f"t{i}" for i in range(8)])

        const_in = sem("const_in")
        x_in = sem("x_in")
        pos_in = sem("pos_in")
        w_in = [sem(f"unit_in{i}") for i in range(RING)]
        sgu_in = sem("sgu_in")
        h_ready = sem("h_ready")
        sq_ready, sq_free = sem("sq_ready"), sem("sq_free")
        std_ready, std_free = sem("std_ready"), sem("std_free")
        y_ready = sem("y_ready")
        pool_turns = sem("pool_turns")
        xl_ready, xl_free = sem("xl_ready"), sem("xl_free")
        xc_ready = sem("xc_ready")
        th_ready = sem("th_ready")
        ri_ready = sem("ri_ready")
        la_ready = sem("la_ready")
        at_ready = sem("at_ready")
        ratio_ready = sem("ratio_ready")
        us_ready = sem("us_ready")
        lru_done = sem("lru_done")
        vn_ready = sem("v_natural_ready")
        qk_ready = sem("qk_ready")
        s_ready = sem("s_ready")
        vs_ready = sem("vs_ready")
        var_ready = sem("var_ready")
        sgu_std = sem("sgu_std")
        vn2_ready = sem("gating_v_ready")
        mix_ready = sem("mix_ready")
        pg_ready = sem("ple_gate_ready")
        prep_v, prep_a = sem("prep_v"), sem("prep_a")

        NSQ, NSTD = 22, 8
        prep_t, prep_n, prep_w, prep_e, prep_l, prep_c, prep_r = (
            prep[:, i, :].rearrange("p (l t) -> p l t", l=L) for i in range(7))

        tail_last = [(BV, f"ada{j}") for j in range(12)] + [
            (BA, f"vx{ST - 1}"), (BV, f"q{QH - 1}"), (BA, "cb3"), (BA, "cc3"), (BV, "cx3"),
            (CV, "w3"), (CV, "w7"), (CV, "logits")]
        f_ready, fm_ready = sem("x_ready"), sem("x_modulated")
        c_in, cm_ready, cmm_ready = sem("ctx_in"), sem("ctx_scaled"), sem("ctx_modulated")
        y2_ready = sem("x_shifted")
        cond_ready = sem("cond_ready")
        sq2_ready, sq2_free, std2_ready, std2_free = (sem(f"{n}2") for n in ("sqr", "sqf", "stdr", "stdf"))
        late_in = sem("late_const_in")
        v_done, qkv_done = sem("v_done"), sem("qkv_done")
        cb_ready, cc_ready = sem("cb_ready"), sem("cc_ready")
        sc_full, max_ready, exp_ready, prob_ready = sem("sc_full"), sem("max_ready"), sem("exp_ready"), sem("prob_ready")
        pt_full, pt_ready, o_full, o_ready = sem("pt_full"), sem("pt_ready"), sem("o_full"), sem("o_ready")
        conv_ready = sem("conv_ready")
        h3_ready, n2_scaled, h2_ready = sem("h3_ready"), sem("norm2_scaled"), sem("h2_ready")
        h2n_ready, h2_out = sem("h2n_ready"), sem("h2_out")
        chosen_ready, gate_exp, gate_d = sem("chosen_ready"), sem("gate_exp"), sem("gate_d")
        ent_ready, be_ready, be_out, be_in, np_ready = (sem(n) for n in ("ent_ready", "be_ready", "be_out", "be_in", "np_ready"))
        list_init, list_out, acc_init = sem("list_init"), sem("list_out"), sem("acc_init")

        ATT_SCALE = float(P) ** -0.5
        SH1, SC1, GT1, SH2, SC2, GT2 = range(0, 48, 8)

        def tail_sp(sp):
            for t in range(RING, UNITS_TAIL):
                pool, g = tail_last[t - RING]
                sp.wait_ge(pool.full, pool.done(0, g))
                sp.dma_start(ring[:, t % RING, :], io["units"][L * UNITS_LAYER + t]).then_inc(w_in[t % RING], 16)
            bias_sp(sp)
            for t in range(ST):
                sp.wait_ge(h2n_ready, t + 1)
                sp.dma_start(h2_dram[t * P:(t + 1) * P, :], h2n[:, t, :]).then_inc(h2_out, 16)
            sp.wait_ge(be_ready, 1)
            sp.dma_start(be_dram[:, :], be_i[:]).then_inc(be_out, 16)
            sp.wait_ge(be_out, 16)
            sp.dma_start(be_r[:], be_dram.rearrange("p a -> a p")).then_inc(be_in, 16)
            sp.dma_start(be_bi[:], be_dram.rearrange("p a -> (p a)").partition_broadcast(2 * E_N)).then_inc(be_bc_in, 16)
            experts_sp(sp)

        def tail_pe(pe, mm):
            def need(t):
                pe.wait_ge(w_in[t % RING], 16 * ((L * UNITS_LAYER + t) // RING + 1))
                return ring[:, t % RING, :].rearrange("p (k n) -> p k n", k=DK)

            def slot(t):
                return ring[:, t % RING, :].rearrange("p (k n) -> p k n", k=DK)

            def group(pool, g, pairs, out=None, cols=S):
                pe.wait_ge(pool.free, pool.reusable(0, g))
                out = ps[:, pool.bank(g), 0:cols] if out is None else out
                for j, (a, b) in enumerate(pairs):
                    m = mm(out, a, b, j == 0, j == len(pairs) - 1)
                m.then_inc(pool.full, 1)

            def sums(pool, g, first, n, free_n=True, cols=S):
                pe.wait_ge(pool.free, pool.reusable(0, g))
                for k in range(n):
                    pe.wait_ge(sq2_ready, first + k + 1)
                    m = mm(ps[:, pool.bank(g), 0:cols], ones[:], sq2[:, (first + k) % 2, 0:cols], k == 0, k == n - 1)
                    if k < n - 2:
                        m.then_inc(sq2_free, 1)
                m.then_inc(pool.full, 1)

            pe.wait_ge(V.free, L * V.n + len(V.banks))
            pe.wait_ge(A.free, L * A.n + len(A.banks))
            pe.wait_ge(cond_ready, 1)

            def modulation(j):
                g = f"ada{j}"
                w = need(j)
                pe.wait_ge(BV.free, BV.reusable(0, g))
                for i in range(4):
                    for k in range(DK):
                        m = mm(ps[:, BV.bank(g), 2 * i:2 * i + 2], w[:, k, i * P:(i + 1) * P], cond[:, k, :],
                               k == 0, k == DK - 1)
                m.then_inc(BV.full, 1)

            for j in range(4):
                modulation(j)
            sums(BA, "norm0", 0, DK)
            for j in range(4, 12):
                modulation(j)
            sums(BA, "cnorm", DK, DK, cols=CTX)
            sums(BA, "xnorm", 2 * DK, DK)

            w = need(12)
            pe.wait_ge(cmm_ready, DK)
            for i in range(KVH):
                group(BV, f"kc{i}", [(w[:, k, i * P:(i + 1) * P], hcT[:, k, :]) for k in range(DK)], cols=CTX)
            pe.wait_ge(y2_ready, DK)
            for i in range(KVH):
                group(BV, f"kx{i}", [(w[:, k, i * P:(i + 1) * P], yT[:, k, :]) for k in range(DK)])
            for t in range(2):
                group(BA, f"vc{t}", [(hcT[:, k, t * P:(t + 1) * P], w[:, k, 256:512]) for k in range(DK)], cols=256)
            for t in range(ST):
                group(BA, f"vx{t}", [(yT[:, k, t * P:(t + 1) * P], w[:, k, 256:512]) for k in range(DK)], cols=256)
            for i, g in enumerate(("skc0", "skc1", "skx0", "skx1")):
                sums(BA, g, 3 * DK + i, 1, cols=CTX if i < 2 else S)
            w = need(13)
            for i in range(QH):
                group(BV, f"q{i}", [(w[:, k, i * P:(i + 1) * P], yT[:, k, :]) for k in range(DK)])
            w = need(14)
            for i in range(4):
                group(BA, f"cb{i}", [(w[:, k, i * P:(i + 1) * P], yT[:, k, :]) for k in range(DK)])
            for i in range(QH):
                sums(BA, f"sq{i}", 3 * DK + 4 + i, 1)
            w = need(15)
            for i in range(4):
                group(BA, f"cc{i}", [(w[:, k, i * P:(i + 1) * P], yT[:, k, :]) for k in range(DK)])
            w = need(16)
            for i in range(4):
                group(BV, f"cx{i}", [(w[:, k, i * P:(i + 1) * P], yT[:, k, :]) for k in range(DK)])

            pe.wait_ge(BV.free, BV.n + len(BV.banks))
            pe.wait_ge(BA.free, BA.n + len(BA.banks))
            pe.wait_ge(qkv_done, 1)

            def scores(n):
                h, t, b = n // ST, n % ST, 2 * (n % 2)
                if n >= 2:
                    pe.wait_ge(exp_ready, n - 1)
                q = qTa[:, h, t * P:(t + 1) * P]
                mm(ps[:, b, :], q, kTa[:, h // 2, 0:S], True, True)
                mm(ps[:, b + 1, 0:CTX], q, kTa[:, h // 2, S:KEYS], True, True).then_inc(sc_full, 1)

            def turned(n):
                pe.wait_ge(prob_ready, n + 1)
                if n >= 1:
                    pe.wait_ge(pt_ready, n)
                for j in range(KT):
                    m = pe.transpose(ps[:, 4 + j // 4, (j % 4) * P:(j % 4 + 1) * P],
                                     prob[:, n % 2, j * P:(j + 1) * P], ident[:])
                m.then_inc(pt_full, 1)

            scores(0)
            for n in range(QH * ST):
                if n + 1 < QH * ST:
                    scores(n + 1)
                turned(n)
                if n % ST == ST - 1:
                    h = n // ST
                    pe.wait_ge(pt_ready, n + 1)
                    if h >= 1:
                        pe.wait_ge(o_ready, h)
                    for j in range(KT):
                        m = mm(ps[:, 6, :], vall[:, j, (h // 2) * P:(h // 2 + 1) * P], eT[:, j, :], j == 0, j == KT - 1)
                    m.then_inc(o_full, 1)
            pe.wait_ge(o_ready, QH)
            pe.wait_ge(conv_ready, 4)
            for m_ in range(DK):
                w = need(17 + m_ // 4) if m_ % 4 == 0 else slot(17 + m_ // 4)
                group(CV, f"w{m_}", [(w[:, k, (m_ % 4) * P:(m_ % 4 + 1) * P], mix[:, 8 + k, :]) for k in range(DK)])
            sums(CA, "norm2", 3 * DK + 8, DK)

            w = need(19)
            g = "logits"
            pe.wait_ge(CV.free, CV.reusable(0, g))
            pe.wait_ge(h2_ready, DK)
            for t in range(ST):
                for k in range(DK):
                    m = mm(ps[:, CV.bank(g), t * E_N:(t + 1) * E_N], yT[:, k, t * P:(t + 1) * P], w[:, k, 0:E_N],
                           k == 0, k == DK - 1)
            m.then_inc(CV.full, 1)
            for i in range(8):
                g, t = f"t{i}", i // 2
                pe.wait_ge(CA.free, CA.reusable(0, g))
                for j in range(4):
                    m = pe.transpose(ps[:, CA.bank(g), j * P:(j + 1) * P],
                                     yT[:, 4 * (i % 2) + j, t * P:(t + 1) * P], ident[:])
                m.then_inc(CA.full, 1)
            g = "pos"
            pe.wait_ge(chosen_ready, 1)
            pe.wait_ge(CV.free, CV.reusable(0, g))
            for t in range(ST + 1):
                for t2 in range(min(t + 1, ST)):
                    lhs = before[:] if t2 == t else ones[:]
                    m = mm(ps[:, CV.bank(g), t * E_N:(t + 1) * E_N], lhs, chosen[:, t2, :], t2 == 0, t2 == min(t, ST - 1))
            m.then_inc(CV.full, 1)
            experts_pe(pe, mm)

        def tail_act(act, squares, root):
            sk = dict(rd=sq2_ready, fr=sq2_free)

            def copy(out, pool, g, cols=S):
                act.wait_ge(pool.full, pool.done(0, g))
                nc.scalar.activation(out, ps[:, pool.bank(g), 0:cols], ACT.Copy).then_inc(pool.free, 1)

            def root2(pool, g, i, width, cols=S):
                root(pool, g, 0, i, width, std2, cols=cols, ready=std2_ready, free=std2_free)
                act.drain().then_inc(pool.free, 1)

            squares(0, DK, lambda k: hT[:, k, :], h_ready, lambda k: L * 2 * DK + k + 1, sq2, free_at=0, **sk)
            root2(BA, "norm0", 0, D)
            act.wait_ge(c_in, 16)
            squares(DK, DK, lambda k: ctxT[:, k, :], c_in, lambda k: 16, sq2, cols=CTX, free_at=DK - 2, **sk)
            root2(BA, "cnorm", 1, D, cols=CTX)
            squares(2 * DK, DK, lambda k: hT[:, k, :], f_ready, lambda k: k + 1, sq2, free_at=2 * (DK - 2), **sk)
            root2(BA, "xnorm", 2, D)

            def shift(tile, k, row, who, ready, at, out):
                act.wait_ge(ready, at)
                nc.scalar.activation(tile, tile, ACT.Identity, bias=ada[:, row + k, who:who + 1]).then_inc(out, 1)

            for k in range(DK):
                shift(hcT[:, k, :], k, SH1, 1, cm_ready, k + 1, cmm_ready)
            for k in range(DK):
                shift(yT[:, k, :], k, SH1, 0, fm_ready, k + 1, y2_ready)

            def head_square(i, pool, g, cols=S):
                squares(3 * DK + i, 1, lambda k: ps[:, pool.bank(g), 0:cols], pool.full, lambda k: pool.done(0, g),
                        sq2, cols=cols, **sk)

            head_square(0, BV, "kc0", CTX)
            head_square(1, BV, "kc1", CTX)
            for t in range(2):
                copy(vall[:, ST + t, :], BA, f"vc{t}", 256)
            for t in range(ST):
                copy(vall[:, t, :], BA, f"vx{t}", 256)
            root2(BA, "skc0", 3, P, cols=CTX)
            head_square(2, BV, "kx0")
            root2(BA, "skc1", 4, P, cols=CTX)
            head_square(3, BV, "kx1")
            root2(BA, "skx0", 5, P)
            root2(BA, "skx1", 6, P)
            head_square(4, BV, "q0")
            head_square(5, BV, "q1")
            for i in range(4):
                copy(mix[:, 12 + i, :], BA, f"cb{i}")
            act.drain().then_inc(cb_ready, 1)
            for i in range(QH):
                root2(BA, f"sq{i}", 7 + i, P)
                if i < 2:
                    head_square(6 + i, BV, f"q{2 + i}")
            for i in range(4):
                copy(ccb[:, i, :], BA, f"cc{i}")
            act.drain().then_inc(cc_ready, 1)

            for n in range(QH * ST):
                act.wait_ge(max_ready, n + 1)
                if n >= 2:
                    act.wait_ge(pt_full, n - 1)
                b = 2 * (n % 2)
                s_ = ps[:, b:b + 2, :].rearrange("p a b -> p (a b)")[:, 0:KEYS]
                nc.scalar.activation(prob[:, n % 2, :], s_, ACT.Exp, bias=small[:, 16 + n % 2:17 + n % 2],
                                     scale=ATT_SCALE, accum_out=small[:, 18 + n % 2:19 + n % 2]).then_inc(exp_ready, 1)
                if n >= 1:
                    turned_copy(act, n - 1)
            turned_copy(act, QH * ST - 1)

            squares(3 * DK + 8, DK, lambda k: hT[:, k, :], h3_ready, lambda k: k + 1, sq2, free_at=3 * (DK - 2), **sk)
            root2(CA, "norm2", 11, D)
            for k in range(DK):
                shift(yT[:, k, :], k, SH2, 0, n2_scaled, k + 1, h2_ready)
            for i in range(8):
                t = i // 2
                copy(h2n[:, t, (i % 2) * S:(i % 2 + 1) * S], CA, f"t{i}")
                if i % 2:
                    act.drain().then_inc(h2n_ready, 1)
            bias_act(act)
            act.wait_ge(gate_d, 1)
            nc.scalar.activation(gates, gates, ACT.Exp).then_inc(gate_exp, 1)
            experts_act(act)

        def turned_copy(act, n):
            act.wait_ge(pt_full, n + 1)
            t = n % ST
            src = ps[:, 4:6, :].rearrange("p a b -> p (a b)")[:, 0:KEYS].rearrange("p (j q) -> p j q", j=KT)
            nc.scalar.activation(eT[:, :, t * P:(t + 1) * P], src, ACT.Copy).then_inc(pt_ready, 1)

        def tail_dve(dve, inverse, rope):
            def full(pool, g, cols=S):
                dve.wait_ge(pool.full, pool.done(0, g))
                return ps[:, pool.bank(g), 0:cols]

            dve.sem_inc(BV.free, len(BV.banks))
            dve.sem_inc(BA.free, len(BA.banks))
            dve.sem_inc(std2_free, 2)

            def modulation(j):
                x = full(BV, f"ada{j}")[:, 0:8].rearrange("p (m c) -> p m c", m=4)
                b = q_(par2, "b_ada", 4 * j, 4).unsqueeze(2).to_broadcast([P, 4, 2])
                nc.vector.tensor_tensor(ada[:, 4 * j:4 * j + 4, :], x, b, ALU.add).then_inc(BV.free, 1)

            for j in range(4):
                modulation(j)
            r = inverse(0, std2_ready, 1, std2)
            for k in range(DK):
                nc.vector.scalar_tensor_tensor(hT[:, k, :], hT[:, k, :], q_(par2, "final_norm", k), r, ALU.mult,
                                               ALU.mult).then_inc(f_ready, 1)
            dve.drain().then_inc(std2_free, 1)
            for j in range(4, 12):
                modulation(j)
            dve.drain()
            for i, (sc, who, gn) in enumerate(((SC1, 0, "g_norm1"), (SC1, 1, "g_norm1"), (SC2, 0, "g_norm2"))):
                nc.vector.scalar_tensor_tensor(coef[:, i, :], ada[:, sc:sc + DK, who], 1.0, q_(par2, gn, 0, DK),
                                               ALU.add, ALU.mult)
            dve.drain()
            r = inverse(1, std2_ready, 2, std2, cols=CTX)
            for k in range(DK):
                nc.vector.scalar_tensor_tensor(hcT[:, k, :], ctxT[:, k, :], coef[:, 1, k:k + 1], r, ALU.mult,
                                               ALU.mult).then_inc(cm_ready, 1)
            dve.drain().then_inc(std2_free, 1)
            r = inverse(2, std2_ready, 3, std2)
            for k in range(DK):
                nc.vector.scalar_tensor_tensor(yT[:, k, :], hT[:, k, :], coef[:, 0, k:k + 1], r, ALU.mult,
                                               ALU.mult).then_inc(fm_ready, 1)
            dve.drain().then_inc(std2_free, 1)

            quads = [((a, a + 32), (b, b + 32)) for a, b in ((0, 32), (32, 0), (64, 96), (96, 64))]

            def head(i, g, gain, out, cols, rotate):
                x = full(BV, g, cols)
                r = inverse(3 + i, std2_ready, 3 + i + 1, std2, cols=cols)
                dst = tmp2[:, 0, :] if rotate else out
                nc.vector.scalar_tensor_tensor(dst, x, q_(par2, gain), r, ALU.mult, ALU.mult)
                dve.drain().then_inc(BV.free, 1)
                dve.sem_inc(std2_free, 1)
                if rotate:
                    rope(tmp2[:, 0, :], out, tmp2[:, 1, :], acos, asin, quads)
                    dve.drain()

            dve.wait_ge(late_in, 32)
            head(0, "kc0", "g_k", kTa[:, 0, S:KEYS], CTX, False)
            head(1, "kc1", "g_k", kTa[:, 1, S:KEYS], CTX, False)
            head(2, "kx0", "g_k", kTa[:, 0, 0:S], S, True)
            head(3, "kx1", "g_k", kTa[:, 1, 0:S], S, True)
            for i in range(QH):
                head(4 + i, f"q{i}", "g_q", qTa[:, i, :], S, True)
            dve.drain().then_inc(qkv_done, 1)

            nc.vector.memset(ubuf, 0.0)
            dve.wait_ge(cb_ready, 1)
            dve.wait_ge(cc_ready, 1)
            for i in range(4):
                x = full(BV, f"cx{i}")
                dve.drain()
                nc.vector.tensor_tensor(ubuf[:, 1:1 + S], x, ccb[:, i, :], ALU.mult)
                dve.drain().then_inc(BV.free, 1)
                t = tmp2[:, i % 2, :]
                nc.vector.tensor_scalar(t, ubuf[:, 0:S], q_(par2, "w_conv", i), None, ALU.mult)
                for w in (1, 2):
                    dve.drain()
                    nc.vector.scalar_tensor_tensor(t, ubuf[:, w:w + S], q_(par2, "w_conv", 4 * w + i), t, ALU.mult,
                                                   ALU.add)
                dve.drain()
                nc.vector.tensor_tensor(mix[:, 12 + i, :], mix[:, 12 + i, :], t, ALU.mult).then_inc(conv_ready, 1)

            def rows_max(n):
                b = 2 * (n % 2)
                dve.wait_ge(sc_full, n + 1)
                s_ = ps[:, b:b + 2, :].rearrange("p a b -> p (a b)")[:, 0:KEYS]
                nc.vector.reduce_max(small[:, 20 + n % 2:21 + n % 2], s_, AX.X)
                dve.drain()
                nc.vector.tensor_scalar(small[:, 16 + n % 2:17 + n % 2], small[:, 20 + n % 2:21 + n % 2], -ATT_SCALE, None,
                                        ALU.mult).then_inc(max_ready, 1)

            rows_max(0)
            for n in range(QH * ST):
                if n + 1 < QH * ST:
                    if n >= 1:
                        dve.wait_ge(exp_ready, n)
                    rows_max(n + 1)
                dve.wait_ge(exp_ready, n + 1)
                nc.vector.reciprocal(small[:, 22:23], small[:, 18 + n % 2:19 + n % 2])
                dve.drain()
                nc.vector.tensor_scalar(prob[:, n % 2, :], prob[:, n % 2, :], small[:, 22:23], None,
                                        ALU.mult).then_inc(prob_ready, 1)
                dve.drain()
                if n % ST == ST - 1:
                    h = n // ST
                    dve.wait_ge(o_full, h + 1)
                    nc.vector.tensor_copy(mix[:, 8 + h, :], ps[:, 6, :]).then_inc(o_ready, 1)

            dve.sem_inc(CV.free, len(CV.banks))
            dve.sem_inc(CA.free, len(CA.banks))
            for m in range(DK):
                nc.vector.scalar_tensor_tensor(hT[:, m, :], full(CV, f"w{m}"), ada[:, GT1 + m, 0:1], hT[:, m, :],
                                               ALU.mult, ALU.add).then_inc(h3_ready, 1)
                dve.drain().then_inc(CV.free, 1)
            r = inverse(11, std2_ready, 12, std2)
            for k in range(DK):
                nc.vector.scalar_tensor_tensor(yT[:, k, :], hT[:, k, :], coef[:, 2, k:k + 1], r, ALU.mult,
                                               ALU.mult).then_inc(n2_scaled, 1)
            dve.drain()

            x = full(CV, "logits")[:, 0:ST * E_N].rearrange("p (t e) -> p t e", t=ST)
            nc.vector.tensor_tensor(logits, x, brt[:].unsqueeze(1).to_broadcast([P, ST, E_N]), ALU.add)
            dve.drain().then_inc(CV.free, 1)
            for t in range(ST):
                nc.vector.max(mx8[:, t, :], logits[:, t, :])
            dve.drain()
            for t in range(ST):
                nc.vector.max_index(ix8[:, t, :].bitcast(U32), mx8[:, t, :], logits[:, t, :])
                nc.vector.tensor_scalar(gates[:, t, :], mx8[:, t, 0:TOP], mx8[:, t, 0:1], None, ALU.subtract)
            dve.drain().then_inc(gate_d, 1)
            nc.vector.tensor_copy(ixf, ix8.bitcast(U32))
            dve.drain()
            for t in range(ST):
                for k in range(TOP):
                    nc.vector.tensor_scalar(hot[:, t * TOP + k, :], cst[:, 0:E_N], ixf[:, t, k:k + 1], None, ALU.is_equal)
            dve.drain()
            hk = hot.rearrange("p (t k) e -> p t k e", k=TOP)
            nc.vector.tensor_tensor(chosen, hk[:, :, 0, :], hk[:, :, 1, :], ALU.add)
            for k in (2, 3):
                dve.drain()
                nc.vector.tensor_tensor(chosen, chosen, hk[:, :, k, :], ALU.add)
            dve.drain().then_inc(chosen_ready, 1)
            dve.wait_ge(gate_exp, 1)
            nc.vector.reduce_sum(gsum, gates, AX.X)
            dve.drain()
            nc.vector.reciprocal(gsum, gsum)
            dve.drain()
            nc.vector.tensor_tensor(gates, gates, gsum.unsqueeze(2).to_broadcast([P, ST, TOP]), ALU.mult)
            dve.drain()
            x = full(CV, "pos")
            nc.vector.tensor_copy(posn, x[:, 0:ST * E_N].rearrange("p (t e) -> p t e", t=ST))
            count = x[:, ST * E_N:(ST + 1) * E_N]
            nc.vector.tensor_scalar(nblk, count, 0.0, None, ALU.is_gt)
            nc.vector.memset(zer, 0.0)
            for t in range(1, ST):
                dve.drain()
                nc.vector.scalar_tensor_tensor(nblk, count, float(t * P), nblk, ALU.is_gt, ALU.add)
            dve.drain().then_inc(CV.free, 1)
            nc.vector.tensor_tensor_scan(pend, nblk, zer, 0.0, ALU.add, ALU.add)
            dve.drain()
            nc.vector.tensor_tensor(pbase, pend, nblk, ALU.subtract)
            nc.vector.tensor_scalar(ended, pend, q_(par2, "part"), None, ALU.is_le)
            nc.vector.tensor_scalar(hot2n, cst[:, E_N:E_N + 24], pend[:, E_N - 1:E_N], None, ALU.is_lt)
            dve.drain()
            nc.vector.reduce_sum(beI, ended, AX.X)
            nc.vector.reduce_sum(npI, hot2n, AX.X)
            nc.vector.tensor_scalar(pbase, pbase, float(P), None, ALU.mult)
            dve.drain()
            nc.vector.tensor_scalar(be_i[:], beI, float(E_N - 1), None, ALU.min).then_inc(be_ready, 1)
            nc.vector.tensor_copy(np_i[:], npI[0:1, :]).then_inc(np_ready, 1)
            nc.vector.tensor_tensor(posn, posn, pbase.unsqueeze(1).to_broadcast([P, ST, E_N]), ALU.add)
            dve.drain()
            h2k = hot2.rearrange("p (t k) e -> p t k e", k=TOP)
            for k in range(TOP):
                nc.vector.tensor_tensor(h2k[:, :, k, :], hk[:, :, k, :], posn, ALU.mult)
            dve.drain()
            nc.vector.reduce_sum(slotf, hot2, AX.X)
            nc.vector.tensor_copy(ent_i[:, :, 0], cst_i[:])
            nc.vector.tensor_copy(ent_i[:, :, 1].bitcast(F32), gates.rearrange("p t k -> p (t k)"))
            dve.drain()
            nc.vector.tensor_copy(slot_u[:], slotf)
            dve.drain().then_inc(ent_ready, 1)
            experts_dve(dve)

        raw_in = [sem(f"half_in{j}") for j in range(RAW)]
        bias_in, bias_high, bias_split, be_bc_in = (sem(n) for n in ("bias_in", "bias_high", "bias_split", "be_bc_in"))
        lst_in, lst_ready, xg_in = sem("slots_in"), sem("slots_ready"), sem("rows_in")
        high = sem("high_ready")
        low_v, low_p = sem("low_ready_v"), sem("low_ready_p")
        used = sem("half_used")
        t_full, t_high, t_out = sem("t_full"), sem("t_high"), sem("t_out")
        sel_ready = sem("sel_ready")
        glu_ready, th2_ready, act_ready = sem("glu_ready"), sem("tanh_ready"), sem("act_ready")
        ye_ready, scattered, y_free = sem("ye_ready"), sem("scattered"), sem("y_free")
        acc_in, fin_ready, out_done, z_ready = sem("acc_in"), sem("fin_ready"), sem("out_done"), sem("z_ready")
        sq3_ready, std3_ready = sem("sq3_ready"), sem("std3_ready")

        def block_pairs(eng):
            eng.wait_ge(np_ready, 1)
            return eng.value_load(np_i[0:1, 0:1], min_val=1, max_val=BLOCKS // 2)

        def low_done(b, h):
            s_, own = (low_p, POOL_LOW) if h in POOL_LOW else (low_v, DVE_LOW)
            return s_, len(own) * (b + 1) + own.index(h) + 1

        def raw_landed(b, h):
            return raw_in[h % RAW], 16 * (2 * b + h // RAW + 1)

        def bias_sp(sp):
            sp.wait_ge(CV.full, CV.done(0, "w7"))
            for i in range(2):
                sp.dma_start(b_raw[i * E_N:(i + 1) * E_N, :], io["b_moe"]).then_inc(bias_in, 16)

        def bias_act(act):
            act.wait_ge(bias_in, 32)
            nc.scalar.activation(b_split[:], b_raw, ACT.Copy).then_inc(bias_high, 1)

        def bias_pool(pool):
            pool.wait_ge(bias_high, 1)
            nc.gpsimd.tensor_tensor(b_split[E_N:2 * E_N, :], b_raw[E_N:2 * E_N, :],
                                    b_split[E_N:2 * E_N, :].bitcast(F32), ALU.subtract).then_inc(bias_split, 1)
            pool.drain()
            nc.gpsimd.memset(xgy[:], 0.0)
            pool.drain()

        def experts_sp(sp):
            sp.wait_ge(be_in, 16)
            n = block_pairs(sp)
            sp.wait_ge(CV.full, CV.n)

            def load(b, hs):
                e = sp.value_load(be_r[0:1, bass.ds(b, 1)], min_val=0, max_val=E_N - 1)
                for h in hs:
                    j, q = ORDER[h]
                    before_, hb = (b - 1, h + RAW) if h < RAW else (b, h - RAW)
                    sp.wait_ge(*low_done(before_, hb))
                    sp.dma_start(raw[:, h % RAW, :].unsqueeze(1),
                                 io["w_moe"][bass.ds(6 * e + j, 1), :, q * HALF:(q + 1) * HALF]
                                 .rearrange("a p n -> p a n")).then_inc(raw_in[h % RAW], 16)

            with sp.Fori(0, n) as i:
                for s in range(2):
                    load(2 * i + s, range(HALVES))
            load(2 * n, range(SPLIT))
            final_sp(sp, n)

        def experts_pe(pe, mm):
            n = block_pairs(pe)
            pe.wait_ge(CA.free, CA.n + len(CA.banks))
            pe.wait_ge(CV.free, CV.n + len(CV.banks))

            def turn(src, bank):
                for j in range(4):
                    m = pe.transpose(ps[:, bank, j * P:(j + 1) * P], src[:, j * P:(j + 1) * P], ident[:])
                m.then_inc(t_full, 1)

            def half(b, s, h):
                j, q = ORDER[h]
                rows = xgT[:, s] if j < 4 else hTe[:]
                w = wsp[:, h % SPLIT]
                if q == 0:
                    mm(ps[:, j, :], sel[:, s, :], b_split[:, j * S:(j + 1) * S], True, False)
                pe.wait_ge(high, HALVES * b + h + 1)
                for k in range(4):
                    at_ = (4 * q + k) * P
                    for part in range(2):
                        mm(ps[:, j, :], rows[:, part, at_:at_ + P], w[:, 0, k * S:(k + 1) * S], False, False)
                pe.wait_ge(*low_done(b, h))
                for k in range(4):
                    at_ = (4 * q + k) * P
                    m = mm(ps[:, j, :], rows[:, 0, at_:at_ + P], w[:, 1, k * S:(k + 1) * S], False,
                           q == 1 and k == 3)
                m.then_inc(used, 1)

            pe.wait_ge(bias_split, 1)
            pe.wait_ge(xg_in, 16)
            turn(xg[:, 0, 0:S], 6)
            turn(xg[:, 0, S:D], 7)
            with pe.Fori(0, n) as i:
                for s in range(2):
                    b = 2 * i + s
                    pe.wait_ge(sel_ready, b + 1)
                    pe.wait_ge(t_out, 4 * b + 1)
                    half(b, s, 0)
                    pe.wait_ge(t_out, 4 * b + 2)
                    for h in range(1, 6):
                        half(b, s, h)
                    pe.wait_ge(act_ready, 2 * b + 1)
                    turn(h_sb[:, 0:S], 6)
                    half(b, s, 6)
                    half(b, s, 7)
                    pe.wait_ge(ye_ready, 2 * b + 2)
                    pe.wait_ge(t_out, 4 * b + 3)
                    half(b, s, 8)
                    half(b, s, 9)
                    pe.wait_ge(act_ready, 2 * b + 2)
                    turn(h_sb[:, S:D], 7)
                    pe.wait_ge(xg_in, 16 * b + 32)
                    turn(xg[:, 1 - s, 0:S], 6)
                    pe.wait_ge(t_out, 4 * b + 4)
                    half(b, s, 10)
                    half(b, s, 11)
                    turn(xg[:, 1 - s, S:D], 7)
            final_pe(pe, mm)

        def experts_act(act):
            n = block_pairs(act)

            def high_part(b, h):
                act.wait_ge(*raw_landed(b, h))
                nc.scalar.activation(wsp[:, h % SPLIT, 0], raw[:, h % RAW, :], ACT.Copy).then_inc(high, 1)

            def turned_high(dst, bank, at, scale=1.0):
                act.wait_ge(t_full, at)
                nc.scalar.activation(dst, ps[:, bank, :], ACT.Copy, scale=scale).then_inc(t_high, 1)

            act.wait_ge(CA.full, CA.n)
            act.wait_ge(CV.full, CV.n)
            for h in range(SPLIT):
                high_part(0, h)
            turned_high(xgT[:, 0, 0, 0:S], 6, 1)
            turned_high(xgT[:, 0, 0, S:D], 7, 2)
            with act.Fori(0, n) as i:
                for s in range(2):
                    b = 2 * i + s
                    for h in range(HALVES):
                        act.wait_ge(used, HALVES * b + h + 1)
                        if h in (2, 6):
                            act.wait_ge(glu_ready, 2 * b + 1 + h // 6)
                            nc.scalar.activation(thb, glu, ACT.Tanh, scale=ALPHA / 2).then_inc(th2_ready, 1)
                        if h == 5:
                            turned_high(hTe[:, 0, 0:S], 6, 4 * b + 3, 0.5)
                        if h == 9:
                            turned_high(hTe[:, 0, S:D], 7, 4 * b + 4, 0.5)
                            turned_high(xgT[:, 1 - s, 0, 0:S], 6, 4 * b + 5)
                        if h == 11:
                            turned_high(xgT[:, 1 - s, 0, S:D], 7, 4 * b + 6)
                        high_part(b + (h + SPLIT) // HALVES, (h + SPLIT) % HALVES)
            final_act(act)

        def low_part(eng, e, b, h):
            eng.wait_ge(high, HALVES * b + h + 1)
            e.tensor_tensor(wsp[:, h % SPLIT, 1], raw[:, h % RAW, :], wsp[:, h % SPLIT, 0].bitcast(F32),
                            ALU.subtract).then_inc(low_p if h in POOL_LOW else low_v, 1)

        def experts_dve(dve):
            n = block_pairs(dve)
            dve.sem_inc(ye_ready, 2)
            dve.sem_inc(y_free, 1)
            dve.sem_inc(low_v, len(DVE_LOW))

            def turned_low(dst, high_, bank, at, scale=1.0):
                dve.wait_ge(t_high, at)
                nc.vector.scalar_tensor_tensor(dst, ps[:, bank, :], scale, high_.bitcast(F32), ALU.mult,
                                               ALU.subtract).then_inc(t_out, 1)

            def select(b, s):
                nc.vector.tensor_scalar(sel[:, s, :], be_bc[:, bass.ds(b, 1)].to_broadcast([2 * E_N, P]),
                                        q_(par2, "part32")[0:2 * E_N], None, ALU.is_equal).then_inc(sel_ready, 1)

            for h in range(SPLIT):
                if h in DVE_LOW:
                    low_part(dve, nc.vector, 0, h)
            dve.wait_ge(be_bc_in, 16)
            nc.vector.tensor_copy(be_bc[:], be_bi[:])
            dve.drain()
            select(0, 0)
            dve.wait_ge(lst_ready, 1)
            turned_low(xgT[:, 0, 1, 0:S], xgT[:, 0, 0, 0:S], 6, 1)
            turned_low(xgT[:, 0, 1, S:D], xgT[:, 0, 0, S:D], 7, 2)
            with dve.Fori(0, n) as i:
                for s in range(2):
                    b = 2 * i + s
                    for h in range(HALVES):
                        if h in (1, 5):
                            dve.wait_ge(used, HALVES * b + h + 1)
                            nc.vector.tensor_scalar(glu, ps[:, h // 2, :], LIMIT, None, ALU.min).then_inc(glu_ready, 1)
                        if h == 5:
                            turned_low(hTe[:, 1, 0:S], hTe[:, 0, 0:S], 6, 4 * b + 3, 0.5)
                        if h in (3, 7):
                            at_ = h // 4
                            dve.wait_ge(used, HALVES * b + h + 1)
                            nc.vector.tensor_scalar(lin, ps[:, h // 2, :], LIMIT, -LIMIT, ALU.min, ALU.max)
                            dve.wait_ge(th2_ready, 2 * b + at_ + 1)
                            nc.vector.scalar_tensor_tensor(glu, thb, 1.0, glu, ALU.add, ALU.mult)
                            dve.drain()
                            nc.vector.scalar_tensor_tensor(h_sb[:, at_ * S:(at_ + 1) * S], lin, 1.0, glu, ALU.add,
                                                           ALU.mult).then_inc(act_ready, 1)
                            dve.drain()
                        if h == 9:
                            turned_low(hTe[:, 1, S:D], hTe[:, 0, S:D], 7, 4 * b + 4, 0.5)
                            turned_low(xgT[:, 1 - s, 1, 0:S], xgT[:, 1 - s, 0, 0:S], 6, 4 * b + 5)
                            select(b + 1, 1 - s)
                        if h == 11:
                            turned_low(xgT[:, 1 - s, 1, S:D], xgT[:, 1 - s, 0, S:D], 7, 4 * b + 6)
                        if h in (10, 11):
                            dve.wait_ge(used, HALVES * b + h + 1)
                            if h == 10:
                                dve.wait_ge(y_free, b + 1)
                            at_ = h - 10
                            nc.vector.tensor_scalar(y_sb[:, s, at_ * S:(at_ + 1) * S], ps[:, 4 + at_, :],
                                                    lst[:, s, 1:2].bitcast(F32), None, ALU.mult).then_inc(ye_ready, 1)
                        ahead = (h + SPLIT) % HALVES
                        if ahead in DVE_LOW:
                            low_part(dve, nc.vector, b + (h + SPLIT) // HALVES, ahead)
            final_dve(dve)

        def experts_pool(pool):
            n = block_pairs(pool)
            pool.sem_inc(low_p, len(POOL_LOW))
            low_part(pool, nc.gpsimd, 0, 2)
            pool.wait_ge(list_out, 16 * ST * TOP)
            pool.wait_ge(h2_out, 16 * ST)

            pool.dma_start(lst_all[:], list_dram.rearrange("(b p) c -> p b c", p=P)).then_inc(lst_in, 16)

            def fetch(b, s):
                nc.gpsimd.tensor_copy(rows_i[:, s:s + 1], lst_all[:, bass.ds(b, 1), 0])
                pool.drain()
                nc.gpsimd.indirect_dma_start(out=xg[:, s, :], out_offset=None, in_=h2_dram[:, :],
                                             in_offset=bass.IndirectOffsetOnAxis(ap=rows_i[:, s:s + 1].bitcast(U32), axis=0),
                                             bounds_check=S - 1, oob_is_err=False).then_inc(xg_in, 16)

            def take_list(b, s):
                nc.gpsimd.tensor_copy(lst[:, s, 0:1], lst_all[:, bass.ds(b, 1), 0])
                nc.gpsimd.tensor_copy(lst[:, s, 1:2].bitcast(F32), lst_all[:, bass.ds(b, 1), 1].bitcast(F32))
                pool.drain()

            def add_rows(s, at):
                pool.wait_ge(ye_ready, at)
                pool.sem_inc(pool_turns, 1)
                nc.gpsimd.indirect_dma_start(out=acc_dram[:, :],
                                             out_offset=bass.IndirectOffsetOnAxis(ap=lst[:, s, 0:1].bitcast(U32), axis=0),
                                             in_=y_sb[:, s, :], in_offset=None, compute_op=ALU.add).then_inc(scattered, 16)

            pool.wait_ge(lst_in, 16)
            pool.sem_inc(pool_turns, 1)
            fetch(0, 0)
            take_list(0, 0)
            take_list(BLOCKS, 1)
            pool.sem_inc(lst_ready, 1)
            with pool.Fori(0, n) as i:
                for s in range(2):
                    b = 2 * i + s
                    pool.wait_ge(t_out, 4 * b + 2)
                    pool.sem_inc(pool_turns, 1)
                    fetch(b + 1, 1 - s)
                    add_rows(1 - s, 2 * b + 2)
                    low_part(pool, nc.gpsimd, b, 6)
                    pool.wait_ge(scattered, 16 * b + 16)
                    pool.sem_inc(pool_turns, 1)
                    take_list(b + 1, 1 - s)
                    pool.sem_inc(y_free, 1)
                    low_part(pool, nc.gpsimd, b, 10)
                    low_part(pool, nc.gpsimd, b + 1, 2)
            add_rows(1, 4 * n + 2)
            pool.wait_ge(scattered, 32 * n + 16)
            pool.wait_ge(xg_in, 32 * n + 16)
            pool.sem_inc(z_ready, 1)

        accn = yT[:].rearrange("p a b -> p (a b)").rearrange("p (t n) -> p t n", t=ST)

        def final_sp(sp, n):
            sp.wait_ge(z_ready, 1)
            sp.wait_ge(low_v, len(DVE_LOW) * (2 * n + 1) + 3)
            sp.wait_ge(low_p, len(POOL_LOW) * (2 * n + 1) + 1)
            for t in range(ST):
                sp.dma_start(accn[:, t, :], acc_dram[t * P:(t + 1) * P, :]).then_inc(acc_in, 16)
            for k in range(DK):
                sp.wait_ge(fin_ready, DK + k + 1)
                sp.dma_start(io["out"][k * P:(k + 1) * P, :], hT[:, k, :]).then_inc(out_done, 16)
            sp.wait_ge(out_done, 16 * DK)

        def final_pe(pe, mm):
            pe.wait_ge(acc_in, 16 * ST)
            pe.wait_ge(z_ready, 1)
            for k in range(DK):
                g = f"t{k}"
                pe.wait_ge(DV.free, DV.reusable(0, g))
                for t in range(ST):
                    m = pe.transpose(ps[:, DV.bank(g), t * P:(t + 1) * P], accn[:, t, k * P:(k + 1) * P], ident[:])
                m.then_inc(DV.full, 1)
            for k in range(DK):
                pe.wait_ge(sq3_ready, k + 1)
                m = mm(ps[:, 6, :], ones[:], xg_flat[:, k * S:(k + 1) * S], k == 0, k == DK - 1)
            m.then_inc(sq3_ready, 1)

        def final_act(act):
            act.drain()
            for k in range(DK):
                act.wait_ge(fin_ready, k + 1)
                nc.scalar.activation(xg_flat[:, k * S:(k + 1) * S], hT[:, k, :], ACT.Square).then_inc(sq3_ready, 1)
            act.wait_ge(sq3_ready, DK + 1)
            nc.scalar.activation(glu, ps[:, 6, :], ACT.Sqrt, bias=EPSC, scale=1.0 / D).then_inc(std3_ready, 1)

        def final_dve(dve):
            dve.sem_inc(DV.free, len(DV.banks))
            for k in range(DK):
                dve.wait_ge(DV.full, DV.done(0, f"t{k}"))
                nc.vector.scalar_tensor_tensor(hT[:, k, :], ps[:, DV.bank(f"t{k}"), :], ada[:, GT2 + k, 0:1],
                                               hT[:, k, :], ALU.mult, ALU.add).then_inc(fin_ready, 1)
                dve.drain().then_inc(DV.free, 1)
            dve.wait_ge(std3_ready, 1)
            nc.vector.reciprocal(glu, glu)
            dve.drain()
            for k in range(DK):
                nc.vector.scalar_tensor_tensor(hT[:, k, :], hT[:, k, :], q_(par2, "g_final", k), glu, ALU.mult,
                                               ALU.mult).then_inc(fin_ready, 1)

        xg_flat = xgy[:].rearrange("p a b -> p (a b)")

        block = ctx.enter_context(nc.Block())

        @block.sync
        def _(sp):
            for kt in range(DK):
                sp.dma_start(hT[:, kt, :], io["xT"][kt * P:(kt + 1) * P, :]).then_inc(x_in, 16)
            for s in range(RING):
                sp.dma_start(ring[:, s, :], io["units"][s]).then_inc(w_in[s], 16)
            with sp.Fori(0, L) as layer:
                for u, (pool, g) in enumerate(unit_last):
                    sp.wait_ge(pool.full, pool.done(layer, g))
                    n = layer * UNITS_LAYER + (u + RING)
                    sp.dma_start(ring[:, u % RING, :].unsqueeze(1),
                                 io["units"][bass.ds(n, 1)].rearrange("a p n -> p a n")).then_inc(w_in[u % RING], 16)

            tail_sp(sp)

        def unit_landed(layer, u):
            return w_in[u % RING], 16 * (layer * (UNITS_LAYER // RING) + u // RING + 1)

        @block.tensor
        def _(pe):
            pe.wait_ge(const_in, 16 * N_CONST)

            def mm(out, lhsT, rhs, start, stop):
                return pe.matmul(out, lhsT, rhs, start=start, stop=stop)

            def norm_sums(pool, g, layer, first, n, ready, free, buf, cols=S, per=NSQ):
                pe.wait_ge(pool.free, pool.reusable(layer, g))
                for k in range(n):
                    pe.wait_ge(ready, layer * per + first + k + 1)
                    m = mm(ps[:, pool.bank(g), 0:cols], ones[:], buf[:, (first + k) % 2, 0:cols], k == 0, k == n - 1)
                    if k < n - 2:
                        m.then_inc(free, 1)
                m.then_inc(pool.full, 1)

            def project(pool, g, layer, w, rhs, n=DK):
                pe.wait_ge(pool.free, pool.reusable(layer, g))
                for k in range(n):
                    m = mm(ps[:, pool.bank(g), :], w(k), rhs(k), k == 0, k == n - 1)
                m.then_inc(pool.full, 1)

            def natural(pool, g, layer, t, w, cols):
                pe.wait_ge(pool.free, pool.reusable(layer, g))
                for k in range(DK):
                    m = mm(ps[:, pool.bank(g), 0:cols], yT[:, k, t * P:(t + 1) * P], w(k), k == 0, k == DK - 1)
                m.then_inc(pool.full, 1)

            with pe.Fori(0, L) as layer:
                def need(u):
                    s, value = unit_landed(layer, u)
                    pe.wait_ge(s, value)
                    return ring[:, u % RING, :]

                def columns(u, j):
                    w = need(u) if j == 0 else ring[:, u % RING, :]
                    w = w.rearrange("p (k n) -> p k n", k=DK)
                    return lambda k: w[:, k, j * P:(j + 1) * P]

                y = lambda k: yT[:, k, :]

                norm_sums(A, "norm1", layer, 0, DK, sq_ready, sq_free, sq)
                pe.wait_ge(y_ready, layer * 2 * DK + DK)
                for u in range(3):
                    for j in range(4):
                        if u < 2:
                            pool, g = (A, f"xl{3 * u + j}") if j < 3 else (V, f"gl{u}")
                        else:
                            pool, g = V, f"gl{2 + j}"
                        project(pool, g, layer, columns(u, j), y)

                wbd = need(3)[:, 0:2 * 2 * 7 * P].rearrange("p (w g n m) -> p w g n m", w=2, g=2, n=7)
                for g in range(2):
                    pe.wait_ge(xc_ready, layer * 6 + 3 * g + 3)
                    for m in range(3):
                        ks = [(n, k) for n, (k, mm_) in enumerate(PAIRS) if mm_ == m]
                        for wi, wn in enumerate(("r", "i")):
                            name = f"{wn}{3 * g + m}"
                            pe.wait_ge(A.free, A.reusable(layer, name))
                            for j, (n, k) in enumerate(ks):
                                x = mm(ps[:, A.bank(name), :], wbd[:, wi, g, n, :], xc[:, 3 * g + k, :],
                                       j == 0, j == len(ks) - 1)
                            x.then_inc(A.full, 1)
                    w = need(4 + g).rearrange("p (k n) -> p k n", k=DK)
                    cols = 512 if g == 0 else 256
                    for t in range(ST):
                        natural(A, f"v{g}.{t}", layer, t, lambda k: w[:, k, 0:cols], cols)
                for j in range(2):
                    w5 = ring[:, 5 % RING, :].rearrange("p (k n) -> p k n", k=DK)
                    project(V, f"gr{j}", layer, lambda k: w5[:, k, (2 + j) * P:(3 + j) * P], y)
                for j in range(4):
                    project(V, f"gr{2 + j}", layer, columns(6, j), y)

                def out_sums(h):
                    norm_sums(A, f"oss{h}", layer, DK + h, 1, sq_ready, sq_free, sq)

                for h in range(HEADS + 1):
                    if h < HEADS:
                        u, j = 7 + h // 2, 2 * (h % 2)
                        project(V, f"q{h}", layer, columns(u, j), y)
                        project(V, f"k{h}", layer, columns(u, j + 1), y)
                    if h >= 2:
                        out_sums(h - 2)
                    if h == 0:
                        pe.wait_ge(vn_ready, layer + 1)
                        continue
                    g = h - 1
                    pe.wait_ge(qk_ready, layer * HEADS + g + 1)
                    for c in range(ST):
                        name = f"s{g}.{c}"
                        pe.wait_ge(V.free, V.reusable(layer, name))
                        mm(ps[:, V.bank(name), 0:S - c * P], qk[:, 2 * (g % 2) + 1, c * P:(c + 1) * P],
                           qk[:, 2 * (g % 2), c * P:S], True, True).then_inc(V.full, 1)
                    pe.wait_ge(V.free, V.reusable(layer, f"o{g}"))
                    at_c = 0
                    for c in range(ST):
                        pe.wait_ge(s_ready, (layer * HEADS + g) * ST + c + 1)
                        n = S - c * P
                        x = mm(ps[:, V.bank(f"o{g}"), c * P:S], vnat[:, c, g * P:(g + 1) * P],
                               dec_s[:, at_c:at_c + n], c == 0, c == ST - 1)
                        at_c += n
                    x.then_inc(V.full, 1)
                out_sums(5)

                w = need(10).rearrange("p (k n) -> p k n", k=DK)
                for t in range(ST):
                    natural(A, f"vs{t}", layer, t, lambda k: w[:, k, :], S)
                for j in range(4):
                    project(V, f"gs{j}", layer, columns(11, j), y)
                for j in range(4):
                    project(V, f"u{j}", layer, columns(12, j), y)
                pe.wait_ge(vn2_ready, layer + 1)
                for g in range(SGU_G):
                    name = f"mx{g}"
                    pe.wait_ge(V.free, V.reusable(layer, name))
                    for c in range(ST):
                        x = mm(ps[:, V.bank(name), c * P:(c + 1) * P], vs[:, c, g * P:(g + 1) * P],
                               wsT[:, g, :], True, True)
                    x.then_inc(V.full, 1)

                pe.wait_ge(mix_ready, layer + 1)
                for m in range(DK):
                    w = (need(13 + m // 2) if m % 2 == 0 else ring[:, (13 + m // 2) % RING, :])
                    w = w.rearrange("p (k n) -> p k n", k=16)
                    project(V, f"w{m}", layer, lambda k: w[:, k, (m % 2) * P:(m % 2 + 1) * P],
                            lambda k: mix[:, k, :], 16)

                norm_sums(A, "norm2", layer, 14, DK, sq_ready, sq_free, sq)
                pe.wait_ge(y_ready, layer * 2 * DK + 2 * DK)
                for m in range(DK):
                    project(A, f"g{m}", layer, columns(17 + m // 4, m % 4), y)
                w = need(19)
                wp = w[:, 0:2 * D].rearrange("p (k n) -> p k n", k=2)
                pT = w[:, 2 * D:2 * D + 2 * S].rearrange("p (k n) -> p k n", k=2)
                for m in range(DK):
                    project(V, f"p{m}", layer, lambda k: wp[:, k, m * P:(m + 1) * P], lambda k: pT[:, k, :], 2)
            tail_pe(pe, mm)

        @block.scalar
        def _(act):
            act.wait_ge(const_in, 16 * N_CONST)

            act.wait_ge(prep_v, 1)
            nc.scalar.activation(prep_e, prep_n, ACT.Exp).then_inc(prep_a, 1)
            act.wait_ge(prep_v, 2)
            nc.scalar.activation(prep_l, prep_w, ACT.Ln).then_inc(prep_a, 1)
            nc.scalar.activation(cond[:], q_(par2, "cond", 0, 2 * DK).rearrange("p (k c) -> p k c", k=DK), ACT.Tanh,
                                 scale=0.5).then_inc(prep_a, 1)
            act.wait_ge(prep_v, 3)
            nc.scalar.activation(rcos, tmp[:, 0, :], ACT.Sin)
            nc.scalar.activation(rsin, tmp[:, 1, :], ACT.Sin).then_inc(prep_a, 1)

            def squares(first, n, tile, ready, ready_at, buf, cols=S, free_at=0, rd=None, fr=None):
                for k in range(n):
                    act.wait_ge(ready, ready_at(k))
                    if k >= 2:
                        act.wait_ge(fr or sq_free, free_at + k - 1)
                    nc.scalar.activation(buf[:, (first + k) % 2, 0:cols], tile(k), ACT.Square).then_inc(rd or sq_ready, 1)

            def root(pool, g, layer, i, width, out, cols=S, ready=None, free=None, per=NSTD):
                act.wait_ge(pool.full, pool.done(layer, g))
                act.wait_ge(free or std_free, layer * per + i + 1)
                nc.scalar.activation(out[:, i % 2, 0:cols], ps[:, pool.bank(g), 0:cols], ACT.Sqrt,
                                     bias=EPSC, scale=1.0 / width).then_inc(ready or std_ready, 1)

            with act.Fori(0, L) as layer:
                def full(pool, g):
                    pool_ = pool
                    act.wait_ge(pool_.full, pool_.done(layer, g))
                    return ps[:, pool.bank(g), :]

                squares(0, DK, lambda k: hT[:, k, :], h_ready, lambda k: layer * 2 * DK + k + 1, sq,
                        free_at=layer * 2 * (DK - 2))
                root(A, "norm1", layer, 0, D, std)
                act.drain().then_inc(A.free, 1)

                def gate(g, tile, i):
                    nc.scalar.activation(mix[:, tile, :], full(V, g), ACT.Tanh, scale=0.5).then_inc(th_ready, 1)

                for u in range(2):
                    for j in range(3):
                        i = 3 * u + j
                        x = full(A, f"xl{i}")
                        act.wait_ge(xl_free, layer * 6 + i + 1)
                        nc.scalar.activation(xl[:, i % 2, 4:4 + S], x, ACT.Copy).then_inc(xl_ready, 1)
                        act.drain().then_inc(A.free, 1)
                    gate(f"gl{u}", u, u)
                for i in range(2, 6):
                    gate(f"gl{i}", i, i)

                for g in range(2):
                    if g == 1:
                        act.wait_ge(lru_done, layer * 6 + 3)
                    for m in range(3):
                        i = 3 * g + m
                        nc.scalar.activation(mix[:, 9 + m, :], full(A, f"r{i}"), ACT.Tanh, scale=0.5,
                                             bias=par[:, PC["b_a"] + i:PC["b_a"] + i + 1]).then_inc(A.free, 1)
                        nc.scalar.activation(tmp[:, m, :], full(A, f"i{i}"), ACT.Tanh, scale=0.5,
                                             bias=par[:, PC["b_x"] + i:PC["b_x"] + i + 1]).then_inc(A.free, 1)
                        act.drain().then_inc(ri_ready, 1)
                    for m in range(3):
                        act.wait_ge(la_ready, layer * 6 + 3 * g + m + 1)
                        nc.scalar.activation(mix[:, 6 + m, :], mix[:, 9 + m, :], ACT.Exp)
                        nc.scalar.activation(mix[:, 9 + m, :], mix[:, 9 + m, :], ACT.Tanh).then_inc(at_ready, 1)
                    for t in range(ST):
                        cols = 512 if g == 0 else 256
                        nc.scalar.activation(vnat[:, t, 512 * g:512 * g + cols], full(A, f"v{g}.{t}")[:, 0:cols],
                                             ACT.Copy).then_inc(A.free, 1)
                    for m in range(3):
                        act.wait_ge(ratio_ready, layer * 6 + 3 * g + m + 1)
                        nc.scalar.activation(mix[:, 9 + m, :], mix[:, 9 + m, :], ACT.Sqrt).then_inc(us_ready, 1)
                act.drain().then_inc(vn_ready, 1)
                act.wait_ge(lru_done, layer * 6 + 6)
                for i in range(6):
                    gate(f"gr{i}", 6 + i, 6 + i)

                def out_root(h):
                    root(A, f"oss{h}", layer, 1 + h, P, std)
                    act.drain().then_inc(A.free, 1)

                for h in range(HEADS):
                    if h >= 1:
                        out_root(h - 1)
                    squares(DK + h, 1, lambda k: ps[:, V.bank(f"o{h}"), :], V.full,
                            lambda k: V.done(layer, f"o{h}"), sq)
                out_root(5)

                for t in range(ST):
                    x = full(A, f"vs{t}")
                    nc.scalar.activation(vs[:, t, :], x, ACT.Copy).then_inc(A.free, 1)
                act.drain().then_inc(vs_ready, 1)
                for j in range(4):
                    gate(f"gs{j}", 12 + j, 12 + j)
                act.wait_ge(var_ready, layer + 1)
                nc.scalar.activation(small[:, 0:ST], mv[:, :, 1], ACT.Sqrt, bias=EPSC).then_inc(sgu_std, 1)

                squares(14, DK, lambda k: hT[:, k, :], h_ready, lambda k: layer * 2 * DK + DK + k + 1, sq,
                        free_at=layer * 2 * (DK - 2) + DK - 2)
                root(A, "norm2", layer, 7, D, std)
                act.drain().then_inc(A.free, 1)
                for m in range(DK):
                    nc.scalar.activation(mix[:, m, :], full(A, f"g{m}"), ACT.Tanh, scale=0.5).then_inc(A.free, 1)
                    act.drain().then_inc(pg_ready, 1)
            tail_act(act, squares, root)

        @block.vector
        def _(dve):
            dve.sem_inc(V.free, len(V.banks))
            dve.sem_inc(A.free, len(A.banks))
            dve.sem_inc(std_free, 2)
            dve.sem_inc(xl_free, 2)
            nc.vector.memset(xl[:, :, 0:4], 0.0)
            nc.vector.memset(ones[:], 1.0)
            dve.wait_ge(const_in, 16 * N_CONST)

            lam = par_all[:, :, PC["lam"]:PC["lam"] + LRU_T]
            rate = par_all[:, :, PC["decay_rate"]:PC["decay_rate"] + LRU_T]
            nc.vector.tensor_scalar(prep_t, lam, -1.0, None, ALU.mult)
            dve.drain()
            nc.vector.tensor_tensor(prep_n, prep_t, lam, ALU.min).then_inc(prep_v, 1)
            dve.wait_ge(prep_a, 1)
            nc.vector.tensor_scalar(prep_w, prep_e, 1.0, None, ALU.add).then_inc(prep_v, 1)
            dve.wait_ge(prep_v, 2)
            nc.vector.tensor_scalar(prep_c, prep_w, -1.0, None, ALU.add)
            nc.vector.reciprocal(prep_r, prep_w)
            dve.drain()
            nc.vector.tensor_tensor(prep_c, prep_e, prep_c, ALU.subtract)
            nc.vector.tensor_scalar(prep_t, prep_t, 0.0, None, ALU.max)
            dve.drain()
            nc.vector.tensor_tensor(prep_c, prep_c, prep_r, ALU.mult)
            dve.drain()
            dve.wait_ge(prep_a, 2)
            nc.vector.tensor_tensor(prep_c, prep_c, prep_l, ALU.add)
            dve.drain()
            nc.vector.tensor_tensor(prep_c, prep_c, prep_t, ALU.add)
            dve.drain()
            nc.vector.tensor_scalar(rate, prep_c, -4.0, None, ALU.mult)
            for name in ("b_a", "b_x"):
                v = par_all[:, :, PC[name]:PC[name] + LRU_T]
                nc.vector.tensor_scalar(v, v, 0.5, None, ALU.mult)

            dve.wait_ge(prep_a, 3)
            nc.vector.scalar_tensor_tensor(cond[:], cond[:], 1.0, q_(par2, "cond", 0, 2 * DK).rearrange(
                "p (k c) -> p k c", k=DK), ALU.add, ALU.mult)
            dve.drain()
            nc.vector.tensor_scalar(cond[:], cond[:], 0.5, None, ALU.mult).then_inc(cond_ready, 1)

            dve.wait_ge(pos_in, 16)
            posi, ang, turn, turni = tmp[:, 2, :], tmp[:, 3, :], xc[:, 0, :], xc[:, 1, :]
            nc.vector.tensor_copy(ang, posi.bitcast(I32))
            dve.drain()
            nc.vector.tensor_scalar(ang, ang, q_(par2, "inv_freq"), None, ALU.mult)
            dve.drain()
            for out, quarter in ((tmp[:, 0, :], 0.25), (tmp[:, 1, :], 0.0)):
                nc.vector.tensor_scalar(turni.bitcast(I32), ang, 1.0 / (2 * np.pi), quarter, ALU.mult, ALU.add)
                dve.drain()
                nc.vector.tensor_copy(turn, turni.bitcast(I32))
                dve.drain()
                if quarter:
                    nc.vector.tensor_scalar(turn, turn, -quarter, None, ALU.add)
                    dve.drain()
                nc.vector.scalar_tensor_tensor(out, turn, -TWO_PI[0], ang, ALU.mult, ALU.add)
                dve.drain()
                for part in TWO_PI[1:]:
                    nc.vector.scalar_tensor_tensor(out, turn, -part, out, ALU.mult, ALU.add)
                    dve.drain()
                nc.vector.tensor_scalar(out, out, 3.1415925, -3.1415925, ALU.min, ALU.max)
                dve.drain()
            dve.sem_inc(prep_v, 1)
            dve.wait_ge(prep_a, 4)
            nc.vector.tensor_scalar(rsin, rsin, q_(par2, "rope_sign"), None, ALU.mult)
            dve.drain()
            dve.wait_ge(x_in, 16 * DK)
            dve.sem_inc(h_ready, DK)

            def p_(name, i, n=1):
                return par[:, PC[name] + i:PC[name] + i + n]

            def inverse(i, ready, free_at, buf, cols=S):
                dve.wait_ge(ready, free_at)
                r = buf[:, i % 2, 0:cols]
                nc.vector.reciprocal(r, r)
                dve.drain()
                return r

            def rope(src, dst, t, cos, sin, halves):
                nc.vector.tensor_tensor(dst, src, cos, ALU.mult)
                for a, b in halves:
                    nc.vector.tensor_tensor(t[b[0]:b[1]], src[a[0]:a[1]], sin[a[0]:a[1]], ALU.mult)
                dve.drain()
                return nc.vector.tensor_tensor(dst, dst, t, ALU.add)

            with dve.Fori(0, L) as layer:
                def full(pool, g):
                    dve.wait_ge(pool.full, pool.done(layer, g))
                    return ps[:, pool.bank(g), :]

                nc.vector.tensor_copy(par[:].unsqueeze(1), par_all[:, bass.ds(layer, 1), :])
                dve.drain()

                r = inverse(0, std_ready, layer * NSTD + 1, std)
                for k in range(DK):
                    nc.vector.scalar_tensor_tensor(yT[:, k, :], hT[:, k, :], p_("mix_norm", k), r, ALU.mult,
                                                   ALU.mult).then_inc(y_ready, 1)
                dve.drain().then_inc(std_free, 1)

                def silu2(g, tile, n):
                    x = full(V, g)
                    dve.wait_ge(th_ready, layer * 16 + n + 1)
                    nc.vector.scalar_tensor_tensor(mix[:, tile, :], mix[:, tile, :], 1.0, x, ALU.add,
                                                   ALU.mult).then_inc(V.free, 1)

                def conv(i):
                    dve.wait_ge(xl_ready, layer * 6 + i + 1)
                    x, o = xl[:, i % 2, :], xc[:, i, :]
                    nc.vector.tensor_scalar(o, x[:, 1:1 + S], p_("conv_w", i), p_("conv_b", i), ALU.mult, ALU.add)
                    for w in range(1, CONV):
                        dve.drain()
                        last = nc.vector.scalar_tensor_tensor(o, x[:, 1 + w:1 + w + S], p_("conv_w", w * LRU_T + i),
                                                              o, ALU.mult, ALU.add)
                    last.then_inc(xc_ready, 1)
                    dve.drain().then_inc(xl_free, 1)

                for u in range(2):
                    for j in range(3):
                        conv(3 * u + j)
                    silu2(f"gl{u}", u, u)
                for i in range(2, 6):
                    silu2(f"gl{i}", i, i)

                for g in range(2):
                    for m in range(3):
                        dve.wait_ge(ri_ready, layer * 6 + 3 * g + m + 1)
                        t = mix[:, 9 + m, :]
                        nc.vector.tensor_scalar(t, t, 1.0, p_("decay_rate", 3 * g + m), ALU.add,
                                                ALU.mult).then_inc(la_ready, 1)
                    for m in range(3):
                        dve.wait_ge(at_ready, layer * 6 + 3 * g + m + 1)
                        t, d = mix[:, 9 + m, :], tmp[:, 3, :]
                        nc.vector.tensor_scalar(d, t, -1.0, 1.0, ALU.mult, ALU.add)
                        dve.drain()
                        nc.vector.reciprocal(d, d)
                        dve.drain()
                        nc.vector.scalar_tensor_tensor(t, t, -2.0, d, ALU.mult, ALU.mult).then_inc(ratio_ready, 1)
                        dve.drain()
                    dve.wait_ge(A.full, A.done(layer, f"i{3 * g + 2}"))
                    for m in range(3):
                        i = 3 * g + m
                        x, a, uu = xc[:, i, :], mix[:, 6 + m, :], mix[:, 9 + m, :]
                        nc.vector.scalar_tensor_tensor(x, tmp[:, m, :], 1.0, x, ALU.add, ALU.mult)
                        dve.drain()
                        dve.wait_ge(us_ready, layer * 6 + i + 1)
                        nc.vector.scalar_tensor_tensor(uu, x, 0.5, uu, ALU.mult, ALU.mult)
                        dve.drain()
                        nc.vector.tensor_tensor_scan(x, a, uu, 0.0, ALU.mult, ALU.add)
                        dve.drain()
                        nc.vector.scalar_tensor_tensor(mix[:, i, :], x, 0.5, mix[:, i, :], ALU.mult,
                                                       ALU.mult).then_inc(lru_done, 1)
                dve.drain()
                for i in range(6):
                    silu2(f"gr{i}", 6 + i, 6 + i)
                dve.drain()

                def rotated(h):
                    for w, name in enumerate(("q", "k")):
                        x = full(V, f"{name}{h}")
                        last = rope(x, qk[:, 2 * (h % 2) + w, :], tmp[:, w, :], rcos, rsin,
                                    (((0, 64), (64, 128)), ((64, 128), (0, 64))))
                        dve.drain().then_inc(V.free, 1)
                    dve.drain().then_inc(qk_ready, 1)

                def normed(h):
                    r = inverse(1 + h, std_ready, layer * NSTD + 1 + h + 1, std)
                    nc.vector.scalar_tensor_tensor(mix[:, 6 + h, :], mix[:, 6 + h, :], 0.5, r, ALU.mult, ALU.mult)
                    dve.drain().then_inc(std_free, 1)

                rotated(0)
                for h in range(1, HEADS + 1):
                    if h < HEADS:
                        rotated(h)
                    if h >= 2:
                        normed(h - 2)
                    g, at_c = h - 1, 0
                    for c in range(ST):
                        x, n = full(V, f"s{g}.{c}"), S - c * P
                        nc.vector.tensor_tensor(dec_s[:, at_c:at_c + n], x[:, 0:n], decay[:, g, 0:n],
                                                ALU.mult).then_inc(s_ready, 1)
                        dve.drain().then_inc(V.free, 1)
                        at_c += n
                    x = full(V, f"o{g}")
                    dve.wait_ge(sq_ready, layer * NSQ + DK + g + 1)
                    nc.vector.scalar_tensor_tensor(mix[:, 6 + g, :], x, p_("ret_norm", g), mix[:, 6 + g, :],
                                                   ALU.mult, ALU.mult)
                    dve.drain().then_inc(V.free, 1)
                normed(5)

                dve.wait_ge(sgu_in, layer * 64 + 64)
                nc.vector.tensor_tensor(wsT, wsT, tri[:].unsqueeze(1).to_broadcast([P, SGU_G, P]), ALU.mult)
                dve.wait_ge(vs_ready, layer + 1)
                for t in range(ST):
                    nc.vector.bn_stats(bn[:, t, :], vs[:, t, :])
                dve.drain()
                for t in range(ST):
                    nc.vector.bn_aggr(mv[:, t, :], bn[:, t, :])
                dve.drain().then_inc(var_ready, 1)
                for j in range(4):
                    silu2(f"gs{j}", 12 + j, 12 + j)
                dve.wait_ge(sgu_std, layer + 1)
                nc.vector.reciprocal(small[:, 4:4 + ST], small[:, 0:ST])
                dve.drain()
                for t in range(ST):
                    nc.vector.tensor_scalar(vs[:, t, :], vs[:, t, :], mv[:, t, 0:1], small[:, 4 + t:5 + t],
                                            ALU.subtract, ALU.mult)
                for k, op in ((0, ALU.mult), (1, ALU.add)):
                    dve.drain()
                    for t in range(ST):
                        nc.vector.tensor_tensor(vs[:, t, :], vs[:, t, :], lngb[:, k, :], op)
                dve.drain().then_inc(vn2_ready, 1)
                for j in range(4):
                    x = full(V, f"u{j}")
                    nc.vector.scalar_tensor_tensor(mix[:, 12 + j, :], x, 0.5, mix[:, 12 + j, :], ALU.mult,
                                                   ALU.mult).then_inc(V.free, 1)
                for j in range(4):
                    x = full(V, f"mx{j}")
                    nc.vector.tensor_tensor(tmp[:, j, :].rearrange("p (c i) -> p c i", c=ST),
                                            x.rearrange("p (c i) -> p c i", c=ST),
                                            bsb[:, j, :].unsqueeze(1).to_broadcast([P, ST, P]),
                                            ALU.add).then_inc(V.free, 1)
                dve.drain()
                for j in range(4):
                    nc.vector.tensor_tensor(mix[:, 12 + j, :], mix[:, 12 + j, :], tmp[:, j, :], ALU.mult)
                dve.drain().then_inc(mix_ready, 1)

                for m in range(DK):
                    nc.vector.tensor_tensor(hT[:, m, :], full(V, f"w{m}"), hT[:, m, :], ALU.add).then_inc(h_ready, 1)
                    dve.drain().then_inc(V.free, 1)
                r = inverse(7, std_ready, layer * NSTD + 8, std)
                for k in range(DK):
                    nc.vector.scalar_tensor_tensor(yT[:, k, :], hT[:, k, :], p_("ple_norm", k), r, ALU.mult,
                                                   ALU.mult).then_inc(y_ready, 1)
                dve.drain().then_inc(std_free, 1)
                for m in range(DK):
                    x = full(V, f"p{m}")
                    dve.wait_ge(pg_ready, layer * DK + m + 1)
                    t = tmp[:, m % 2, :]
                    nc.vector.scalar_tensor_tensor(t, mix[:, m, :], 1.0, x, ALU.add, ALU.mult)
                    dve.drain().then_inc(V.free, 1)
                    nc.vector.scalar_tensor_tensor(hT[:, m, :], t, 0.5, hT[:, m, :], ALU.mult,
                                                   ALU.add).then_inc(h_ready, 1)
                dve.drain()
            tail_dve(dve, inverse, rope)

        @block.gpsimd
        def _(pool):
            for dst, name in ((ident[:], "ident"), (tri[:], "tri"), (before[:], "before"), (cst[:], "cst"),
                              (par_all[:], "par"), (par2[:], "par2"), (cst_i[:], "cst_i")):
                pool.dma_start(dst, io[name]).then_inc(const_in, 16)
            pool.dma_start(decay, io["decay"]).then_inc(const_in, 16)
            pool.dma_start(brt[:], io["b_router"].partition_broadcast(P)).then_inc(const_in, 16)
            pool.dma_start(tmp[:, 2, :].bitcast(I32), io["positions"].partition_broadcast(P)).then_inc(pos_in, 16)
            pool.dma_start(list_dram[:, :], io["list_init"]).then_inc(list_init, 16)
            for t in range(ACC_ROWS // P):
                pool.dma_start(acc_dram[t * P:(t + 1) * P, :], io["zeros"]).then_inc(acc_init, 16)
            for layer in range(L):
                if layer:
                    pool.wait_ge(mix_ready, layer)
                pool.dma_start(lngb[:, 0, :], io["ln_g"][layer].partition_broadcast(P)).then_inc(sgu_in, 16)
                pool.dma_start(lngb[:, 1, :], io["ln_b"][layer].partition_broadcast(P)).then_inc(sgu_in, 16)
                pool.dma_start(bsb, io["b_s"][layer].partition_broadcast(P)).then_inc(sgu_in, 16)
                pool.dma_start(wsT, io["wsT"][layer]).then_inc(sgu_in, 16)
            pool.wait_ge(h_ready, (2 * L + 1) * DK)
            pool.dma_start(ctxT, io["ctxT"]).then_inc(c_in, 16)
            pool.dma_start(acos, io["axial_cos"]).then_inc(late_in, 16)
            pool.dma_start(asin, io["axial_sin"]).then_inc(late_in, 16)

            bias_pool(pool)
            pool.wait_ge(list_init, 16)
            pool.wait_ge(acc_init, 16 * (ACC_ROWS // P))
            pool.wait_ge(ent_ready, 1)
            for j in range(ST * TOP):
                nc.gpsimd.indirect_dma_start(out=list_dram[:, :],
                                             out_offset=bass.IndirectOffsetOnAxis(ap=slot_u[:, j:j + 1], axis=0),
                                             in_=ent_i[:, j, :], in_offset=None).then_inc(list_out, 16)
            experts_pool(pool)


def constants():
    f = np.float32
    p = np.arange(P)
    j = np.arange(S)
    log_g = np.log1p(-np.exp2(f(-5.0) - np.arange(HEADS, dtype=f))).astype(f)
    diff = j[None, :] - p[:, None]
    decay = np.where(diff[:, None, :] >= 0,
                     np.exp(np.maximum(diff, 0)[:, None, :] * log_g[None, :, None].astype(np.float64)), 0.0)
    half = np.arange(64, dtype=f)
    inv = (f(10000.0) ** (-half / f(64))).astype(f)
    inv2 = (f(10000.0) ** (-np.arange(0, 64, 2, dtype=f) / f(64))).astype(f)
    axis, i = p // 64, p % 32
    place = np.where(axis[:, None] == 0, (j // 64)[None, :], (j % 64)[None, :]).astype(f)
    ang = (place * inv2[i][:, None]).astype(f).astype(np.float64)
    sign = np.where((p // 32) % 2 == 0, 1.0, -1.0)[:, None]
    slots = np.arange(LIST_ROWS)
    return {
        "ident": np.eye(P, dtype=f), "tri": np.triu(np.ones((P, P), f)), "before": np.triu(np.ones((P, P), f), 1),
        "cst": np.tile(np.concatenate([np.arange(E_N), 2 * np.arange(24)]).astype(f), (P, 1)),
        "cst_i": (p[:, None] + P * (np.arange(ST * TOP) // TOP)[None, :]).astype(np.int32),
        "decay": (decay * P ** -0.5).astype(f),
        "axial_cos": np.cos(ang).astype(f), "axial_sin": (np.sin(ang) * sign).astype(f),
        "list_init": np.stack([S + slots % P, 0 * slots], 1).astype(np.int32),
        "inv_freq": inv[p % 64][:, None], "rope_sign": np.where(p < 64, 1.0, -1.0).astype(f)[:, None],
        "part": p.astype(f)[:, None], "part32": (p % E_N).astype(f)[:, None], "zeros": np.zeros((P, D), f),
    }


def tiles(v):
    v = np.asarray(v)
    return np.moveaxis(v.reshape(*v.shape[:-1], -1, P), -1, 0)


def unit(w, k):
    w = w.reshape(k, P, -1).transpose(1, 0, 2).reshape(P, -1)
    return np.pad(w, ((0, 0), (0, UNIT - w.shape[1])))


def layout(x):
    c = constants()
    X = {k: np.asarray(v) for k, v in x.items()}
    units = []
    for l in range(L):
        w = X["w_in"][l]
        sizes = np.cumsum([0, 768, 768, 768, 768, 768, 768, 512, 512, 512])
        xl, gl, q, k, v, gr, u, vs, gs = (w[:, a:b] for a, b in zip(sizes[:-1], sizes[1:]))
        t = lambda m, i, n=1: m[:, i * P:(i + n) * P]
        cat = lambda *a: np.concatenate(a, axis=1)
        wbd = np.zeros((2, 2, len(PAIRS), P, P), np.float32)
        for wi, name in enumerate(("lru_w_a", "lru_w_x")):
            for g in range(2):
                for n, (kt, mt) in enumerate(PAIRS):
                    for b in range(4):
                        r0, r1 = max(kt * P, b * 96), min((kt + 1) * P, (b + 1) * 96)
                        c0, c1 = max(mt * P, b * 96), min((mt + 1) * P, (b + 1) * 96)
                        if r0 < r1 and c0 < c1:
                            wbd[wi, g, n, r0 - kt * P:r1 - kt * P, c0 - mt * P:c1 - mt * P] = \
                                X[name][l, 4 * g + b, r0 - b * 96:r1 - b * 96, c0 - b * 96:c1 - b * 96]
        lru = wbd.transpose(3, 0, 1, 2, 4).reshape(P, -1)
        mats = [cat(t(xl, 0, 3), t(gl, 0)), cat(t(xl, 3, 3), t(gl, 1)), t(gl, 2, 4), None,
                v[:, 0:512], cat(v[:, 512:], t(gr, 0, 2)), t(gr, 2, 4)]
        mats += [cat(t(q, 2 * i), t(k, 2 * i), t(q, 2 * i + 1), t(k, 2 * i + 1)) for i in range(3)]
        mats += [vs, gs, u]
        units += [np.pad(lru, ((0, 0), (0, UNIT - lru.shape[1]))) if m is None else unit(m, DK) for m in mats]
        units += [unit(X["w_out"][l][:, i * 256:(i + 1) * 256], 16) for i in range(4)]
        units += [unit(X["w_ple_gate"][l][:, i * 512:(i + 1) * 512], DK) for i in range(2)]
        wp = X["w_ple_proj"][l].reshape(2, P, D).transpose(1, 0, 2).reshape(P, -1)
        pT = X["p"][l, 0].T.reshape(2, P, S).transpose(1, 0, 2).reshape(P, -1)
        last = np.concatenate([wp, pT], axis=1)
        units.append(np.pad(last, ((0, 0), (0, UNIT - last.shape[1]))))
    w = X["w_ada_2"][0]
    units += [unit(w[:, i * 512:(i + 1) * 512], DK) for i in range(12)]
    w = X["w_in_2"][0]
    units += [unit(w[:, 512:1024], DK), unit(w[:, 0:512], DK)]
    units += [unit(w[:, 1024 + 512 * i:1536 + 512 * i], DK) for i in range(3)]
    w = X["w_out_2"][0]
    units += [unit(w[:, i * 512:(i + 1) * 512], DK) for i in range(2)]
    units.append(np.pad(X["w_router_2"][0].reshape(DK, P, E_N), ((0, 0), (0, 0), (0, 512 - E_N)))
                 .transpose(1, 0, 2).reshape(P, -1))
    assert len(units) == L * UNITS_LAYER + UNITS_TAIL

    gu = X["w_gate_up_2"][0].reshape(E_N, DK, P, 2, 2, 512)
    dn = X["w_down_2"][0].reshape(E_N, DK, P, 2, 512)
    w_moe = np.empty((E_N, 6, P, DK, 512), np.float32)
    for half in range(2):
        for part in range(2):
            w_moe[:, 2 * half + part] = gu[:, :, :, part, half].transpose(0, 2, 1, 3)
        w_moe[:, 4 + half] = dn[:, :, :, half].transpose(0, 2, 1, 3)
    bg = X["b_gate_up_2"][0].reshape(E_N, 2, 2, 512).transpose(0, 2, 1, 3).reshape(E_N, 2048)
    par = np.concatenate([tiles(X["mix_norm"]), tiles(X["ple_norm"]),
                          tiles(X["lru_conv_w"]).reshape(P, L, -1), tiles(X["lru_conv_b"]), tiles(X["lru_b_a"]),
                          tiles(X["lru_b_x"]), tiles(X["lru_lambda"]), tiles(X["ret_norm"]),
                          np.zeros((P, L, LRU_T), np.float32)], axis=2)
    cond = np.stack([tiles(X["c_2"][0]), tiles(X["c_ctx_2"])], axis=-1).reshape(P, -1)
    par2 = np.concatenate([tiles(X["final_norm"]), tiles(X["b_ada_2"][0]), tiles(X["g_norm1_2"][0]),
                           tiles(X["g_norm2_2"][0]), X["g_q_2"][0][:, None], X["g_k_2"][0][:, None],
                           tiles(X["w_conv_2"][0]).reshape(P, -1), tiles(X["g_final_2"]), cond,
                           c.pop("inv_freq"), c.pop("rope_sign"), c.pop("part"), c.pop("part32")], axis=1)
    out = dict(c)
    out.update({
        "xT": X["x"][0].T, "units": np.stack(units), "w_moe": w_moe.reshape(E_N * 6, P, UNIT),
        "b_moe": np.concatenate([bg, X["b_down_2"][0]], axis=1), "par": par, "par2": par2,
        "b_router": X["b_router_2"][0], "positions": X["positions"][0],
        "ln_g": X["sgu_ln_g"], "ln_b": X["sgu_ln_b"], "b_s": X["sgu_b_s"],
        "wsT": X["sgu_w_s"].transpose(0, 3, 1, 2),
        "ctxT": X["ctx_2"][0].T.reshape(DK, P, CTX).transpose(1, 0, 2),
    })
    return {k: np.ascontiguousarray(v) for k, v in out.items()}


def kernel(**inputs):
    import concourse.bacc as bacc
    from concourse.bass_utils import run_bass_kernel_spmd as run

    nc = bacc.Bacc("TRN2", target_bir_lowering=False, num_devices=1)
    arrays = {f"in_{k}": v for k, v in layout(inputs).items()}
    io = {k[3:]: nc.dram_tensor(k, v.shape, mybir.dt.from_np(v.dtype), kind="ExternalInput").ap()
          for k, v in arrays.items()}
    io["out"] = nc.dram_tensor("out_T", (D, S), F32, kind="ExternalOutput").ap()
    build(nc, io)
    r = run(nc, [arrays], core_ids=[0])
    return np.ascontiguousarray(np.asarray(r.results[0]["out_T"]).T).reshape(1, S, D)
```

```python
from contextlib import ExitStack

import numpy as np
import concourse.bass as bass
from concourse import mybir

F32 = mybir.dt.float32
F32R = mybir.dt.float32r
I32 = mybir.dt.int32
U32 = mybir.dt.uint32
ALU = mybir.AluOpType
ACT = mybir.ActivationFunctionType
AX = mybir.AxisListType

N_CONST = 6
EPSC = 1e-6
_LOW = int((2 * np.pi - 6.28125) * 2 ** 21) / 2 ** 21
TWO_PI = (6.28125, _LOW, 2 * np.pi - 6.28125 - _LOW)

P = 128
S = 512
D = 1024
DK = D // P
ST = S // P
L = 2
LRU_T = 768 // P
LRU_BLOCK = 96
HEADS = 6
CONV = 4
SGU_G = 4
CTX = 256
QH, KVH = 4, 2
KEYS = S + CTX
KT = KEYS // P
E_N, TOP = 32, 4
DFF = 1024
LIMIT, ALPHA = 7.0, 1.702
BLOCKS = 48
LISTS = BLOCKS + 1
ACC_ROWS = S + P

UNIT = 4096
HALF = UNIT // 2
HALVES = 12
RAW, SPLIT = 6, 4
ORDER = [(j, q) for j in range(4) for q in range(2)] + [(4, 0), (5, 0), (4, 1), (5, 1)]
POOL_LOW = (2, 6, 10)
DVE_LOW = tuple(h for h in range(HALVES) if h not in POOL_LOW)

PIECE = UNIT // 4
A_RAW, A_SPLIT = 5, 4


def layer_pieces():
    v, a, n = "V", "A", iter(range(1, 100))
    col = lambda pool, *names: [(g, True, pool, g) for g in names]

    def partial(name, count, last):
        return [(f"{name}.{q}", True, "part", next(n)) if q < count - 1 else (f"{name}.{q}", True, a, last)
                for q in range(count)]

    out = col(a, "xl0", "xl1", "xl2") + col(v, "gl0") + col(a, "xl3", "xl4", "xl5") + \
        col(v, *(f"gl{i}" for i in range(1, 6)))
    for g, count in ((0, 4), (1, 2)):
        out += [(f"lru{g}.{w}", False, a, f"i{3 * g + 2}") for w in range(2)]
        out += partial(f"v{g}", count, f"v{g}.{ST - 1}")
        out += col(v, *(f"gr{i}" for i in (range(2) if g == 0 else range(2, 6))))
    for h in range(HEADS):
        out += col(v, f"q{h}", f"k{h}")
    out += partial("vs", 4, f"vs{ST - 1}")
    out += col(v, *(f"gs{i}" for i in range(4)), *(f"u{i}" for i in range(4)))
    out += partial("wo", 16, f"w{DK - 1}")
    out += col(a, *(f"g{i}" for i in range(DK)))
    out += [(f"ple{i}", False, v, f"p{DK - 1}") for i in range(4)]
    return out, next(n) - 1


def tail_pieces():
    out = [("k0", True, "BV", "kx0"), ("k1", True, "BV", "kx1")]
    out += [(f"v{q}", True, "BA", f"vx{ST - 1}") for q in range(2)]
    for j in range(12):
        out += [(f"ada{j}.{c}", False, "ada_part", 3 * j + c + 1) if c < 3 else (f"ada{j}.3", False, "BA", f"ar{j}")
                for c in range(4)]
    out += [(f"{n}{i}", True, pool, f"{n}{i}") for n, pool in (("q", "BV"), ("cb", "BA"), ("cc", "BA"), ("cx", "BV"))
            for i in range(4)]
    out += [(f"w{i}", True, "CV", f"w{i}") for i in range(DK)]
    return out + [("router", False, "CV", "logits")]


LAYER, PARTS = layer_pieces()
TAIL = tail_pieces()
L_SPLIT = [i for i, x in enumerate(LAYER) if x[1]]
T_SPLIT = [i for i, x in enumerate(TAIL) if x[1]]
NP, NS = len(LAYER), len(L_SPLIT)
L_AT = {LAYER[i][0]: n for n, i in enumerate(L_SPLIT)}
T_AT = {TAIL[i][0]: n for n, i in enumerate(T_SPLIT)}
assert NP % A_RAW == 0 and NS % A_SPLIT == 0
assert L_SPLIT[:A_SPLIT] == T_SPLIT[:A_SPLIT] == list(range(A_SPLIT))

PC = {}
_n = 0
for _name, _w in (("mix_norm", DK), ("ple_norm", DK), ("conv_w", CONV * LRU_T), ("conv_b", LRU_T),
                  ("b_a", LRU_T), ("b_x", LRU_T), ("lam", LRU_T), ("ret_norm", HEADS),
                  ("decay_rate", LRU_T)):
    PC[_name] = _n
    _n += _w
NPAR = _n
QC = {}
_n = 0
for _name, _w in (("final_norm", DK), ("b_ada", 48), ("g_norm1", DK), ("g_norm2", DK), ("g_q", 1), ("g_k", 1),
                  ("w_conv", 12), ("g_final", DK), ("cond", 2 * DK), ("inv_freq", 1), ("rope_sign", 1),
                  ("part", 1), ("part32", 1), ("dump", 1)):
    QC[_name] = _n
    _n += _w
NPAR2 = _n


def q_(par2, name, i=0, n=1):
    return par2[:, QC[name] + i:QC[name] + i + n]


C_IOTA, C_EVEN, C_EDGE, C_NEG, C_TOKEN = 0, E_N, E_N + 24, E_N + 24 + LISTS + 1, E_N + 24 + LISTS + 1 + P
C_END = C_TOKEN + ST * TOP


class Groups:

    def __init__(self, nc, ctx, name, banks, order, pre=0):
        self.full = ctx.enter_context(nc.semaphore(f"{name}_full"))
        self.free = ctx.enter_context(nc.semaphore(f"{name}_free"))
        self.banks, self.order, self.n, self.pre = banks, order, len(order), pre
        self.at = {g: i for i, g in enumerate(order)}
        assert len(self.at) == self.n

    def bank(self, g):
        return self.banks[self.at[g] % len(self.banks)]

    def done(self, layer, g):
        return layer * self.n + self.at[g] + 1 + self.pre

    def reusable(self, layer, g):
        i, c = self.at[g], len(self.banks)
        if i >= c:
            return layer * self.n + i + 1 + self.pre
        last = max(j for j in range(self.n) if j % c == i)
        return layer * self.n + last + 1 + c - self.n + self.pre


class Ahead:

    def __init__(self, n):
        self.n = n

    def up_to(self, n, end):
        todo = range(self.n, min(n + 1, end))
        self.n = max(self.n, todo.stop)
        return todo


def ret_gate(i):
    return 12 + i if i < 4 else 6 + i


PRODUCTS = ((0, 0), (0, 1), (1, 0))


def lru_pairs():
    return [(k, m) for m in range(3) for k in range(3)
            if any(max(k * P, b * LRU_BLOCK) < min((k + 1) * P, (b + 1) * LRU_BLOCK)
                   and max(m * P, b * LRU_BLOCK) < min((m + 1) * P, (b + 1) * LRU_BLOCK) for b in range(4))]


PAIRS = lru_pairs()


def build(nc, io):
    ctx = ExitStack()
    with ctx:
        def sb(name, shape, dt=F32):
            return ctx.enter_context(nc.sbuf_tensor(name, shape, dt))

        def sem(name):
            return ctx.enter_context(nc.semaphore(name))

        hT = sb("hT", [P, DK, S])
        ident = sb("ident", [P, P])
        ones = sb("ones", [P, P])
        before = sb("before", [P, P])
        cst = sb("cst", [P, C_END])
        brt = sb("router_bias", [P, E_N])
        cond = sb("cond", [P, DK, 2])
        tri = sb("tri", [P, P])
        par_all = sb("par_all", [P, L, NPAR])
        par = sb("par", [P, NPAR])
        par2 = sb("par2", [P, NPAR2])
        mv = sb("mv", [P, ST, 2])
        bn = sb("bn", [P, ST, 6])
        small = sb("small", [P, 64])
        ada = sb("ada", [P, 48, 2])
        coef = sb("coef", [P, 3, DK])
        list_tok = sb("slot_tokens", [P, LISTS], I32)
        list_gate = sb("slot_gates", [P, LISTS])
        lst = sb("lst", [P, 2, 2], I32)
        rows_i = sb("rows_i", [P, 2], I32)
        np_i = sb("np_i", [1, 1], I32)
        be_r = sb("be_r", [1, LISTS], I32)
        scr_size = 17700
        early = ExitStack()
        mix = early.enter_context(nc.sbuf_tensor("mix", [P, 16, S], F32))
        pieces = early.enter_context(nc.sbuf_tensor("pieces", [P, A_RAW, PIECE], F32))
        wps = early.enter_context(nc.sbuf_tensor("pieces_split", [P, A_SPLIT, 2, PIECE], F32R))
        ys = early.enter_context(nc.sbuf_tensor("y_split", [P, 2, DK, S], F32R))
        scr = early.enter_context(nc.sbuf_tensor("scr", [P, scr_size], F32))
        early.close()
        early = ExitStack()
        early.enter_context(nc.sbuf_tensor("tiles_0_3", [P, 4, S], F32))
        hcs = early.enter_context(nc.sbuf_tensor("context_split", [P, 2, DK, CTX], F32R))
        early.close()
        raw = sb("raw", [P, RAW, HALF])
        wsp = sb("w_split", [P, SPLIT, 2, HALF], F32R)
        hTe = sb("hidden_T", [P, 2, D], F32R)
        xgT = sb("rows_T", [P, 2, 2, D], F32R)
        sb("routing_end", [P, D])
        xgy = sb("rows", [P, 4, D])
        h_sb = sb("hidden", [P, D])
        act_buf = sb("act_buf", [P, 3, S])
        b_split = sb("bias_split", [2 * E_N, 3 * D], F32R)
        sel = sb("expert_rows", [2 * E_N, 2, P], F32R)
        be_bc = sb("block_experts", [P, LISTS])
        xg, y_sb = xgy[:, 0:2, :], xgy[:, 2:4, :]
        b_raw = xgy[0:2 * E_N, 0:3, :].rearrange("p a b -> p (a b)")
        place = h_sb[:].rearrange("p (s k q) -> p s k q", s=2, k=TOP)
        flat = act_buf[:].rearrange("p a b -> p (a b)")
        owner = flat[:, 0:2 * TOP * 3 * LISTS].rearrange("p (s k c b) -> p s k c b", s=2, k=TOP, c=3)
        reached = flat[:, 2 * TOP * 3 * LISTS:2 * TOP * 3 * LISTS + TOP * (LISTS + 1)].rearrange("p (k b) -> p k b", k=TOP)
        at_ = 2 * TOP * 3 * LISTS + TOP * (LISTS + 1)
        first_past, rem = flat[:, at_:at_ + TOP], flat[:, at_ + TOP:at_ + 2 * TOP]
        empty = flat[:, at_ + 2 * TOP:at_ + 2 * TOP + LISTS]
        glu, thb, lin = (act_buf[:, i, :] for i in range(3))
        ps = ctx.enter_context(nc.psum_tensor("ps", [P, 8, 512], F32))

        def carve(at, *dims):
            n = int(np.prod(dims))
            assert at[0] + n <= scr_size, at
            v = scr[:, at[0]:at[0] + n]
            at[0] += n
            if len(dims) == 2:
                v = v.rearrange("p (a b) -> p a b", a=dims[0])
            return v

        at = [0]
        vnat = carve(at, ST, 768)
        decay = carve(at, HEADS, S)
        rcos, rsin = carve(at, S), carve(at, S)
        sq = carve(at, 2, S)
        std = carve(at, 2, S)
        tmp = carve(at, 4, S)
        xl = carve(at, 2, S + 4)
        work = carve(at, 3328)
        lngb = carve(at, 2, S)
        bsb = carve(at, SGU_G, P)
        wsT = carve(at, SGU_G, P)
        prep = work[:, 5 * S:5 * S + 7 * L * LRU_T].rearrange("p (a b) -> p a b", a=7)
        xc = work[:, 0:LRU_T * S].rearrange("p (a b) -> p a b", a=LRU_T)
        qk = work[:, 0:4 * S].rearrange("p (a b) -> p a b", a=4)
        dec_s = work[:, 4 * S:4 * S + 1280]
        vs = vnat[:, :, 0:S]

        at = [0]
        acos, asin = carve(at, S), carve(at, S)
        sq2 = carve(at, 2, S)
        std2 = carve(at, 2, S)
        tmp2 = carve(at, 4, S)
        kTa = carve(at, KVH, KEYS)
        vall = carve(at, KT, KVH * P)
        qTa = carve(at, QH, S)
        eT = carve(at, KT, S)
        prob = carve(at, 2, KEYS)
        ccb = carve(at, 4, S)
        ubuf = carve(at, S + 4)
        ctxT = mix[:, 0:4, :].rearrange("p a b -> p (a b)").rearrange("p (a b) -> p a b", a=DK)
        arow = tmp2[0:2, 0:2, :]
        h2T = mix[:, 0:DK, :]

        at = [0]
        logits = carve(at, ST, E_N)
        mx8 = carve(at, ST, 8)
        ix8 = carve(at, ST, 8)
        ixf = carve(at, ST, 8)
        hot = carve(at, ST * TOP, E_N)
        hot2 = carve(at, ST * TOP, E_N)
        chosen = carve(at, ST, E_N)
        posn = carve(at, ST, E_N)
        nblk, pend, pbase, zer, pend128 = (carve(at, E_N) for _ in range(5))
        gates = carve(at, ST, TOP)
        gsum = carve(at, ST)
        slotf = carve(at, ST * TOP)
        npI = carve(at, 1)
        hot2n = carve(at, 24)
        h2n = carve(at, ST, D)
        assert at[0] <= 6 * D

        h2_dram = nc.dram_tensor("h2_rows", [S, D], F32, kind="Internal").ap()
        acc_dram = nc.dram_tensor("acc_rows", [ACC_ROWS, D], F32, kind="Internal").ap()

        v_order, a_order = [], []
        a_order += [f"xl{i}" for i in range(6)]
        v_order += [f"gl{i}" for i in range(6)]
        for g in range(2):
            a_order += [f"{w}{3 * g + m}" for m in range(3) for w in ("r", "i")]
            a_order += [f"v{g}.{t}" for t in range(ST)]
        v_order += [f"gr{i}" for i in range(6)]
        for h in range(HEADS + 1):
            v_order += [f"q{h}"] if h < HEADS else []
            v_order += [f"s{h - 1}.{c}" for c in range(3)] if h >= 1 else []
            v_order += [f"k{h}"] if h < HEADS else []
            v_order += [f"o{h - 1}"] if h >= 1 else []
            a_order += [f"oss{h - 2}"] if h >= 2 else []
        a_order += ["oss5"]
        a_order += [f"vs{t}" for t in range(ST)]
        v_order += [f"gs{i}" for i in range(4)] + [f"u{i}" for i in range(4)] + [f"mx{i}" for i in range(4)]
        v_order += [f"w{i}" for i in range(4)]
        a_order += [f"w{i}" for i in range(4, DK)]
        a_order += ["norm2"] + [f"g{i}" for i in range(DK)] + ["next"]
        v_order += [f"p{i}" for i in range(DK)]
        V = Groups(nc, ctx, "v", [0, 1, 2, 3], v_order)
        A = Groups(nc, ctx, "a", [4, 5, 6, 7], a_order, pre=1)
        bv_order = [f"ada{j}" for j in range(12)] + [f"kc{i}" for i in range(2)] + [f"kx{i}" for i in range(2)]
        ba_order = [f"ar{j}" for j in range(4)] + [f"ar{j}" for j in range(4, 6)] + ["cnorm", "xnorm"] + [f"ar{j}" for j in range(6, 12)] + [f"vc{t}" for t in range(2)] + [f"vx{t}" for t in range(ST)]
        ba_order += ["skc0", "skc1", "skx0", "skx1"]
        bv_order += [f"q{i}" for i in range(QH)]
        ba_order += [f"cb{i}" for i in range(4)] + [f"sq{i}" for i in range(QH)]
        ba_order += [f"cc{i}" for i in range(4)]
        bv_order += [f"cx{i}" for i in range(4)]
        BV = Groups(nc, ctx, "bv", [0, 1, 2, 3], bv_order)
        BA = Groups(nc, ctx, "ba", [4, 5, 6, 7], ba_order)
        CV = Groups(nc, ctx, "cv", [0, 1, 2, 3, 4, 5], [f"w{i}" for i in range(DK)] + ["logits", "pos", "lists"])
        CA = Groups(nc, ctx, "ca", [6, 7], ["norm2"] + [f"t{i}" for i in range(8)])
        DV = Groups(nc, ctx, "dv", [0, 1, 2, 3, 4, 5], [f"t{i}" for i in range(8)])

        const_in = sem("const_in")
        x_in = sem("x_in")
        par_in = sem("parameters_in")
        p_in = [sem(f"piece_in{i}") for i in range(A_RAW)]
        p_high, p_low = sem("piece_high"), sem("piece_low")
        part_used, ada_part = sem("piece_part_used"), sem("ada_part_used")
        yn_ready, yh_ready, yl_pool = sem("y_whole"), sem("y_high"), sem("y_low_pool")
        mixh, mixl = sem("mix_high"), sem("mix_low")
        arow_ready = sem("ada_rows")
        sgu_in = sem("sgu_in")
        h_ready = sem("h_ready")
        sq_ready, sq_free = sem("sq_ready"), sem("sq_free")
        std_ready, std_free = sem("std_ready"), sem("std_free")
        y_ready = sem("y_ready")
        pool_turns = sem("pool_turns")
        xl_ready, xl_free = sem("xl_ready"), sem("xl_free")
        xc_ready = sem("xc_ready")
        th_ready = sem("th_ready")
        ri_ready = sem("ri_ready")
        la_ready = sem("la_ready")
        at_ready = sem("at_ready")
        ratio_ready = sem("ratio_ready")
        us_ready = sem("us_ready")
        lru_done = sem("lru_done")
        vn_ready = sem("v_natural_ready")
        qk_ready = sem("qk_ready")
        s_ready = sem("s_ready")
        vs_ready = sem("vs_ready")
        var_ready = sem("var_ready")
        sgu_std = sem("sgu_std")
        vn2_ready = sem("gating_v_ready")
        mix_ready = sem("mix_ready")
        pg_ready = sem("ple_gate_ready")
        prep_v, prep_a = sem("prep_v"), sem("prep_a")

        NSQ, NSTD = 22, 8
        prep_t, prep_n, prep_w, prep_e, prep_l, prep_c, prep_r = (
            prep[:, i, :].rearrange("p (l t) -> p l t", l=L) for i in range(7))

        pools = {"V": V, "A": A, "BV": BV, "BA": BA, "CV": CV}

        def last_use(layer, piece):
            _, _, by, g = piece
            if by == "part":
                return part_used, layer * PARTS + g
            if by == "ada_part":
                return ada_part, g
            return pools[by].full, pools[by].done(layer, g)

        def landed(layer, n):
            return p_in[n % A_RAW], 16 * (layer * (NP // A_RAW) + n // A_RAW + 1)

        def piece_done(layer, n, tail=False):
            x = (TAIL if tail else LAYER)[n]
            if x[1]:
                return p_low, layer * NS + (T_SPLIT if tail else L_SPLIT).index(n) + 1
            return last_use(0 if tail else layer, x)

        f_ready, fm_ready = sem("x_ready"), sem("x_modulated")
        c_in, cm_ready, cmm_ready = sem("ctx_in"), sem("ctx_scaled"), sem("ctx_modulated")
        ch_ready, y2h_ready = sem("ctx_high"), sem("x_high")
        y2_ready = sem("x_shifted")
        cond_ready = sem("cond_ready")
        sq2_ready, sq2_free, std2_ready, std2_free = (sem(f"{n}2") for n in ("sqr", "sqf", "stdr", "stdf"))
        late_in = sem("late_const_in")
        v_done, qkv_done = sem("v_done"), sem("qkv_done")
        cb_ready, cc_ready = sem("cb_ready"), sem("cc_ready")
        sc_full, max_ready, exp_ready, prob_ready = sem("sc_full"), sem("max_ready"), sem("exp_ready"), sem("prob_ready")
        pt_full, pt_ready, o_full, o_ready = sem("pt_full"), sem("pt_ready"), sem("o_full"), sem("o_ready")
        conv_ready = sem("conv_ready")
        h3_ready, n2_scaled, h2_ready = sem("h3_ready"), sem("norm2_scaled"), sem("h2_ready")
        h2n_ready, h2_out = sem("h2n_ready"), sem("h2_out")
        chosen_ready, gate_exp, gate_d = sem("chosen_ready"), sem("gate_exp"), sem("gate_d")
        be_ready, np_ready = sem("be_ready"), sem("np_ready")
        onehot_ready, onehot_used, list_ready, acc_init = sem("onehot_ready"), sem("onehot_used"), sem("list_ready"), sem("acc_init")

        SCORE_BANK = (0, 2, 6)
        low_v, low_p = sem("low_ready_v"), sem("low_ready_p")
        ATT_SCALE = float(P) ** -0.5
        SH1, SC1, GT1, SH2, SC2, GT2 = range(0, 48, 8)

        def tail_sp(sp):
            for t in range(A_RAW, len(TAIL)):
                sp.wait_ge(*piece_done(L, t - A_RAW, tail=True))
                sp.dma_start(pieces[:, t % A_RAW, :], io["pieces"][L * NP + t]).then_inc(p_in[t % A_RAW], 16)
            bias_sp(sp)
            for t in range(ST):
                sp.wait_ge(h2n_ready, t + 1)
                sp.dma_start(h2_dram[t * P:(t + 1) * P, :], h2n[:, t, :]).then_inc(h2_out, 16)
            experts_sp(sp)

        def tail_pe(pe, mm):
            def direct(name):
                t = [x[0] for x in TAIL].index(name)
                pe.wait_ge(*landed(L, t))
                return pieces[:, t % A_RAW, :].rearrange("p (k n) -> p k n", k=DK)

            def direct_router():
                t = len(TAIL) - 1
                pe.wait_ge(*landed(L, t))
                return pieces[:, t % A_RAW, 0:DK * E_N].rearrange("p (k n) -> p k n", k=DK)

            def high_of(name):
                pe.wait_ge(p_high, L * NS + T_AT[name] + 1)
                return wps[:, T_AT[name] % A_SPLIT]

            def low_of(name):
                pe.wait_ge(p_low, L * NS + T_AT[name] + 1)

            def features(pool, g, name, rows, cols=S):
                w = high_of(name).rearrange("p c (k n) -> p c k n", k=DK)
                low_of(name)
                pe.wait_ge(pool.free, pool.reusable(0, g))
                out = ps[:, pool.bank(g), 0:cols]
                for k in range(DK):
                    for a, b in PRODUCTS:
                        m = mm(out, w[:, a, k, :], rows[:, b, k, :], k == 0 and a + b == 0, k == DK - 1 and a == 1)
                m.then_inc(pool.full, 1)

            def by_token(g, rows, t):
                pe.wait_ge(BA.free, BA.reusable(0, g))
                for k in range(DK):
                    w = wps[:, T_AT[f"v{k // 4}"] % A_SPLIT].rearrange("p c (k n) -> p c k n", k=4)
                    for a, b in PRODUCTS:
                        m = mm(ps[:, BA.bank(g), 0:256], rows[:, b, k, t * P:(t + 1) * P], w[:, a, k % 4, :],
                               k == 0 and a + b == 0, k == DK - 1 and a == 1)
                m.then_inc(BA.full, 1)

            def group(pool, g, pairs, out=None, cols=S):
                pe.wait_ge(pool.free, pool.reusable(0, g))
                out = ps[:, pool.bank(g), 0:cols] if out is None else out
                for j, (a, b) in enumerate(pairs):
                    m = mm(out, a, b, j == 0, j == len(pairs) - 1)
                m.then_inc(pool.full, 1)

            def sums(pool, g, first, n, free_n=True, cols=S):
                pe.wait_ge(pool.free, pool.reusable(0, g))
                for k in range(n):
                    pe.wait_ge(sq2_ready, first + k + 1)
                    m = mm(ps[:, pool.bank(g), 0:cols], ones[:], sq2[:, (first + k) % 2, 0:cols], k == 0, k == n - 1)
                    if k < n - 2:
                        m.then_inc(sq2_free, 1)
                m.then_inc(pool.full, 1)

            pe.wait_ge(V.free, L * V.n + len(V.banks))
            pe.wait_ge(A.free, L * A.n + len(A.banks) + A.pre)
            pe.wait_ge(cond_ready, 1)

            def modulation(j):
                g = f"ar{j}"
                pe.wait_ge(BA.free, BA.reusable(0, g))
                for c in range(4):
                    w = direct(f"ada{j}.{c}")
                    for k in range(DK):
                        m = mm(ps[0:2, BA.bank(g), c * P:(c + 1) * P], cond[:, k, :], w[:, k, :], k == 0, k == DK - 1)
                    m.then_inc(BA.full if c == 3 else ada_part, 1)

            def turn_modulation(j):
                g = f"ada{j}"
                pe.wait_ge(arow_ready, j + 1)
                pe.wait_ge(BV.free, BV.reusable(0, g))
                for i in range(4):
                    m = pe.transpose(ps[:, BV.bank(g), 2 * i:2 * i + 2], arow[:, j % 2, i * P:(i + 1) * P],
                                     ident[0:2, 0:2])
                m.then_inc(BV.full, 1)

            for j in range(12):
                modulation(j)
                if j:
                    turn_modulation(j - 1)
                if j == 5:
                    sums(BA, "cnorm", 0, DK, cols=CTX)
                    sums(BA, "xnorm", DK, DK)
            turn_modulation(11)

            pe.wait_ge(cmm_ready, DK)
            for i in range(KVH):
                features(BV, f"kc{i}", f"k{i}", hcs, CTX)
            for q in range(2):
                high_of(f"v{q}")
                low_of(f"v{q}")
            for t in range(2):
                by_token(f"vc{t}", hcs, t)
            pe.wait_ge(y2_ready, DK)
            for i in range(KVH):
                features(BV, f"kx{i}", f"k{i}", ys)
            for t in range(ST):
                by_token(f"vx{t}", ys, t)
            for i, g in enumerate(("skc0", "skc1", "skx0", "skx1")):
                sums(BA, g, 2 * DK + i, 1, cols=CTX if i < 2 else S)
            for i in range(QH):
                features(BV, f"q{i}", f"q{i}", ys)
            for i in range(4):
                features(BA, f"cb{i}", f"cb{i}", ys)
            for i in range(QH):
                sums(BA, f"sq{i}", 2 * DK + 4 + i, 1)
            for i in range(4):
                features(BA, f"cc{i}", f"cc{i}", ys)
            for i in range(4):
                features(BV, f"cx{i}", f"cx{i}", ys)

            pe.wait_ge(BV.free, BV.n + len(BV.banks))
            pe.wait_ge(BA.free, BA.n + len(BA.banks))
            pe.wait_ge(qkv_done, 1)

            def scores(n):
                h, t, b = n // ST, n % ST, SCORE_BANK[n % 3]
                if n >= 3:
                    pe.wait_ge(exp_ready, n - 2)
                q = qTa[:, h, t * P:(t + 1) * P]
                mm(ps[:, b, :], q, kTa[:, h // 2, 0:S], True, True)
                mm(ps[:, b + 1, 0:CTX], q, kTa[:, h // 2, S:KEYS], True, True).then_inc(sc_full, 1)

            def turned(n):
                pe.wait_ge(prob_ready, n + 1)
                if n >= 1:
                    pe.wait_ge(pt_ready, n)
                for j in range(KT):
                    if j == 4 and n % ST == 0 and n:
                        pe.wait_ge(o_ready, n // ST)
                    m = pe.transpose(ps[:, 4 + j // 4, (j % 4) * P:(j % 4 + 1) * P],
                                     prob[:, n % 2, j * P:(j + 1) * P], ident[:])
                m.then_inc(pt_full, 1)

            scores(0)
            scores(1)
            for n in range(QH * ST):
                if n + 2 < QH * ST:
                    scores(n + 2)
                turned(n)
                if n % ST == ST - 1:
                    h = n // ST
                    pe.wait_ge(pt_ready, n + 1)
                    for j in range(KT):
                        m = mm(ps[:, 5, :], vall[:, j, (h // 2) * P:(h // 2 + 1) * P], eT[:, j, :], j == 0, j == KT - 1)
                    m.then_inc(o_full, 1)
            pe.wait_ge(o_ready, QH)
            pe.wait_ge(conv_ready, 4)
            pe.wait_ge(mixl, 16 * L + DK)
            for m_ in range(DK):
                features(CV, f"w{m_}", f"w{m_}", ys)
            sums(CA, "norm2", 2 * DK + 8, DK)

            w = direct_router()
            g = "logits"
            pe.wait_ge(CV.free, CV.reusable(0, g))
            pe.wait_ge(h2_ready, DK)
            for t in range(ST):
                for k in range(DK):
                    m = mm(ps[:, CV.bank(g), t * E_N:(t + 1) * E_N], h2T[:, k, t * P:(t + 1) * P], w[:, k, :],
                           k == 0, k == DK - 1)
            m.then_inc(CV.full, 1)
            for i in range(8):
                g, t = f"t{i}", i // 2
                pe.wait_ge(CA.free, CA.reusable(0, g))
                for j in range(4):
                    m = pe.transpose(ps[:, CA.bank(g), j * P:(j + 1) * P],
                                     h2T[:, 4 * (i % 2) + j, t * P:(t + 1) * P], ident[:])
                m.then_inc(CA.full, 1)
            g = "pos"
            pe.wait_ge(chosen_ready, 1)
            pe.wait_ge(CV.free, CV.reusable(0, g))
            for t in range(ST + 1):
                for t2 in range(min(t + 1, ST)):
                    lhs = before[:] if t2 == t else ones[:]
                    m = mm(ps[:, CV.bank(g), t * E_N:(t + 1) * E_N], lhs, chosen[:, t2, :], t2 == 0, t2 == min(t, ST - 1))
            m.then_inc(CV.full, 1)
            g = "lists"
            pe.wait_ge(CV.free, CV.reusable(0, g))
            for t in range(ST):
                pe.wait_ge(onehot_ready, t + 1)
                for k in range(TOP):
                    m = mm(ps[:, CV.bank(g), 0:3 * LISTS], place[:, t % 2, k, :],
                           owner[:, t % 2, k].rearrange("p c b -> p (c b)"), t + k == 0, t + k == ST + TOP - 2)
                m.then_inc(onehot_used if t < ST - 1 else CV.full, 1)
            experts_pe(pe, mm)

        def tail_act(act, squares, root):
            sk = dict(rd=sq2_ready, fr=sq2_free)

            def copy(out, pool, g, cols=S):
                act.wait_ge(pool.full, pool.done(0, g))
                nc.scalar.activation(out, ps[:, pool.bank(g), 0:cols], ACT.Copy).then_inc(pool.free, 1)

            def root2(pool, g, i, width, cols=S):
                root(pool, g, 0, i, width, std2, cols=cols, ready=std2_ready, free=std2_free)
                act.drain().then_inc(pool.free, 1)

            def rows(j):
                act.wait_ge(BA.full, BA.done(0, f"ar{j}"))
                if j >= 2:
                    act.wait_ge(BV.full, BV.done(0, f"ada{j - 2}"))
                nc.scalar.activation(arow[:, j % 2, :], ps[0:2, BA.bank(f"ar{j}"), :], ACT.Copy).then_inc(arow_ready, 1)
                act.drain().then_inc(BA.free, 1)

            ahead_of = Ahead(A_SPLIT)

            def ahead(n):
                for i in ahead_of.up_to(n + A_SPLIT, len(T_SPLIT)):
                    act.wait_ge(*last_use(0, TAIL[T_SPLIT[i - A_SPLIT]]))
                    act.wait_ge(*landed(L, T_SPLIT[i]))
                    nc.scalar.activation(wps[:, i % A_SPLIT, 0], pieces[:, T_SPLIT[i] % A_RAW, :],
                                         ACT.Copy).then_inc(p_high, 1)

            def mixed_high(k):
                nc.scalar.activation(ys[:, 0, k, :], mix[:, 8 + k, :], ACT.Copy).then_inc(mixh, 1)

            root(A, "next", L - 1, 0, D, std2, ready=std2_ready, free=std2_free, per=0)
            act.drain().then_inc(A.free, 1)
            for i in range(1, A_SPLIT):
                act.wait_ge(*landed(L, i))
                nc.scalar.activation(wps[:, i, 0], pieces[:, i % A_RAW, :], ACT.Copy).then_inc(p_high, 1)
            for j in range(6):
                rows(j)
            act.wait_ge(c_in, 16)
            squares(0, DK, lambda k: ctxT[:, k, :], c_in, lambda k: 16, sq2, cols=CTX, free_at=0, **sk)
            root2(BA, "cnorm", 1, D, cols=CTX)
            squares(DK, DK, lambda k: hT[:, k, :], f_ready, lambda k: k + 1, sq2, free_at=DK - 2, **sk)
            root2(BA, "xnorm", 2, D)
            for j in range(6, 12):
                rows(j)

            def shift(tile, k, row, who, ready, at, out, dst=None):
                act.wait_ge(ready, at)
                nc.scalar.activation(tile if dst is None else dst, tile, ACT.Identity,
                                     bias=ada[:, row + k, who:who + 1]).then_inc(out, 1)

            for k in range(DK):
                shift(ctxT[:, k, :], k, SH1, 1, cm_ready, k + 1, ch_ready, hcs[:, 0, k, :])
            for k in range(DK):
                shift(tmp2[:, k % 4, :], k, SH1, 0, fm_ready, k + 1, y2h_ready, ys[:, 0, k, :])

            def head_square(i, pool, g, cols=S):
                squares(2 * DK + i, 1, lambda k: ps[:, pool.bank(g), 0:cols], pool.full, lambda k: pool.done(0, g),
                        sq2, cols=cols, **sk)

            head_square(0, BV, "kc0", CTX)
            head_square(1, BV, "kc1", CTX)
            for t in range(2):
                copy(vall[:, ST + t, :], BA, f"vc{t}", 256)
            ahead(1)
            for t in range(ST):
                copy(vall[:, t, :], BA, f"vx{t}", 256)
            ahead(3)
            root2(BA, "skc0", 3, P, cols=CTX)
            head_square(2, BV, "kx0")
            root2(BA, "skc1", 4, P, cols=CTX)
            head_square(3, BV, "kx1")
            root2(BA, "skx0", 5, P)
            root2(BA, "skx1", 6, P)
            ahead(T_AT["q0"])
            head_square(4, BV, "q0")
            ahead(T_AT["q1"])
            head_square(5, BV, "q1")
            ahead(T_AT["q3"])
            for i in range(4):
                ahead(T_AT[f"cb{i}"])
                copy(mix[:, 12 + i, :], BA, f"cb{i}")
            act.drain().then_inc(cb_ready, 1)
            for i in range(QH):
                root2(BA, f"sq{i}", 7 + i, P)
                if i < 2:
                    head_square(6 + i, BV, f"q{2 + i}")
            for i in range(4):
                ahead(T_AT[f"cc{i}"])
                copy(ccb[:, i, :], BA, f"cc{i}")
            act.drain().then_inc(cc_ready, 1)
            ahead(T_AT["cx3"])
            for k in range(4):
                act.wait_ge(conv_ready, k + 1)
                mixed_high(4 + k)

            for n in range(QH * ST):
                act.wait_ge(max_ready, n + 1)
                if n >= 2:
                    act.wait_ge(pt_full, n - 1)
                b, c = SCORE_BANK[n % 3], 16 + n % 3
                s_ = ps[:, b:b + 2, :].rearrange("p a b -> p (a b)")[:, 0:KEYS]
                nc.scalar.activation(prob[:, n % 2, :], s_, ACT.Exp, bias=small[:, c:c + 1],
                                     scale=ATT_SCALE, accum_out=small[:, c + 3:c + 4]).then_inc(exp_ready, 1)
                if n >= 1:
                    turned_copy(act, n - 1)
                if n > ST and n % ST == 2:
                    act.wait_ge(o_ready, n // ST)
                    mixed_high(n // ST - 1)
            turned_copy(act, QH * ST - 1)
            act.wait_ge(o_ready, QH)
            mixed_high(QH - 1)
            ahead(T_AT["w3"])

            squares(2 * DK + 8, DK, lambda k: hT[:, k, :], h3_ready, lambda k: k + 1, sq2, free_at=2 * (DK - 2), **sk)
            root2(CA, "norm2", 11, D)
            for k in range(DK):
                shift(h2T[:, k, :], k, SH2, 0, n2_scaled, k + 1, h2_ready)
            bias_act(act)
            for i in range(8):
                t = i // 2
                copy(h2n[:, t, (i % 2) * S:(i % 2 + 1) * S], CA, f"t{i}")
                if i % 2:
                    act.drain().then_inc(h2n_ready, 1)
            act.wait_ge(gate_d, 1)
            nc.scalar.activation(gates, gates, ACT.Exp).then_inc(gate_exp, 1)
            experts_act(act)

        def turned_copy(act, n):
            act.wait_ge(pt_full, n + 1)
            t = n % ST
            src = ps[:, 4:6, :].rearrange("p a b -> p (a b)")[:, 0:KEYS].rearrange("p (j q) -> p j q", j=KT)
            nc.scalar.activation(eT[:, :, t * P:(t + 1) * P], src, ACT.Copy).then_inc(pt_ready, 1)

        def tail_dve(dve, inverse, rope):
            def full(pool, g, cols=S):
                dve.wait_ge(pool.full, pool.done(0, g))
                return ps[:, pool.bank(g), 0:cols]

            dve.sem_inc(BV.free, len(BV.banks))
            dve.sem_inc(BA.free, len(BA.banks))
            dve.sem_inc(std2_free, 2)

            def modulation(j):
                x = full(BV, f"ada{j}")[:, 0:8].rearrange("p (m c) -> p m c", m=4)
                b = q_(par2, "b_ada", 4 * j, 4).unsqueeze(2).to_broadcast([P, 4, 2])
                nc.vector.tensor_tensor(ada[:, 4 * j:4 * j + 4, :], x, b, ALU.add).then_inc(BV.free, 1)

            r = inverse(0, std2_ready, 1, std2)
            for k in range(DK):
                nc.vector.scalar_tensor_tensor(hT[:, k, :], hT[:, k, :], q_(par2, "final_norm", k), r, ALU.mult,
                                               ALU.mult).then_inc(f_ready, 1)
            dve.drain().then_inc(std2_free, 1)
            for j in range(6):
                modulation(j)
            rc = inverse(1, std2_ready, 2, std2, cols=CTX)
            rx = inverse(2, std2_ready, 3, std2)
            for j in range(6, 12):
                modulation(j)
            dve.drain()
            for i, (sc, who, gn) in enumerate(((SC1, 0, "g_norm1"), (SC1, 1, "g_norm1"), (SC2, 0, "g_norm2"))):
                nc.vector.scalar_tensor_tensor(coef[:, i, :], ada[:, sc:sc + DK, who], 1.0, q_(par2, gn, 0, DK),
                                               ALU.add, ALU.mult)
            dve.drain()
            for k in range(DK):
                nc.vector.scalar_tensor_tensor(ctxT[:, k, :], ctxT[:, k, :], coef[:, 1, k:k + 1], rc, ALU.mult,
                                               ALU.mult).then_inc(cm_ready, 1)
            dve.drain().then_inc(std2_free, 1)
            for k in range(DK):
                dve.wait_ge(ch_ready, k + 1)
                nc.vector.scalar_tensor_tensor(hcs[:, 1, k, :], ctxT[:, k, :], ada[:, SH1 + k, 1:2],
                                               hcs[:, 0, k, :].bitcast(F32), ALU.add, ALU.subtract).then_inc(cmm_ready, 1)

            def shifted_low(k):
                dve.wait_ge(y2h_ready, k + 1)
                nc.vector.scalar_tensor_tensor(ys[:, 1, k, :], tmp2[:, k % 4, :], ada[:, SH1 + k, 0:1],
                                               ys[:, 0, k, :].bitcast(F32), ALU.add, ALU.subtract).then_inc(y2_ready, 1)

            for k in range(DK):
                if k >= 2:
                    shifted_low(k - 2)
                dve.drain()
                nc.vector.scalar_tensor_tensor(tmp2[:, k % 4, :], hT[:, k, :], coef[:, 0, k:k + 1], rx, ALU.mult,
                                               ALU.mult).then_inc(fm_ready, 1)
            dve.drain().then_inc(std2_free, 1)
            for k in range(DK - 2, DK):
                shifted_low(k)
            dve.drain()

            quads = [((a, a + 32), (b, b + 32)) for a, b in ((0, 32), (32, 0), (64, 96), (96, 64))]

            def head(i, g, gain, out, cols, rotate):
                x = full(BV, g, cols)
                r = inverse(3 + i, std2_ready, 3 + i + 1, std2, cols=cols)
                dst = tmp2[:, 0, :] if rotate else out
                nc.vector.scalar_tensor_tensor(dst, x, q_(par2, gain), r, ALU.mult, ALU.mult)
                dve.drain().then_inc(BV.free, 1)
                dve.sem_inc(std2_free, 1)
                if rotate:
                    rope(tmp2[:, 0, :], out, tmp2[:, 1, :], acos, asin, quads)
                    dve.drain()

            dve.wait_ge(late_in, 32)
            head(0, "kc0", "g_k", kTa[:, 0, S:KEYS], CTX, False)
            head(1, "kc1", "g_k", kTa[:, 1, S:KEYS], CTX, False)
            head(2, "kx0", "g_k", kTa[:, 0, 0:S], S, True)
            head(3, "kx1", "g_k", kTa[:, 1, 0:S], S, True)
            for i in range(QH):
                head(4 + i, f"q{i}", "g_q", qTa[:, i, :], S, True)
            dve.drain().then_inc(qkv_done, 1)

            nc.vector.memset(ubuf, 0.0)
            dve.wait_ge(cb_ready, 1)
            dve.wait_ge(cc_ready, 1)
            for i in range(4):
                x = full(BV, f"cx{i}")
                dve.drain()
                nc.vector.tensor_tensor(ubuf[:, 1:1 + S], x, ccb[:, i, :], ALU.mult)
                dve.drain().then_inc(BV.free, 1)
                t = tmp2[:, i % 2, :]
                nc.vector.tensor_scalar(t, ubuf[:, 0:S], q_(par2, "w_conv", i), None, ALU.mult)
                for w in (1, 2):
                    dve.drain()
                    nc.vector.scalar_tensor_tensor(t, ubuf[:, w:w + S], q_(par2, "w_conv", 4 * w + i), t, ALU.mult,
                                                   ALU.add)
                dve.drain()
                nc.vector.tensor_tensor(mix[:, 12 + i, :], mix[:, 12 + i, :], t, ALU.mult).then_inc(conv_ready, 1)

            def rows_max(n):
                b, c = SCORE_BANK[n % 3], 16 + n % 3
                dve.wait_ge(sc_full, n + 1)
                s_ = ps[:, b:b + 2, :].rearrange("p a b -> p (a b)")[:, 0:KEYS]
                nc.vector.reduce_max(small[:, c + 6:c + 7], s_, AX.X)
                dve.drain()
                nc.vector.tensor_scalar(small[:, c:c + 1], small[:, c + 6:c + 7], -ATT_SCALE, None,
                                        ALU.mult).then_inc(max_ready, 1)

            rows_max(0)
            rows_max(1)
            for n in range(QH * ST):
                dve.wait_ge(exp_ready, n + 1)
                nc.vector.reciprocal(small[:, 25:26], small[:, 19 + n % 3:20 + n % 3])
                dve.drain()
                nc.vector.tensor_scalar(prob[:, n % 2, :], prob[:, n % 2, :], small[:, 25:26], None,
                                        ALU.mult).then_inc(prob_ready, 1)
                dve.drain()
                if n + 2 < QH * ST:
                    rows_max(n + 2)
                if n % ST == ST - 1:
                    h = n // ST
                    dve.wait_ge(o_full, h + 1)
                    nc.vector.tensor_copy(mix[:, 8 + h, :], ps[:, 5, :]).then_inc(o_ready, 1)

            dve.sem_inc(CV.free, len(CV.banks))
            dve.sem_inc(CA.free, len(CA.banks))
            for m in range(DK):
                nc.vector.scalar_tensor_tensor(hT[:, m, :], full(CV, f"w{m}"), ada[:, GT1 + m, 0:1], hT[:, m, :],
                                               ALU.mult, ALU.add).then_inc(h3_ready, 1)
                dve.drain().then_inc(CV.free, 1)
            r = inverse(11, std2_ready, 12, std2)
            for k in range(DK):
                nc.vector.scalar_tensor_tensor(h2T[:, k, :], hT[:, k, :], coef[:, 2, k:k + 1], r, ALU.mult,
                                               ALU.mult).then_inc(n2_scaled, 1)
            dve.drain()

            x = full(CV, "logits")[:, 0:ST * E_N].rearrange("p (t e) -> p t e", t=ST)
            nc.vector.tensor_tensor(logits, x, brt[:].unsqueeze(1).to_broadcast([P, ST, E_N]), ALU.add)
            dve.drain().then_inc(CV.free, 1)
            for t in range(ST):
                nc.vector.max(mx8[:, t, :], logits[:, t, :])
            dve.drain()
            for t in range(ST):
                nc.vector.max_index(ix8[:, t, :].bitcast(U32), mx8[:, t, :], logits[:, t, :])
                nc.vector.tensor_scalar(gates[:, t, :], mx8[:, t, 0:TOP], mx8[:, t, 0:1], None, ALU.subtract)
            dve.drain().then_inc(gate_d, 1)
            nc.vector.tensor_copy(ixf, ix8.bitcast(U32))
            dve.drain()
            nc.vector.tensor_tensor(hot.rearrange("p (t k) e -> p t k e", k=TOP),
                                    cst[:, 0:E_N].unsqueeze(1).unsqueeze(1).to_broadcast([P, ST, TOP, E_N]),
                                    ixf[:, :, 0:TOP].unsqueeze(3).to_broadcast([P, ST, TOP, E_N]), ALU.is_equal)
            dve.drain()
            hk = hot.rearrange("p (t k) e -> p t k e", k=TOP)
            nc.vector.tensor_tensor(chosen, hk[:, :, 0, :], hk[:, :, 1, :], ALU.add)
            for k in (2, 3):
                dve.drain()
                nc.vector.tensor_tensor(chosen, chosen, hk[:, :, k, :], ALU.add)
            dve.drain().then_inc(chosen_ready, 1)
            x = full(CV, "pos")
            nc.vector.tensor_copy(posn, x[:, 0:ST * E_N].rearrange("p (t e) -> p t e", t=ST))
            count = x[:, ST * E_N:(ST + 1) * E_N]
            nc.vector.tensor_scalar(nblk, count, 0.0, None, ALU.is_gt)
            nc.vector.memset(zer, 0.0)
            for t in range(1, ST):
                dve.drain()
                nc.vector.scalar_tensor_tensor(nblk, count, float(t * P), nblk, ALU.is_gt, ALU.add)
            dve.drain().then_inc(CV.free, 1)
            nc.vector.tensor_tensor_scan(pend, nblk, zer, 0.0, ALU.add, ALU.add)
            dve.drain()
            nc.vector.tensor_tensor(pbase, pend, nblk, ALU.subtract)
            nc.vector.tensor_scalar(pend128, pend, float(P), None, ALU.mult)
            nc.vector.tensor_scalar(hot2n, cst[:, C_EVEN:C_EVEN + 24], pend[:, E_N - 1:E_N], None, ALU.is_lt)
            dve.drain()
            nc.vector.reduce_sum(npI, hot2n, AX.X)
            nc.vector.tensor_scalar(pbase, pbase, float(P), None, ALU.mult)
            dve.drain()
            parts = ((0, E_N, h_sb[:]), (E_N, LISTS, flat))
            for b0, b1, buf in parts:
                n = b1 - b0
                nc.vector.tensor_tensor(buf[:, 0:n * E_N].rearrange("p (b e) -> p b e", e=E_N),
                                        pend128.unsqueeze(1).to_broadcast([P, n, E_N]),
                                        cst[:, C_EDGE + b0:C_EDGE + b1].unsqueeze(2).to_broadcast([P, n, E_N]), ALU.is_le)
            dve.drain()
            for b0, b1, buf in parts:
                nc.vector.reduce_sum(be_bc[:, b0:b1], buf[:, 0:(b1 - b0) * E_N].rearrange("p (b e) -> p b e", e=E_N), AX.X)
            dve.drain()
            nc.vector.tensor_scalar(be_bc[:], be_bc[:], float(E_N - 1), None, ALU.min)
            dve.drain()
            nc.vector.tensor_copy(be_r[:], be_bc[0:1, :]).then_inc(be_ready, 1)
            nc.vector.tensor_copy(np_i[:], npI[0:1, :]).then_inc(np_ready, 1)
            dve.sem_inc(low_v, len(DVE_LOW))
            nc.vector.tensor_tensor(posn, posn, pbase.unsqueeze(1).to_broadcast([P, ST, E_N]), ALU.add)
            dve.drain()
            h2k = hot2.rearrange("p (t k) e -> p t k e", k=TOP)
            nc.vector.tensor_tensor(h2k, hk, posn.unsqueeze(2).to_broadcast([P, ST, TOP, E_N]), ALU.mult)
            dve.drain()
            nc.vector.reduce_sum(slotf, hot2, AX.X)
            dve.wait_ge(gate_exp, 1)
            nc.vector.reduce_sum(gsum, gates, AX.X)
            dve.drain()
            nc.vector.reciprocal(gsum, gsum)
            dve.drain()
            nc.vector.tensor_tensor(gates, gates, gsum.unsqueeze(2).to_broadcast([P, ST, TOP]), ALU.mult)
            dve.drain()
            token = cst[:, C_TOKEN:C_END].rearrange("p (t k) -> p t k", k=TOP)
            edges = cst[:, C_EDGE:C_NEG].unsqueeze(1).to_broadcast([P, TOP, LISTS + 1])
            for t in range(ST):
                slot, own = slotf[:, t * TOP:(t + 1) * TOP], owner[:, t % 2]
                wide = lambda v: v.unsqueeze(2).to_broadcast([P, TOP, LISTS])
                nc.vector.tensor_tensor(reached, edges, slot.unsqueeze(2).to_broadcast([P, TOP, LISTS + 1]), ALU.is_le)
                if t >= 2:
                    dve.wait_ge(onehot_used, t - 1)
                dve.drain()
                nc.vector.reduce_sum(first_past, reached, AX.X)
                nc.vector.tensor_tensor(own[:, :, 0, :], reached[:, :, 0:LISTS], reached[:, :, 1:LISTS + 1], ALU.subtract)
                dve.drain()
                nc.vector.scalar_tensor_tensor(rem, first_past, -float(P), slot, ALU.mult, ALU.add)
                nc.vector.tensor_tensor(own[:, :, 1, :], own[:, :, 0, :], wide(token[:, t, :]), ALU.mult)
                nc.vector.tensor_tensor(own[:, :, 2, :], own[:, :, 0, :], wide(gates[:, t, :]), ALU.mult)
                dve.drain()
                nc.vector.tensor_tensor(place[:, t % 2], cst[:, C_NEG:C_TOKEN].unsqueeze(1).to_broadcast([P, TOP, P]),
                                        rem.unsqueeze(2).to_broadcast([P, TOP, P]), ALU.is_equal)
                dve.drain().then_inc(onehot_ready, 1)
            x = full(CV, "lists")[:, 0:3 * LISTS].rearrange("p (c b) -> p c b", c=3)
            nc.vector.tensor_scalar(empty, x[:, 0, :], -1.0, 1.0, ALU.mult, ALU.add)
            nc.vector.tensor_copy(list_gate[:], x[:, 2, :])
            dve.drain()
            nc.vector.scalar_tensor_tensor(list_tok[:], empty, q_(par2, "dump"), x[:, 1, :], ALU.mult, ALU.add)
            dve.drain().then_inc(list_ready, 1)
            dve.sem_inc(CV.free, 1)
            experts_dve(dve)

        raw_in = [sem(f"half_in{j}") for j in range(RAW)]
        bias_in, bias_high, bias_split = (sem(n) for n in ("bias_in", "bias_high", "bias_split"))
        lst_ready, xg_in = sem("slots_ready"), sem("rows_in")
        high = sem("high_ready")
        used = sem("half_used")
        t_full, t_high, t_out = sem("t_full"), sem("t_high"), sem("t_out")
        sel_ready = sem("sel_ready")
        glu_ready, th2_ready, act_ready = sem("glu_ready"), sem("tanh_ready"), sem("act_ready")
        ye_ready, scattered, y_free = sem("ye_ready"), sem("scattered"), sem("y_free")
        acc_in, fin_ready, out_done, z_ready = sem("acc_in"), sem("fin_ready"), sem("out_done"), sem("z_ready")
        sq3_ready, std3_ready = sem("sq3_ready"), sem("std3_ready")

        def block_pairs(eng):
            eng.wait_ge(np_ready, 1)
            return eng.value_load(np_i[0:1, 0:1], min_val=1, max_val=BLOCKS // 2)

        def low_done(b, h):
            s_, own = (low_p, POOL_LOW) if h in POOL_LOW else (low_v, DVE_LOW)
            return s_, len(own) * (b + 1) + own.index(h) + 1

        def raw_landed(b, h):
            return raw_in[h % RAW], 16 * (2 * b + h // RAW + 1)

        def bias_sp(sp):
            sp.wait_ge(CV.full, CV.done(0, "w7"))
            for i in range(2):
                sp.dma_start(b_raw[i * E_N:(i + 1) * E_N, :], io["b_moe"]).then_inc(bias_in, 16)

        def bias_act(act):
            act.wait_ge(bias_in, 32)
            nc.scalar.activation(b_split[:], b_raw, ACT.Copy).then_inc(bias_high, 1)

        def bias_pool(pool):
            pool.wait_ge(bias_high, 1)
            nc.gpsimd.tensor_tensor(b_split[E_N:2 * E_N, :], b_raw[E_N:2 * E_N, :],
                                    b_split[E_N:2 * E_N, :].bitcast(F32), ALU.subtract).then_inc(bias_split, 1)
            pool.drain()
            nc.gpsimd.memset(xgy[:], 0.0)
            pool.drain()

        def experts_sp(sp):
            sp.wait_ge(be_ready, 1)
            n = block_pairs(sp)
            sp.wait_ge(CV.full, CV.done(0, "pos"))
            sp.wait_ge(CA.full, CA.n)

            def load(b, hs):
                e = sp.value_load(be_r[0:1, bass.ds(b, 1)], min_val=0, max_val=E_N - 1)
                for h in hs:
                    j, q = ORDER[h]
                    before_, hb = (b - 1, h + RAW) if h < RAW else (b, h - RAW)
                    sp.wait_ge(*low_done(before_, hb))
                    sp.dma_start(raw[:, h % RAW, :].unsqueeze(1),
                                 io["w_moe"][bass.ds(6 * e + j, 1), :, q * HALF:(q + 1) * HALF]
                                 .rearrange("a p n -> p a n")).then_inc(raw_in[h % RAW], 16)

            with sp.Fori(0, n) as i:
                for s in range(2):
                    load(2 * i + s, range(HALVES))
            load(2 * n, range(SPLIT))
            final_sp(sp, n)

        def experts_pe(pe, mm):
            n = block_pairs(pe)
            pe.wait_ge(CA.free, CA.n + len(CA.banks))
            pe.wait_ge(CV.free, CV.n + len(CV.banks))

            def turn(src, bank):
                for j in range(4):
                    m = pe.transpose(ps[:, bank, j * P:(j + 1) * P], src[:, j * P:(j + 1) * P], ident[:])
                m.then_inc(t_full, 1)

            def half(b, s, h):
                j, q = ORDER[h]
                rows = xgT[:, s] if j < 4 else hTe[:]
                w = wsp[:, h % SPLIT]
                if q == 0:
                    mm(ps[:, j, :], sel[:, s, :], b_split[:, j * S:(j + 1) * S], True, False)
                pe.wait_ge(high, HALVES * b + h + 1)
                for k in range(4):
                    at_ = (4 * q + k) * P
                    for part in range(2):
                        mm(ps[:, j, :], rows[:, part, at_:at_ + P], w[:, 0, k * S:(k + 1) * S], False, False)
                pe.wait_ge(*low_done(b, h))
                for k in range(4):
                    at_ = (4 * q + k) * P
                    m = mm(ps[:, j, :], rows[:, 0, at_:at_ + P], w[:, 1, k * S:(k + 1) * S], False,
                           q == 1 and k == 3)
                m.then_inc(used, 1)

            pe.wait_ge(bias_split, 1)
            pe.wait_ge(xg_in, 16)
            turn(xg[:, 0, 0:S], 6)
            turn(xg[:, 0, S:D], 7)
            with pe.Fori(0, n) as i:
                for s in range(2):
                    b = 2 * i + s
                    pe.wait_ge(sel_ready, b + 1)
                    pe.wait_ge(t_out, 4 * b + 1)
                    half(b, s, 0)
                    pe.wait_ge(t_out, 4 * b + 2)
                    for h in range(1, 6):
                        half(b, s, h)
                    pe.wait_ge(act_ready, 2 * b + 1)
                    turn(h_sb[:, 0:S], 6)
                    half(b, s, 6)
                    half(b, s, 7)
                    pe.wait_ge(ye_ready, 2 * b + 2)
                    pe.wait_ge(t_out, 4 * b + 3)
                    half(b, s, 8)
                    pe.wait_ge(act_ready, 2 * b + 2)
                    turn(h_sb[:, S:D], 7)
                    half(b, s, 9)
                    pe.wait_ge(xg_in, 16 * b + 32)
                    turn(xg[:, 1 - s, 0:S], 6)
                    pe.wait_ge(t_out, 4 * b + 4)
                    half(b, s, 10)
                    turn(xg[:, 1 - s, S:D], 7)
                    half(b, s, 11)
            final_pe(pe, mm)

        def experts_act(act):
            n = block_pairs(act)

            def high_part(b, h):
                act.wait_ge(*raw_landed(b, h))
                nc.scalar.activation(wsp[:, h % SPLIT, 0], raw[:, h % RAW, :], ACT.Copy).then_inc(high, 1)

            def turned_high(dst, bank, at, scale=1.0):
                act.wait_ge(t_full, at)
                nc.scalar.activation(dst, ps[:, bank, :], ACT.Copy, scale=scale).then_inc(t_high, 1)

            act.wait_ge(CA.full, CA.n)
            act.wait_ge(CV.full, CV.done(0, "pos"))
            for h in range(SPLIT - 1):
                high_part(0, h)
            turned_high(xgT[:, 0, 0, 0:S], 6, 1)
            turned_high(xgT[:, 0, 0, S:D], 7, 2)
            high_part(0, SPLIT - 1)
            with act.Fori(0, n) as i:
                for s in range(2):
                    b = 2 * i + s
                    for h in range(HALVES):
                        act.wait_ge(used, HALVES * b + h + 1)
                        if h in (2, 6):
                            act.wait_ge(glu_ready, 2 * b + 1 + h // 6)
                            nc.scalar.activation(thb, glu, ACT.Tanh, scale=ALPHA / 2).then_inc(th2_ready, 1)
                        if h == 5:
                            turned_high(hTe[:, 0, 0:S], 6, 4 * b + 3, 0.5)
                        if h == 8:
                            turned_high(hTe[:, 0, S:D], 7, 4 * b + 4, 0.5)
                        if h == 9:
                            turned_high(xgT[:, 1 - s, 0, 0:S], 6, 4 * b + 5)
                        if h == 10:
                            turned_high(xgT[:, 1 - s, 0, S:D], 7, 4 * b + 6)
                        high_part(b + (h + SPLIT) // HALVES, (h + SPLIT) % HALVES)
            final_act(act)

        def low_part(eng, e, b, h):
            eng.wait_ge(high, HALVES * b + h + 1)
            e.tensor_tensor(wsp[:, h % SPLIT, 1], raw[:, h % RAW, :], wsp[:, h % SPLIT, 0].bitcast(F32),
                            ALU.subtract).then_inc(low_p if h in POOL_LOW else low_v, 1)

        def experts_dve(dve):
            n = block_pairs(dve)
            dve.sem_inc(ye_ready, 2)
            dve.sem_inc(y_free, 1)

            def turned_low(dst, high_, bank, at, scale=1.0):
                dve.wait_ge(t_high, at)
                nc.vector.scalar_tensor_tensor(dst, ps[:, bank, :], scale, high_.bitcast(F32), ALU.mult,
                                               ALU.subtract).then_inc(t_out, 1)

            def select(b, s):
                nc.vector.tensor_scalar(sel[:, s, :], be_bc[0:2 * E_N, bass.ds(b, 1)].to_broadcast([2 * E_N, P]),
                                        q_(par2, "part32")[0:2 * E_N], None, ALU.is_equal).then_inc(sel_ready, 1)

            select(0, 0)
            low_part(dve, nc.vector, 0, 0)
            low_part(dve, nc.vector, 0, 1)
            turned_low(xgT[:, 0, 1, 0:S], xgT[:, 0, 0, 0:S], 6, 1)
            turned_low(xgT[:, 0, 1, S:D], xgT[:, 0, 0, S:D], 7, 2)
            low_part(dve, nc.vector, 0, 3)
            dve.wait_ge(lst_ready, 1)
            with dve.Fori(0, n) as i:
                for s in range(2):
                    b = 2 * i + s
                    for h in range(HALVES):
                        if h in (1, 5):
                            dve.wait_ge(used, HALVES * b + h + 1)
                            nc.vector.tensor_scalar(glu, ps[:, h // 2, :], LIMIT, None, ALU.min).then_inc(glu_ready, 1)
                        if h == 5:
                            turned_low(hTe[:, 1, 0:S], hTe[:, 0, 0:S], 6, 4 * b + 3, 0.5)
                        if h in (3, 7):
                            at_ = h // 4
                            dve.wait_ge(used, HALVES * b + h + 1)
                            nc.vector.tensor_scalar(lin, ps[:, h // 2, :], LIMIT, -LIMIT, ALU.min, ALU.max)
                            dve.wait_ge(th2_ready, 2 * b + at_ + 1)
                            nc.vector.scalar_tensor_tensor(glu, thb, 1.0, glu, ALU.add, ALU.mult)
                            dve.drain()
                            nc.vector.scalar_tensor_tensor(h_sb[:, at_ * S:(at_ + 1) * S], lin, 1.0, glu, ALU.add,
                                                           ALU.mult).then_inc(act_ready, 1)
                            dve.drain()
                        if h == 8:
                            turned_low(hTe[:, 1, S:D], hTe[:, 0, S:D], 7, 4 * b + 4, 0.5)
                        if h == 9:
                            turned_low(xgT[:, 1 - s, 1, 0:S], xgT[:, 1 - s, 0, 0:S], 6, 4 * b + 5)
                            select(b + 1, 1 - s)
                        if h == 10:
                            turned_low(xgT[:, 1 - s, 1, S:D], xgT[:, 1 - s, 0, S:D], 7, 4 * b + 6)
                        if h in (10, 11):
                            dve.wait_ge(used, HALVES * b + h + 1)
                            if h == 10:
                                dve.wait_ge(y_free, b + 1)
                            at_ = h - 10
                            nc.vector.tensor_scalar(y_sb[:, s, at_ * S:(at_ + 1) * S], ps[:, 4 + at_, :],
                                                    lst[:, s, 1:2].bitcast(F32), None, ALU.mult).then_inc(ye_ready, 1)
                        ahead = (h + SPLIT) % HALVES
                        if ahead in DVE_LOW:
                            low_part(dve, nc.vector, b + (h + SPLIT) // HALVES, ahead)
            final_dve(dve)

        def experts_pool(pool):
            n = block_pairs(pool)
            pool.sem_inc(low_p, len(POOL_LOW))
            pool.wait_ge(h2_out, 16 * ST)
            pool.wait_ge(acc_init, 16 * (ACC_ROWS // P))
            pool.wait_ge(list_ready, 1)

            def fetch(b, s):
                nc.gpsimd.tensor_copy(rows_i[:, s:s + 1], list_tok[:, bass.ds(b, 1)])
                pool.drain()
                nc.gpsimd.indirect_dma_start(out=xg[:, s, :], out_offset=None, in_=h2_dram[:, :],
                                             in_offset=bass.IndirectOffsetOnAxis(ap=rows_i[:, s:s + 1].bitcast(U32), axis=0),
                                             bounds_check=S - 1, oob_is_err=False).then_inc(xg_in, 16)

            def take_list(b, s):
                nc.gpsimd.tensor_copy(lst[:, s, 0:1], list_tok[:, bass.ds(b, 1)])
                nc.gpsimd.tensor_copy(lst[:, s, 1:2].bitcast(F32), list_gate[:, bass.ds(b, 1)])
                pool.drain()

            def add_rows(s, at):
                pool.wait_ge(ye_ready, at)
                pool.sem_inc(pool_turns, 1)
                nc.gpsimd.indirect_dma_start(out=acc_dram[:, :],
                                             out_offset=bass.IndirectOffsetOnAxis(ap=lst[:, s, 0:1].bitcast(U32), axis=0),
                                             in_=y_sb[:, s, :], in_offset=None, compute_op=ALU.add).then_inc(scattered, 16)

            fetch(0, 0)
            low_part(pool, nc.gpsimd, 0, 2)
            take_list(0, 0)
            take_list(BLOCKS, 1)
            pool.sem_inc(lst_ready, 1)
            with pool.Fori(0, n) as i:
                for s in range(2):
                    b = 2 * i + s
                    pool.wait_ge(t_out, 4 * b + 2)
                    pool.sem_inc(pool_turns, 1)
                    fetch(b + 1, 1 - s)
                    add_rows(1 - s, 2 * b + 2)
                    low_part(pool, nc.gpsimd, b, 6)
                    pool.wait_ge(scattered, 16 * b + 16)
                    pool.sem_inc(pool_turns, 1)
                    take_list(b + 1, 1 - s)
                    pool.sem_inc(y_free, 1)
                    low_part(pool, nc.gpsimd, b, 10)
                    low_part(pool, nc.gpsimd, b + 1, 2)
            add_rows(1, 4 * n + 2)
            pool.wait_ge(scattered, 32 * n + 16)
            pool.wait_ge(xg_in, 32 * n + 16)
            pool.sem_inc(z_ready, 1)

        accn = mix[:, 0:DK, :].rearrange("p a b -> p (a b)").rearrange("p (t n) -> p t n", t=ST)

        def final_sp(sp, n):
            sp.wait_ge(z_ready, 1)
            sp.wait_ge(low_v, len(DVE_LOW) * (2 * n + 1) + 3)
            sp.wait_ge(low_p, len(POOL_LOW) * (2 * n + 1) + 1)
            for t in range(ST):
                sp.dma_start(accn[:, t, :], acc_dram[t * P:(t + 1) * P, :]).then_inc(acc_in, 16)
            for k in range(DK):
                sp.wait_ge(fin_ready, DK + k + 1)
                sp.dma_start(io["out"][k * P:(k + 1) * P, :], hT[:, k, :]).then_inc(out_done, 16)
            sp.wait_ge(out_done, 16 * DK)

        def final_pe(pe, mm):
            pe.wait_ge(acc_in, 16 * ST)
            pe.wait_ge(z_ready, 1)
            for k in range(DK):
                g = f"t{k}"
                pe.wait_ge(DV.free, DV.reusable(0, g))
                for t in range(ST):
                    m = pe.transpose(ps[:, DV.bank(g), t * P:(t + 1) * P], accn[:, t, k * P:(k + 1) * P], ident[:])
                m.then_inc(DV.full, 1)
            for k in range(DK):
                pe.wait_ge(sq3_ready, k + 1)
                m = mm(ps[:, 6, :], ones[:], xg_flat[:, k * S:(k + 1) * S], k == 0, k == DK - 1)
            m.then_inc(sq3_ready, 1)

        def final_act(act):
            act.drain()
            for k in range(DK):
                act.wait_ge(fin_ready, k + 1)
                nc.scalar.activation(xg_flat[:, k * S:(k + 1) * S], hT[:, k, :], ACT.Square).then_inc(sq3_ready, 1)
            act.wait_ge(sq3_ready, DK + 1)
            nc.scalar.activation(glu, ps[:, 6, :], ACT.Sqrt, bias=EPSC, scale=1.0 / D).then_inc(std3_ready, 1)

        def final_dve(dve):
            dve.sem_inc(DV.free, len(DV.banks))
            for k in range(DK):
                dve.wait_ge(DV.full, DV.done(0, f"t{k}"))
                nc.vector.scalar_tensor_tensor(hT[:, k, :], ps[:, DV.bank(f"t{k}"), :], ada[:, GT2 + k, 0:1],
                                               hT[:, k, :], ALU.mult, ALU.add).then_inc(fin_ready, 1)
                dve.drain().then_inc(DV.free, 1)
            dve.wait_ge(std3_ready, 1)
            nc.vector.reciprocal(glu, glu)
            dve.drain()
            for k in range(DK):
                nc.vector.scalar_tensor_tensor(hT[:, k, :], hT[:, k, :], q_(par2, "g_final", k), glu, ALU.mult,
                                               ALU.mult).then_inc(fin_ready, 1)

        xg_flat = xgy[:].rearrange("p a b -> p (a b)")

        block = ctx.enter_context(nc.Block())

        @block.sync
        def _(sp):
            for kt in range(DK):
                sp.dma_start(hT[:, kt, :], io["xT"][kt * P:(kt + 1) * P, :]).then_inc(x_in, 16)
            for n in range(A_RAW):
                sp.dma_start(pieces[:, n, :], io["pieces"][n]).then_inc(p_in[n], 16)
            with sp.Fori(0, L) as layer:
                for n in range(NP):
                    if n == L_SPLIT[L_AT["q0"]]:
                        sp.wait_ge(h_ready, (2 * layer + 1) * DK)
                        one = bass.ds(layer, 1)
                        sp.dma_start(lngb[:, 0:1, :], io["ln_g"][one].partition_broadcast(P)).then_inc(sgu_in, 16)
                        sp.dma_start(lngb[:, 1:2, :], io["ln_b"][one].partition_broadcast(P)).then_inc(sgu_in, 16)
                        sp.dma_start(bsb.unsqueeze(1), io["b_s"][one].partition_broadcast(P)).then_inc(sgu_in, 16)
                        sp.dma_start(wsT.unsqueeze(1), io["wsT"][one].rearrange("a p g n -> p a g n")).then_inc(sgu_in, 16)
                    sp.wait_ge(*piece_done(layer, n))
                    sp.dma_start(pieces[:, n % A_RAW, :].unsqueeze(1),
                                 io["pieces"][bass.ds(layer * NP + (n + A_RAW), 1)]
                                 .rearrange("a p n -> p a n")).then_inc(p_in[n % A_RAW], 16)

            tail_sp(sp)

        @block.tensor
        def _(pe):
            pe.wait_ge(const_in, 16 * N_CONST)

            def mm(out, lhsT, rhs, start, stop):
                return pe.matmul(out, lhsT, rhs, start=start, stop=stop)

            def norm_sums(pool, g, layer, first, n, ready, free, buf, cols=S, per=NSQ):
                pe.wait_ge(pool.free, pool.reusable(layer, g))
                for k in range(n):
                    pe.wait_ge(ready, layer * per + first + k + 1)
                    m = mm(ps[:, pool.bank(g), 0:cols], ones[:], buf[:, (first + k) % 2, 0:cols], k == 0, k == n - 1)
                    if k < n - 2:
                        m.then_inc(free, 1)
                m.then_inc(pool.full, 1)

            def next_sum(layer, k):
                pe.wait_ge(sq_ready, layer * NSQ + NSQ + k + 1)
                m = mm(ps[:, A.bank("next"), :], ones[:], sq[:, k % 2, :], k == 0, k == DK - 1)
                if k < DK - 2:
                    m.then_inc(sq_free, 1)
                if k == DK - 1:
                    m.then_inc(A.full, 1)

            for k in range(DK):
                next_sum(-1, k)
            with pe.Fori(0, L) as layer:
                def high_of(n):
                    pe.wait_ge(p_high, layer * NS + n + 1)
                    return wps[:, n % A_SPLIT]

                def low_of(n):
                    pe.wait_ge(p_low, layer * NS + n + 1)

                def project(pool, g, first=None):
                    n = L_AT[g]
                    w = high_of(n).rearrange("p c (k n) -> p c k n", k=DK)
                    pe.wait_ge(pool.free, pool.reusable(layer, g))
                    out = ps[:, pool.bank(g), :]
                    for k in range(DK):
                        if first is not None:
                            pe.wait_ge(yl_pool if k % 2 else y_ready, layer * DK + first // 2 + k // 2 + 1)
                        for b in range(2):
                            mm(out, w[:, 0, k, :], ys[:, b, k, :], k == 0 and b == 0, False)
                    low_of(n)
                    for k in range(DK):
                        m = mm(out, w[:, 1, k, :], ys[:, 0, k, :], False, k == DK - 1)
                    m.then_inc(pool.full, 1)

                def natural(name, piece, count, cols):
                    per = DK // count
                    for q in range(count):
                        n = L_AT[f"{piece}.{q}"]
                        w = high_of(n).rearrange("p c (k n) -> p c k n", k=per)
                        for t in range(ST):
                            if q == 0:
                                pe.wait_ge(A.free, A.reusable(layer, name(t)))
                            for k in range(per):
                                for b in range(2):
                                    mm(ps[:, A.bank(name(t)), 0:cols], ys[:, b, q * per + k, t * P:(t + 1) * P],
                                       w[:, 0, k, :], q + k + b == 0, False)
                        low_of(n)
                        for t in range(ST):
                            for k in range(per):
                                m = mm(ps[:, A.bank(name(t)), 0:cols], ys[:, 0, q * per + k, t * P:(t + 1) * P],
                                       w[:, 1, k, :], False, q == count - 1 and k == per - 1)
                            if q == count - 1:
                                m.then_inc(A.full, 1)
                            elif t == ST - 1:
                                m.then_inc(part_used, 1)

                def direct(name):
                    n = [x[0] for x in LAYER].index(name)
                    pe.wait_ge(*landed(layer, n))
                    return pieces[:, n % A_RAW, :]

                for n, (name, _, pool, g) in enumerate(LAYER[:12]):
                    project(pools[pool], g, first=0 if n == 0 else None)

                for g in range(2):
                    pe.wait_ge(xc_ready, layer * 6 + 3 * g + 3)
                    wbd = [direct(f"lru{g}.{wi}")[:, 0:7 * P].rearrange("p (n m) -> p n m", n=7) for wi in range(2)]
                    for m in range(3):
                        ks = [(n, k) for n, (k, mm_) in enumerate(PAIRS) if mm_ == m]
                        for wi, wn in enumerate(("r", "i")):
                            name = f"{wn}{3 * g + m}"
                            pe.wait_ge(A.free, A.reusable(layer, name))
                            for j, (n, k) in enumerate(ks):
                                x = mm(ps[:, A.bank(name), :], wbd[wi][:, n, :], xc[:, 3 * g + k, :],
                                       j == 0, j == len(ks) - 1)
                            x.then_inc(A.full, 1)
                    natural(lambda t: f"v{g}.{t}", f"v{g}", *((4, 512) if g == 0 else (2, 256)))
                    for j in range(2) if g == 0 else range(2, 6):
                        project(V, f"gr{j}")

                def out_sums(h):
                    norm_sums(A, f"oss{h}", layer, DK + h, 1, sq_ready, sq_free, sq)

                def scores(g):
                    pe.wait_ge(qk_ready, layer * HEADS + g + 1)
                    for c in (0, 1, 3, 2):
                        name, first = f"s{g}.{min(c, 4 - c)}", 3 * P if c == 3 else 0
                        if c != 3:
                            pe.wait_ge(V.free, V.reusable(layer, name))
                        x = mm(ps[:, V.bank(name), first:first + S - c * P],
                               qk[:, 2 * (g % 2) + 1, c * P:(c + 1) * P], qk[:, 2 * (g % 2), c * P:S], True, True)
                        if c != 1:
                            x.then_inc(V.full, 1)

                for h in range(HEADS + 1):
                    if h < HEADS:
                        project(V, f"q{h}")
                    if h >= 1:
                        scores(h - 1)
                    if h < HEADS:
                        project(V, f"k{h}")
                    if h >= 2:
                        out_sums(h - 2)
                    if h == 0:
                        pe.wait_ge(vn_ready, layer + 1)
                        continue
                    g = h - 1
                    pe.wait_ge(V.free, V.reusable(layer, f"o{g}"))
                    at_c = 0
                    for c in range(ST):
                        if c == 0:
                            pe.wait_ge(s_ready, layer * HEADS + g + 1)
                        n = S - c * P
                        x = mm(ps[:, V.bank(f"o{g}"), c * P:S], vnat[:, c, g * P:(g + 1) * P],
                               dec_s[:, at_c:at_c + n], c == 0, c == ST - 1)
                        at_c += n
                    x.then_inc(V.full, 1)
                out_sums(5)

                natural(lambda t: f"vs{t}", "vs", 4, S)
                for j in range(4):
                    project(V, f"gs{j}")
                for j in range(4):
                    project(V, f"u{j}")
                pe.wait_ge(vn2_ready, layer + 1)
                for g in range(SGU_G):
                    name = f"mx{g}"
                    pe.wait_ge(V.free, V.reusable(layer, name))
                    for c in range(ST):
                        x = mm(ps[:, V.bank(name), c * P:(c + 1) * P], vs[:, c, g * P:(g + 1) * P],
                               wsT[:, g, :], True, True)
                    x.then_inc(V.full, 1)

                w_of = [(V if m < 4 else A, f"w{m}") for m in range(DK)]
                for k in range(16):
                    n = L_AT[f"wo.{k}"]
                    w = high_of(n)
                    pe.wait_ge(mixl, layer * 16 + k + 1)
                    if k == 15:
                        low_of(n)
                    for m, (pool, g) in enumerate(w_of):
                        if k == 0:
                            pe.wait_ge(pool.free, pool.reusable(layer, g))
                        for b in range(2):
                            mm(ps[:, pool.bank(g), :], w[:, 0, m * P:(m + 1) * P], ys[:, b, k % DK, :],
                               k == 0 and b == 0, False)
                        if k == 15:
                            mm(ps[:, pool.bank(g), :], w[:, 1, m * P:(m + 1) * P], ys[:, 0, k % DK, :],
                               False, True).then_inc(pool.full, 1)
                    if k < 15:
                        low_of(n)
                        for m, (pool, g) in enumerate(w_of):
                            x = mm(ps[:, pool.bank(g), :], w[:, 1, m * P:(m + 1) * P], ys[:, 0, k % DK, :], False, False)
                        x.then_inc(part_used, 1)

                norm_sums(A, "norm2", layer, 14, DK, sq_ready, sq_free, sq)
                for m in range(DK):
                    project(A, f"g{m}", first=DK if m == 0 else None)
                pT = [direct(f"ple{k}") for k in range(2)]
                wp = [direct(f"ple{2 + k}") for k in range(2)]
                for m in range(DK):
                    g = f"p{m}"
                    pe.wait_ge(V.free, V.reusable(layer, g))
                    for k in range(2):
                        x = mm(ps[:, V.bank(g), :], wp[k][:, m * P:(m + 1) * P], pT[k][:, 0:S], k == 0, k == 1)
                    x.then_inc(V.full, 1)
                    if m == 2:
                        pe.wait_ge(A.free, A.reusable(layer, "next"))
                    if m >= 2:
                        next_sum(layer, m - 2)
                for k in range(DK - 2, DK):
                    next_sum(layer, k)
            tail_pe(pe, mm)

        @block.scalar
        def _(act):
            act.dma_start(par_all[:], io["par"]).then_inc(par_in, 16)
            act.dma_start(par2[:], io["par2"]).then_inc(par_in, 16)
            act.dma_start(tmp[:, 2, :].bitcast(I32), io["positions"].partition_broadcast(P)).then_inc(par_in, 16)
            act.wait_ge(par_in, 48)

            act.wait_ge(prep_v, 1)
            nc.scalar.activation(prep_e, prep_n, ACT.Exp).then_inc(prep_a, 1)
            act.wait_ge(prep_v, 2)
            nc.scalar.activation(prep_l, prep_w, ACT.Ln).then_inc(prep_a, 1)
            nc.scalar.activation(cond[:], q_(par2, "cond", 0, 2 * DK).rearrange("p (k c) -> p k c", k=DK), ACT.Tanh,
                                 scale=0.5).then_inc(prep_a, 1)
            act.wait_ge(prep_v, 3)
            nc.scalar.activation(rcos, tmp[:, 0, :], ACT.Sin)
            nc.scalar.activation(rsin, tmp[:, 1, :], ACT.Sin).then_inc(prep_a, 1)

            def squares(first, n, tile, ready, ready_at, buf, cols=S, free_at=0, rd=None, fr=None):
                for k in range(n):
                    act.wait_ge(ready, ready_at(k))
                    if k >= 2:
                        act.wait_ge(fr or sq_free, free_at + k - 1)
                    nc.scalar.activation(buf[:, (first + k) % 2, 0:cols], tile(k), ACT.Square).then_inc(rd or sq_ready, 1)

            def root(pool, g, layer, i, width, out, cols=S, ready=None, free=None, per=NSTD):
                act.wait_ge(pool.full, pool.done(layer, g))
                act.wait_ge(free or std_free, layer * per + i + 1)
                nc.scalar.activation(out[:, i % 2, 0:cols], ps[:, pool.bank(g), 0:cols], ACT.Sqrt,
                                     bias=EPSC, scale=1.0 / width).then_inc(ready or std_ready, 1)

            squares(0, DK, lambda k: hT[:, k, :], h_ready, lambda k: k + 1, sq)
            act.wait_ge(*landed(0, 0))
            nc.scalar.activation(wps[:, 0, 0], pieces[:, 0, :], ACT.Copy).then_inc(p_high, 1)

            with act.Fori(0, L) as layer:
                ahead_of = Ahead(A_SPLIT)

                def ahead(name):
                    for n in ahead_of.up_to(L_AT[name] + A_SPLIT, NS + A_SPLIT):
                        at_ = L_SPLIT[n] if n < NS else NP + n - NS
                        act.wait_ge(*last_use(layer, LAYER[L_SPLIT[n - A_SPLIT]]))
                        act.wait_ge(*landed(layer, at_))
                        nc.scalar.activation(wps[:, n % A_SPLIT, 0], pieces[:, at_ % A_RAW, :],
                                             ACT.Copy).then_inc(p_high, 1)

                def normalised_high(first):
                    for k in range(DK):
                        act.wait_ge(yn_ready, layer * 2 * DK + first + k + 1)
                        nc.scalar.activation(ys[:, 0, k, :], tmp[:, k % 4, :], ACT.Copy).then_inc(yh_ready, 1)

                def full(pool, g):
                    pool_ = pool
                    act.wait_ge(pool_.full, pool_.done(layer, g))
                    return ps[:, pool.bank(g), :]

                act.wait_ge(A.full, layer * A.n + 1)
                act.wait_ge(std_free, layer * NSTD + 1)
                nc.scalar.activation(std[:, 0, :], ps[:, A.bank("next"), :], ACT.Sqrt, bias=EPSC,
                                     scale=1.0 / D).then_inc(std_ready, 1)
                act.drain().then_inc(A.free, 1)
                for n in range(1, A_SPLIT):
                    act.wait_ge(*landed(layer, n))
                    nc.scalar.activation(wps[:, n, 0], pieces[:, n % A_RAW, :], ACT.Copy).then_inc(p_high, 1)
                normalised_high(0)

                def gate(g, tile, i):
                    nc.scalar.activation(mix[:, tile, :], full(V, g), ACT.Tanh, scale=0.5).then_inc(th_ready, 1)

                for u in range(2):
                    for j in range(3):
                        i = 3 * u + j
                        ahead(f"xl{i}")
                        x = full(A, f"xl{i}")
                        act.wait_ge(xl_free, layer * 6 + i + 1)
                        nc.scalar.activation(xl[:, i % 2, 4:4 + S], x, ACT.Copy).then_inc(xl_ready, 1)
                        act.drain().then_inc(A.free, 1)
                    if u == 0:
                        ahead("gl0")
                        gate("gl0", 0, 0)
                for i in range(1, 6):
                    ahead(f"gl{min(i, 4)}")
                    gate(f"gl{i}", i, i)

                for g in range(2):
                    if g == 1:
                        act.wait_ge(lru_done, layer * 6 + 3)
                    for m in range(3):
                        i = 3 * g + m
                        nc.scalar.activation(mix[:, 9 + m, :], full(A, f"r{i}"), ACT.Tanh, scale=0.5,
                                             bias=par[:, PC["b_a"] + i:PC["b_a"] + i + 1]).then_inc(A.free, 1)
                        nc.scalar.activation(tmp[:, m, :], full(A, f"i{i}"), ACT.Tanh, scale=0.5,
                                             bias=par[:, PC["b_x"] + i:PC["b_x"] + i + 1]).then_inc(A.free, 1)
                        act.drain().then_inc(ri_ready, 1)
                    ahead("gl5" if g == 0 else "gr1")
                    for m in range(3):
                        act.wait_ge(la_ready, layer * 6 + 3 * g + m + 1)
                        nc.scalar.activation(mix[:, 6 + m, :], mix[:, 9 + m, :], ACT.Exp)
                        nc.scalar.activation(mix[:, 9 + m, :], mix[:, 9 + m, :], ACT.Tanh).then_inc(at_ready, 1)
                    ahead("v0.3" if g == 0 else "v1.1")
                    for t in range(ST):
                        cols = 512 if g == 0 else 256
                        nc.scalar.activation(vnat[:, t, 512 * g:512 * g + cols], full(A, f"v{g}.{t}")[:, 0:cols],
                                             ACT.Copy).then_inc(A.free, 1)
                    for m in range(3):
                        act.wait_ge(ratio_ready, layer * 6 + 3 * g + m + 1)
                        nc.scalar.activation(mix[:, 9 + m, :], mix[:, 9 + m, :], ACT.Sqrt).then_inc(us_ready, 1)
                    if g == 0:
                        ahead("gr0")
                        for i in range(2):
                            gate(f"gr{i}", 12 + i, 6 + i)
                act.drain().then_inc(vn_ready, 1)
                for i in range(2, 6):
                    ahead(f"gr{i}")
                    if i == 4:
                        act.wait_ge(lru_done, layer * 6 + 6)
                    gate(f"gr{i}", ret_gate(i), 6 + i)

                def out_root(h):
                    root(A, f"oss{h}", layer, 1 + h, P, std)
                    act.drain().then_inc(A.free, 1)

                ahead("k0")
                for h in range(HEADS):
                    if h + 1 < HEADS:
                        ahead(f"k{h + 1}")
                    if h >= 1:
                        out_root(h - 1)
                    squares(DK + h, 1, lambda k: ps[:, V.bank(f"o{h}"), :], V.full,
                            lambda k: V.done(layer, f"o{h}"), sq)
                out_root(5)

                ahead("vs.3")
                for t in range(ST):
                    x = full(A, f"vs{t}")
                    nc.scalar.activation(vs[:, t, :], x, ACT.Copy).then_inc(A.free, 1)
                act.drain().then_inc(vs_ready, 1)
                act.wait_ge(mix_ready, 2 * layer + 1)
                for j in range(4):
                    ahead(f"gs{j}")
                    gate(f"gs{j}", 12 + j, 12 + j)
                act.wait_ge(var_ready, layer + 1)
                nc.scalar.activation(small[:, 0:ST], mv[:, :, 1], ACT.Sqrt, bias=EPSC).then_inc(sgu_std, 1)
                ahead("u3")
                for k in range(16):
                    if k == 0:
                        act.wait_ge(V.full, V.done(layer, "u3"))
                        act.wait_ge(mix_ready, 2 * layer + 1)
                    if k == 12:
                        act.wait_ge(mix_ready, 2 * layer + 2)
                    if k >= 4:
                        ahead(f"wo.{k - 4}")
                    if k >= DK:
                        act.wait_ge(*last_use(layer, LAYER[L_SPLIT[L_AT[f"wo.{k - DK}"]]]))
                    nc.scalar.activation(ys[:, 0, k % DK, :], mix[:, k, :], ACT.Copy).then_inc(mixh, 1)
                ahead("wo.14")

                squares(14, DK, lambda k: hT[:, k, :], h_ready, lambda k: layer * 2 * DK + DK + k + 1, sq,
                        free_at=layer * 2 * (DK - 2) + DK - 2)
                root(A, "norm2", layer, 7, D, std)
                act.drain().then_inc(A.free, 1)
                ahead("wo.15")
                normalised_high(DK)
                for m in range(DK):
                    ahead(f"g{min(m, 4)}")
                    nc.scalar.activation(mix[:, m, :], full(A, f"g{m}"), ACT.Tanh, scale=0.5).then_inc(A.free, 1)
                    act.drain().then_inc(pg_ready, 1)
                squares(NSQ, DK, lambda k: hT[:, k, :], h_ready, lambda k: layer * 2 * DK + 2 * DK + k + 1, sq,
                        free_at=(layer + 1) * 2 * (DK - 2))
            tail_act(act, squares, root)

        @block.vector
        def _(dve):
            dve.sem_inc(V.free, len(V.banks))
            dve.sem_inc(A.free, len(A.banks))
            dve.sem_inc(std_free, 2)
            dve.sem_inc(xl_free, 2)
            nc.vector.memset(xl[:, :, 0:4], 0.0)
            nc.vector.memset(ones[:], 1.0)
            dve.wait_ge(par_in, 48)

            lam = par_all[:, :, PC["lam"]:PC["lam"] + LRU_T]
            rate = par_all[:, :, PC["decay_rate"]:PC["decay_rate"] + LRU_T]
            nc.vector.tensor_scalar(prep_t, lam, -1.0, None, ALU.mult)
            dve.drain()
            nc.vector.tensor_tensor(prep_n, prep_t, lam, ALU.min).then_inc(prep_v, 1)
            dve.wait_ge(prep_a, 1)
            nc.vector.tensor_scalar(prep_w, prep_e, 1.0, None, ALU.add).then_inc(prep_v, 1)
            dve.wait_ge(prep_v, 2)
            nc.vector.tensor_scalar(prep_c, prep_w, -1.0, None, ALU.add)
            nc.vector.reciprocal(prep_r, prep_w)
            dve.drain()
            nc.vector.tensor_tensor(prep_c, prep_e, prep_c, ALU.subtract)
            nc.vector.tensor_scalar(prep_t, prep_t, 0.0, None, ALU.max)
            dve.drain()
            nc.vector.tensor_tensor(prep_c, prep_c, prep_r, ALU.mult)
            dve.drain()
            dve.wait_ge(prep_a, 2)
            nc.vector.tensor_tensor(prep_c, prep_c, prep_l, ALU.add)
            dve.drain()
            nc.vector.tensor_tensor(prep_c, prep_c, prep_t, ALU.add)
            dve.drain()
            nc.vector.tensor_scalar(rate, prep_c, -4.0, None, ALU.mult)
            for name in ("b_a", "b_x"):
                v = par_all[:, :, PC[name]:PC[name] + LRU_T]
                nc.vector.tensor_scalar(v, v, 0.5, None, ALU.mult)

            dve.wait_ge(prep_a, 3)
            nc.vector.scalar_tensor_tensor(cond[:], cond[:], 1.0, q_(par2, "cond", 0, 2 * DK).rearrange(
                "p (k c) -> p k c", k=DK), ALU.add, ALU.mult)
            dve.drain()
            nc.vector.tensor_scalar(cond[:], cond[:], 0.5, None, ALU.mult).then_inc(cond_ready, 1)

            posi, ang, turn, turni = tmp[:, 2, :], tmp[:, 3, :], xc[:, 0, :], xc[:, 1, :]
            nc.vector.tensor_copy(ang, posi.bitcast(I32))
            dve.drain()
            nc.vector.tensor_scalar(ang, ang, q_(par2, "inv_freq"), None, ALU.mult)
            dve.drain()
            for out, quarter in ((tmp[:, 0, :], 0.25), (tmp[:, 1, :], 0.0)):
                nc.vector.tensor_scalar(turni.bitcast(I32), ang, 1.0 / (2 * np.pi), quarter, ALU.mult, ALU.add)
                dve.drain()
                nc.vector.tensor_copy(turn, turni.bitcast(I32))
                dve.drain()
                if quarter:
                    nc.vector.tensor_scalar(turn, turn, -quarter, None, ALU.add)
                    dve.drain()
                nc.vector.scalar_tensor_tensor(out, turn, -TWO_PI[0], ang, ALU.mult, ALU.add)
                dve.drain()
                for part in TWO_PI[1:]:
                    nc.vector.scalar_tensor_tensor(out, turn, -part, out, ALU.mult, ALU.add)
                    dve.drain()
                nc.vector.tensor_scalar(out, out, 3.1415925, -3.1415925, ALU.min, ALU.max)
                dve.drain()
            dve.sem_inc(prep_v, 1)
            dve.wait_ge(prep_a, 4)
            nc.vector.tensor_scalar(rsin, rsin, q_(par2, "rope_sign"), None, ALU.mult)
            dve.drain()
            dve.wait_ge(x_in, 16 * DK)
            dve.sem_inc(h_ready, DK)
            dve.wait_ge(const_in, 16 * N_CONST)

            def p_(name, i, n=1):
                return par[:, PC[name] + i:PC[name] + i + n]

            def inverse(i, ready, free_at, buf, cols=S):
                dve.wait_ge(ready, free_at)
                r = buf[:, i % 2, 0:cols]
                nc.vector.reciprocal(r, r)
                dve.drain()
                return r

            def rope(src, dst, t, cos, sin, halves):
                nc.vector.tensor_tensor(dst, src, cos, ALU.mult)
                for a, b in halves:
                    nc.vector.tensor_tensor(t[b[0]:b[1]], src[a[0]:a[1]], sin[a[0]:a[1]], ALU.mult)
                dve.drain()
                return nc.vector.tensor_tensor(dst, dst, t, ALU.add)

            def normalised(gain, r, base, half_base):
                def low(k):
                    dve.wait_ge(yh_ready, base + k + 1)
                    nc.vector.tensor_tensor(ys[:, 1, k, :], tmp[:, k % 4, :], ys[:, 0, k, :].bitcast(F32),
                                            ALU.subtract).then_inc(y_ready, 1)

                for k in range(DK):
                    if k >= 4 and k % 2:
                        dve.wait_ge(yl_pool, half_base + (k - 4) // 2 + 1)
                    nc.vector.scalar_tensor_tensor(tmp[:, k % 4, :], hT[:, k, :], gain(k), r, ALU.mult,
                                                   ALU.mult).then_inc(yn_ready, 1)
                    if k >= 1 and k % 2:
                        low(k - 1)
                        dve.drain()
                dve.drain().then_inc(std_free, 1)

            with dve.Fori(0, L) as layer:
                def full(pool, g):
                    dve.wait_ge(pool.full, pool.done(layer, g))
                    return ps[:, pool.bank(g), :]

                nc.vector.tensor_copy(par[:].unsqueeze(1), par_all[:, bass.ds(layer, 1), :])
                dve.drain()

                r = inverse(0, std_ready, layer * NSTD + 1, std)
                normalised(lambda k: p_("mix_norm", k), r, layer * 2 * DK, layer * DK)

                def silu2(g, tile, n):
                    x = full(V, g)
                    dve.wait_ge(th_ready, layer * 16 + n + 1)
                    nc.vector.scalar_tensor_tensor(mix[:, tile, :], mix[:, tile, :], 1.0, x, ALU.add,
                                                   ALU.mult).then_inc(V.free, 1)

                def conv(i):
                    dve.wait_ge(xl_ready, layer * 6 + i + 1)
                    x, o = xl[:, i % 2, :], xc[:, i, :]
                    nc.vector.tensor_scalar(o, x[:, 1:1 + S], p_("conv_w", i), p_("conv_b", i), ALU.mult, ALU.add)
                    for w in range(1, CONV):
                        dve.drain()
                        last = nc.vector.scalar_tensor_tensor(o, x[:, 1 + w:1 + w + S], p_("conv_w", w * LRU_T + i),
                                                              o, ALU.mult, ALU.add)
                    last.then_inc(xc_ready, 1)
                    dve.drain().then_inc(xl_free, 1)

                for u in range(2):
                    for j in range(3):
                        conv(3 * u + j)
                    silu2(f"gl{u}", u, u)
                for i in range(2, 6):
                    silu2(f"gl{i}", i, i)

                for g in range(2):
                    for m in range(3):
                        dve.wait_ge(ri_ready, layer * 6 + 3 * g + m + 1)
                        t = mix[:, 9 + m, :]
                        nc.vector.tensor_scalar(t, t, 1.0, p_("decay_rate", 3 * g + m), ALU.add,
                                                ALU.mult).then_inc(la_ready, 1)
                    for m in range(3):
                        dve.wait_ge(at_ready, layer * 6 + 3 * g + m + 1)
                        t, d = mix[:, 9 + m, :], tmp[:, 3, :]
                        nc.vector.tensor_scalar(d, t, -1.0, 1.0, ALU.mult, ALU.add)
                        dve.drain()
                        nc.vector.reciprocal(d, d)
                        dve.drain()
                        nc.vector.scalar_tensor_tensor(t, t, -2.0, d, ALU.mult, ALU.mult).then_inc(ratio_ready, 1)
                        dve.drain()
                    dve.wait_ge(A.full, A.done(layer, f"i{3 * g + 2}"))
                    for m in range(3):
                        i = 3 * g + m
                        x, a, uu = xc[:, i, :], mix[:, 6 + m, :], mix[:, 9 + m, :]
                        nc.vector.scalar_tensor_tensor(x, tmp[:, m, :], 1.0, x, ALU.add, ALU.mult)
                        dve.drain()
                        dve.wait_ge(us_ready, layer * 6 + i + 1)
                        nc.vector.scalar_tensor_tensor(uu, x, 0.5, uu, ALU.mult, ALU.mult)
                        dve.drain()
                        nc.vector.tensor_tensor_scan(x, a, uu, 0.0, ALU.mult, ALU.add)
                        dve.drain()
                        nc.vector.scalar_tensor_tensor(mix[:, i, :], x, 0.5, mix[:, i, :], ALU.mult,
                                                       ALU.mult).then_inc(lru_done, 1)
                    dve.drain()
                    for i in range(2) if g == 0 else range(2, 6):
                        silu2(f"gr{i}", ret_gate(i), 6 + i)
                dve.drain()

                def rotated(h, w, name):
                    x = full(V, f"{name}{h}")
                    rope(x, qk[:, 2 * (h % 2) + w, :], tmp[:, w, :], rcos, rsin,
                         (((0, 64), (64, 128)), ((64, 128), (0, 64))))
                    dve.drain().then_inc(V.free, 1)
                    if w:
                        dve.sem_inc(qk_ready, 1)

                def normed(h):
                    r = inverse(1 + h, std_ready, layer * NSTD + 1 + h + 1, std)
                    nc.vector.scalar_tensor_tensor(mix[:, 6 + h, :], mix[:, 6 + h, :], 0.5, r, ALU.mult, ALU.mult)
                    dve.drain().then_inc(std_free, 1)

                rotated(0, 0, "q")
                rotated(0, 1, "k")
                for h in range(1, HEADS + 1):
                    if h < HEADS:
                        rotated(h, 0, "q")
                    g = h - 1
                    for c in (0, 1, 3, 2):
                        at_c = c * S - P * c * (c - 1) // 2
                        n, first = S - c * P, 3 * P if c == 3 else 0
                        x = full(V, f"s{g}.{min(c, 4 - c)}")
                        nc.vector.tensor_tensor(dec_s[:, at_c:at_c + n], x[:, first:first + n], decay[:, g, 0:n], ALU.mult)
                        if c != 1:
                            dve.drain().then_inc(V.free, 1)
                    dve.sem_inc(s_ready, 1)
                    if h < HEADS:
                        rotated(h, 1, "k")
                    if h >= 2:
                        normed(h - 2)
                    x = full(V, f"o{g}")
                    dve.wait_ge(sq_ready, layer * NSQ + DK + g + 1)
                    nc.vector.scalar_tensor_tensor(mix[:, 6 + g, :], x, p_("ret_norm", g), mix[:, ret_gate(g), :],
                                                   ALU.mult, ALU.mult)
                    dve.drain().then_inc(V.free, 1)
                normed(5)
                dve.sem_inc(mix_ready, 1)

                dve.wait_ge(sgu_in, layer * 64 + 64)
                nc.vector.tensor_tensor(wsT, wsT, tri[:].unsqueeze(1).to_broadcast([P, SGU_G, P]), ALU.mult)
                dve.wait_ge(vs_ready, layer + 1)
                for t in range(ST):
                    nc.vector.bn_stats(bn[:, t, :], vs[:, t, :])
                dve.drain()
                for t in range(ST):
                    nc.vector.bn_aggr(mv[:, t, :], bn[:, t, :])
                dve.drain().then_inc(var_ready, 1)
                for j in range(4):
                    silu2(f"gs{j}", 12 + j, 12 + j)
                dve.wait_ge(sgu_std, layer + 1)
                nc.vector.reciprocal(small[:, 4:4 + ST], small[:, 0:ST])
                dve.drain()
                for t in range(ST):
                    nc.vector.tensor_scalar(vs[:, t, :], vs[:, t, :], mv[:, t, 0:1], small[:, 4 + t:5 + t],
                                            ALU.subtract, ALU.mult)
                for k, op in ((0, ALU.mult), (1, ALU.add)):
                    dve.drain()
                    for t in range(ST):
                        nc.vector.tensor_tensor(vs[:, t, :], vs[:, t, :], lngb[:, k, :], op)
                dve.drain().then_inc(vn2_ready, 1)
                for j in range(4):
                    x = full(V, f"u{j}")
                    nc.vector.scalar_tensor_tensor(mix[:, 12 + j, :], x, 0.5, mix[:, 12 + j, :], ALU.mult,
                                                   ALU.mult).then_inc(V.free, 1)
                for j in range(4):
                    x = full(V, f"mx{j}")
                    nc.vector.tensor_tensor(tmp[:, j, :].rearrange("p (c i) -> p c i", c=ST),
                                            x.rearrange("p (c i) -> p c i", c=ST),
                                            bsb[:, j, :].unsqueeze(1).to_broadcast([P, ST, P]),
                                            ALU.add).then_inc(V.free, 1)
                dve.drain()
                for j in range(4):
                    nc.vector.tensor_tensor(mix[:, 12 + j, :], mix[:, 12 + j, :], tmp[:, j, :], ALU.mult)
                dve.drain().then_inc(mix_ready, 1)

                for m in range(DK):
                    pool = V if m < 4 else A
                    nc.vector.tensor_tensor(hT[:, m, :], full(pool, f"w{m}"), hT[:, m, :], ALU.add).then_inc(h_ready, 1)
                    dve.drain().then_inc(pool.free, 1)
                r = inverse(7, std_ready, layer * NSTD + 8, std)
                normalised(lambda k: p_("ple_norm", k), r, layer * 2 * DK + DK, layer * DK + DK // 2)
                for m in range(DK):
                    x = full(V, f"p{m}")
                    dve.wait_ge(pg_ready, layer * DK + m + 1)
                    t = tmp[:, m % 2, :]
                    nc.vector.scalar_tensor_tensor(t, mix[:, m, :], 1.0, x, ALU.add, ALU.mult)
                    dve.drain().then_inc(V.free, 1)
                    nc.vector.scalar_tensor_tensor(hT[:, m, :], t, 0.5, hT[:, m, :], ALU.mult,
                                                   ALU.add).then_inc(h_ready, 1)
                dve.drain()
            tail_dve(dve, inverse, rope)

        @block.gpsimd
        def _(pool):
            for dst, name in ((ident[:], "ident"), (tri[:], "tri"), (before[:], "before"), (cst[:], "cst")):
                pool.dma_start(dst, io[name]).then_inc(const_in, 16)
            pool.dma_start(decay, io["decay"]).then_inc(const_in, 16)
            pool.dma_start(brt[:], io["b_router"].partition_broadcast(P)).then_inc(const_in, 16)
            for t in range(ACC_ROWS // P):
                pool.dma_start(acc_dram[t * P:(t + 1) * P, :], io["zeros"]).then_inc(acc_init, 16)

            def low_part_of(count, n, at_):
                pool.wait_ge(p_high, count)
                nc.gpsimd.tensor_tensor(wps[:, n % A_SPLIT, 1], pieces[:, at_ % A_RAW, :],
                                        wps[:, n % A_SPLIT, 0].bitcast(F32), ALU.subtract).then_inc(p_low, 1)

            def mixed_low(count, k, tile):
                pool.wait_ge(mixh, count)
                nc.gpsimd.tensor_tensor(ys[:, 1, k, :], mix[:, tile, :], ys[:, 0, k, :].bitcast(F32),
                                        ALU.subtract).then_inc(mixl, 1)

            for n in range(A_SPLIT):
                low_part_of(n + 1, n, n)
            with pool.Fori(0, L) as layer:
                def odd_lows(first):
                    for k in range(1, DK, 2):
                        pool.wait_ge(yh_ready, layer * 2 * DK + first + k + 1)
                        nc.gpsimd.tensor_tensor(ys[:, 1, k, :], tmp[:, k % 4, :], ys[:, 0, k, :].bitcast(F32),
                                                ALU.subtract).then_inc(yl_pool, 1)

                odd_lows(0)
                for n in range(A_SPLIT, NS + A_SPLIT):
                    if n == L_AT["g0"] + A_SPLIT:
                        odd_lows(DK)
                    k = n - L_AT["wo.0"] - A_SPLIT
                    for tile in range(4) if k == 0 else [k + 3] if 0 < k < 13 else []:
                        mixed_low(layer * 16 + tile + 1, tile % DK, tile)
                    low_part_of(layer * NS + n + 1, n, L_SPLIT[n] if n < NS else NP + n - NS)
            pool.wait_ge(h_ready, (2 * L + 1) * DK)
            pool.dma_start(ctxT, io["ctxT"]).then_inc(c_in, 16)
            pool.dma_start(acos, io["axial_cos"]).then_inc(late_in, 16)
            pool.dma_start(asin, io["axial_sin"]).then_inc(late_in, 16)

            first_w = T_AT["w0"] + A_SPLIT
            for n in range(A_SPLIT, first_w):
                low_part_of(L * NS + n + 1, n, T_SPLIT[n])
            for i, k in enumerate((4, 5, 6, 7, 0, 1, 2, 3)):
                mixed_low(L * 16 + i + 1, k, 8 + k)
            for n in range(first_w, len(T_SPLIT)):
                low_part_of(L * NS + n + 1, n, T_SPLIT[n])
            bias_pool(pool)
            experts_pool(pool)


def constants():
    f = np.float32
    p = np.arange(P)
    j = np.arange(S)
    log_g = np.log1p(-np.exp2(f(-5.0) - np.arange(HEADS, dtype=f))).astype(f)
    diff = j[None, :] - p[:, None]
    decay = np.where(diff[:, None, :] >= 0,
                     np.exp(np.maximum(diff, 0)[:, None, :] * log_g[None, :, None].astype(np.float64)), 0.0)
    half = np.arange(64, dtype=f)
    inv = (f(10000.0) ** (-half / f(64))).astype(f)
    inv2 = (f(10000.0) ** (-np.arange(0, 64, 2, dtype=f) / f(64))).astype(f)
    axis, i = p // 64, p % 32
    place = np.where(axis[:, None] == 0, (j // 64)[None, :], (j % 64)[None, :]).astype(f)
    ang = (place * inv2[i][:, None]).astype(f).astype(np.float64)
    sign = np.where((p // 32) % 2 == 0, 1.0, -1.0)[:, None]
    row = np.concatenate([np.arange(E_N), 2 * np.arange(24), P * np.arange(LISTS + 1), np.arange(-P, 0)])
    token = p[:, None] + P * (np.arange(ST * TOP) // TOP)[None, :]
    return {
        "ident": np.eye(P, dtype=f), "tri": np.triu(np.ones((P, P), f)), "before": np.triu(np.ones((P, P), f), 1),
        "cst": np.concatenate([np.tile(row, (P, 1)), token], axis=1).astype(f),
        "decay": (decay * P ** -0.5).astype(f),
        "axial_cos": np.cos(ang).astype(f), "axial_sin": (np.sin(ang) * sign).astype(f),
        "inv_freq": inv[p % 64][:, None], "rope_sign": np.where(p < 64, 1.0, -1.0).astype(f)[:, None],
        "part": p.astype(f)[:, None], "part32": (p % E_N).astype(f)[:, None], "dump": (S + p).astype(f)[:, None],
        "zeros": np.zeros((P, D), f),
    }


def tiles(v):
    v = np.asarray(v)
    return np.moveaxis(v.reshape(*v.shape[:-1], -1, P), -1, 0)


def piece(w, k):
    w = w.reshape(k, P, -1).transpose(1, 0, 2).reshape(P, -1)
    return np.pad(w, ((0, 0), (0, PIECE - w.shape[1])))


def layout(x):
    c = constants()
    X = {k: np.asarray(v) for k, v in x.items()}
    stream = []
    for l in range(L):
        w = X["w_in"][l]
        sizes = np.cumsum([0, 768, 768, 768, 768, 768, 768, 512, 512, 512])
        xl, gl, q, k, v, gr, u, vs, gs = (w[:, a:b] for a, b in zip(sizes[:-1], sizes[1:]))
        col = {**{f"xl{i}": (xl, i) for i in range(6)}, **{f"gl{i}": (gl, i) for i in range(6)},
               **{f"gr{i}": (gr, i) for i in range(6)}, **{f"q{i}": (q, i) for i in range(6)},
               **{f"k{i}": (k, i) for i in range(6)}, **{f"gs{i}": (gs, i) for i in range(4)},
               **{f"u{i}": (u, i) for i in range(4)}, **{f"g{i}": (X["w_ple_gate"][l], i) for i in range(DK)}}
        wbd = np.zeros((2, 2, len(PAIRS), P, P), np.float32)
        for wi, name in enumerate(("lru_w_a", "lru_w_x")):
            for g in range(2):
                for n, (kt, mt) in enumerate(PAIRS):
                    for b in range(4):
                        r0, r1 = max(kt * P, b * 96), min((kt + 1) * P, (b + 1) * 96)
                        c0, c1 = max(mt * P, b * 96), min((mt + 1) * P, (b + 1) * 96)
                        if r0 < r1 and c0 < c1:
                            wbd[wi, g, n, r0 - kt * P:r1 - kt * P, c0 - mt * P:c1 - mt * P] = \
                                X[name][l, 4 * g + b, r0 - b * 96:r1 - b * 96, c0 - b * 96:c1 - b * 96]
        by_name = {n: piece(m[:, i * P:(i + 1) * P], DK) for n, (m, i) in col.items()}
        for g in range(2):
            for wi in range(2):
                lru = wbd[wi, g].transpose(1, 0, 2).reshape(P, -1)
                by_name[f"lru{g}.{wi}"] = np.pad(lru, ((0, 0), (0, PIECE - lru.shape[1])))
        for i in range(4):
            by_name[f"v0.{i}"] = piece(v[2 * i * P:(2 * i + 2) * P, 0:512], 2)
            by_name[f"vs.{i}"] = piece(vs[2 * i * P:(2 * i + 2) * P], 2)
        for i in range(2):
            by_name[f"v1.{i}"] = piece(v[4 * i * P:(4 * i + 4) * P, 512:], 4)
            by_name[f"ple{i}"] = piece(np.ascontiguousarray(X["p"][l, 0].T[i * P:(i + 1) * P]), 1)
            by_name[f"ple{2 + i}"] = X["w_ple_proj"][l][i * P:(i + 1) * P]
        for i in range(16):
            by_name[f"wo.{i}"] = X["w_out"][l][i * P:(i + 1) * P]
        stream += [by_name[n] for n, *_ in LAYER]
    w, wa, wo = X["w_in_2"][0], X["w_ada_2"][0], X["w_out_2"][0]
    by_name = {f"k{i}": piece(w[:, 512 + i * P:512 + (i + 1) * P], DK) for i in range(2)}
    by_name |= {f"v{i}": piece(w[4 * i * P:(4 * i + 4) * P, 768:1024], 4) for i in range(2)}
    by_name |= {f"ada{i // 4}.{i % 4}": piece(wa[:, i * P:(i + 1) * P], DK) for i in range(48)}
    for n, first in (("q", 0), ("cb", 1024), ("cc", 1536), ("cx", 2048)):
        by_name |= {f"{n}{i}": piece(w[:, first + i * P:first + (i + 1) * P], DK) for i in range(4)}
    by_name |= {f"w{i}": piece(wo[:, i * P:(i + 1) * P], DK) for i in range(DK)}
    by_name["router"] = piece(X["w_router_2"][0], DK)
    stream += [by_name[n] for n, *_ in TAIL]

    gu = X["w_gate_up_2"][0].reshape(E_N, DK, P, 2, 2, 512)
    dn = X["w_down_2"][0].reshape(E_N, DK, P, 2, 512)
    w_moe = np.empty((E_N, 6, P, DK, 512), np.float32)
    for half in range(2):
        for part in range(2):
            w_moe[:, 2 * half + part] = gu[:, :, :, part, half].transpose(0, 2, 1, 3)
        w_moe[:, 4 + half] = dn[:, :, :, half].transpose(0, 2, 1, 3)
    bg = X["b_gate_up_2"][0].reshape(E_N, 2, 2, 512).transpose(0, 2, 1, 3).reshape(E_N, 2048)
    par = np.concatenate([tiles(X["mix_norm"]), tiles(X["ple_norm"]),
                          tiles(X["lru_conv_w"]).reshape(P, L, -1), tiles(X["lru_conv_b"]), tiles(X["lru_b_a"]),
                          tiles(X["lru_b_x"]), tiles(X["lru_lambda"]), tiles(X["ret_norm"]),
                          np.zeros((P, L, LRU_T), np.float32)], axis=2)
    cond = np.stack([tiles(X["c_2"][0]), tiles(X["c_ctx_2"])], axis=-1).reshape(P, -1)
    par2 = np.concatenate([tiles(X["final_norm"]), tiles(X["b_ada_2"][0]), tiles(X["g_norm1_2"][0]),
                           tiles(X["g_norm2_2"][0]), X["g_q_2"][0][:, None], X["g_k_2"][0][:, None],
                           tiles(X["w_conv_2"][0]).reshape(P, -1), tiles(X["g_final_2"]), cond,
                           c.pop("inv_freq"), c.pop("rope_sign"), c.pop("part"), c.pop("part32"), c.pop("dump")], axis=1)
    out = dict(c)
    out.update({
        "xT": X["x"][0].T, "pieces": np.stack(stream), "w_moe": w_moe.reshape(E_N * 6, P, UNIT),
        "b_moe": np.concatenate([bg, X["b_down_2"][0]], axis=1), "par": par, "par2": par2,
        "b_router": X["b_router_2"][0], "positions": X["positions"][0],
        "ln_g": X["sgu_ln_g"], "ln_b": X["sgu_ln_b"], "b_s": X["sgu_b_s"],
        "wsT": X["sgu_w_s"].transpose(0, 3, 1, 2),
        "ctxT": X["ctx_2"][0].T.reshape(DK, P, CTX).transpose(1, 0, 2),
    })
    return {k: np.ascontiguousarray(v) for k, v in out.items()}


def kernel(**inputs):
    import concourse.bacc as bacc
    from concourse.bass_utils import run_bass_kernel_spmd as run

    nc = bacc.Bacc("TRN2", target_bir_lowering=False, num_devices=1)
    arrays = {f"in_{k}": v for k, v in layout(inputs).items()}
    io = {k[3:]: nc.dram_tensor(k, v.shape, mybir.dt.from_np(v.dtype), kind="ExternalInput").ap()
          for k, v in arrays.items()}
    io["out"] = nc.dram_tensor("out_T", (D, S), F32, kind="ExternalOutput").ap()
    build(nc, io)
    r = run(nc, [arrays], core_ids=[0])
    return np.ascontiguousarray(np.asarray(r.results[0]["out_T"]).T).reshape(1, S, D)
```
